# Optimizing a Trainium2 kernel written in Bass

```python
import jax, jax.numpy as jnp
from jax import lax
import numpy as np

D_MODEL = 1024
BATCH = 1
SEQ = 512
DEPTH = 1

CHUNK = 64
HEAD_DIM = 64
N_HEADS_SB = 4
N_HEADS_CH = 8
CONV_CH = 256
CONV_WIDTH = 3
N_PREV_CHUNKS = 8
BAND = (N_PREV_CHUNKS + 1) * CHUNK
REL_CLIP = 128
Q_BLOCK = 128
D_SB = N_HEADS_SB * HEAD_DIM
D_CH = N_HEADS_CH * HEAD_DIM
D_MIX = D_SB + D_CH + CONV_CH
D_IN = 3 * D_SB + 3 * D_CH + 3 * CONV_CH
N_OUT_GROUPS = D_MIX // HEAD_DIM
D_FF = ((8 * D_MODEL // 3 + 255) // 256) * 256
EPS = 1e-6


def rmsnorm(x, w):
    xf = x.astype(jnp.float32)
    y = xf * lax.rsqrt(jnp.mean(xf * xf, axis=-1, keepdims=True) + EPS)
    return (y * w.astype(jnp.float32)).astype(x.dtype)

def group_rmsnorm(y, w):
    b, s, _ = y.shape
    yg = y.astype(jnp.float32).reshape(b, s, N_OUT_GROUPS, HEAD_DIM)
    yg = yg * lax.rsqrt(jnp.mean(yg * yg, axis=-1, keepdims=True) + EPS)
    return (yg.reshape(b, s, D_MIX) * w.astype(jnp.float32)).astype(y.dtype)

def to_heads(t):
    b, s, _ = t.shape
    return t.reshape(b, s, -1, HEAD_DIM).transpose(0, 2, 1, 3)

def from_heads(t):
    b, h, s, d = t.shape
    return t.transpose(0, 2, 1, 3).reshape(b, s, h * d)

def stick_breaking_attention(q, k, v):
    b, h, s, d = q.shape
    n = s // Q_BLOCK
    qb = (q.astype(jnp.float32) * (d ** -0.5)).reshape(b, h, n, Q_BLOCK, d)
    kb = k.astype(jnp.float32).reshape(b, h, n, Q_BLOCK, d)
    vb = v.astype(jnp.float32).reshape(b, h, n, Q_BLOCK, d)
    idx = jnp.arange(Q_BLOCK)
    after_mat = (idx[:, None] > idx[None, :]).astype(jnp.float32)
    diag_mask = idx[None, :] < idx[:, None]
    out = jnp.zeros((b, h, n, Q_BLOCK, d), jnp.float32)
    carry = jnp.zeros((b, h, n, Q_BLOCK), jnp.float32)
    for o in range(n):
        z = jnp.einsum('bhnqd,bhnkd->bhnqk', qb[:, :, o:], kb[:, :, :n - o])
        log_rest = jax.nn.log_sigmoid(-z)
        if o == 0:
            log_rest = jnp.where(diag_mask, log_rest, 0.0)
        after = jnp.einsum('bhnqj,js->bhnqs', log_rest, after_mat) + carry[:, :, o:, :, None]
        w = jnp.exp(jax.nn.log_sigmoid(z) + after)
        if o == 0:
            w = jnp.where(diag_mask, w, 0.0)
        out = out.at[:, :, o:].add(jnp.einsum('bhnqk,bhnkd->bhnqd', w, vb[:, :, :n - o]))
        carry = carry.at[:, :, o:].add(jnp.sum(log_rest, axis=-1))
    return out.reshape(b, h, s, d).astype(v.dtype)

def chunked_relpos_attention(q, k, v, rel_bias):
    b, h, s, d = q.shape
    nc = s // CHUNK
    pad = N_PREV_CHUNKS * CHUNK
    qc = (q.astype(jnp.float32) * (d ** -0.5)).reshape(b, h, nc, CHUNK, d)
    kpad = jnp.pad(k, ((0, 0), (0, 0), (pad, 0), (0, 0))).reshape(b, h, nc + N_PREV_CHUNKS, CHUNK, d)
    vpad = jnp.pad(v, ((0, 0), (0, 0), (pad, 0), (0, 0))).reshape(b, h, nc + N_PREV_CHUNKS, CHUNK, d)
    band_idx = jnp.arange(nc)[:, None] + jnp.arange(N_PREV_CHUNKS + 1)[None, :]
    kb = kpad[:, :, band_idx].reshape(b, h, nc, BAND, d).astype(jnp.float32)
    vb = vpad[:, :, band_idx].reshape(b, h, nc, BAND, d).astype(jnp.float32)
    scores = jnp.einsum('bhcqd,bhckd->bhcqk', qc, kb)
    p = jnp.arange(CHUNK)[:, None]
    m = jnp.arange(BAND)[None, :]
    rel = jnp.clip(N_PREV_CHUNKS * CHUNK + p - m, -REL_CLIP, REL_CLIP) + REL_CLIP
    bias = rel_bias.astype(jnp.float32)[:, rel]
    valid = jnp.repeat(band_idx >= N_PREV_CHUNKS, CHUNK, axis=1)
    scores = jnp.where(valid[None, None, :, None, :], scores + bias[None, :, None], -jnp.inf)
    probs = jax.nn.softmax(scores, axis=-1)
    out = jnp.einsum('bhcqk,bhckd->bhcqd', probs, vb)
    return out.reshape(b, h, s, d).astype(v.dtype)

def short_conv_mixer(gate_b, gate_c, xc, conv_w):
    hc = gate_c * xc
    y = lax.conv_general_dilated(
        hc, conv_w[:, None, :].astype(hc.dtype), window_strides=(1,),
        padding=[(CONV_WIDTH - 1, 0)], dimension_numbers=('NWC', 'WIO', 'NWC'),
        feature_group_count=CONV_CH)
    return gate_b * y

def swiglu(x, w_gate, w_up, w_down):
    return (jax.nn.silu(x @ w_gate) * (x @ w_up)) @ w_down

def first_inputs(seed: int = 0) -> dict:
    key = jax.random.key(seed)
    ks = jax.random.split(key, 14)
    f32 = jnp.float32

    def gain(k, n):
        return 1.0 + 0.02 * jax.random.normal(k, (DEPTH, n), f32)

    return {
        "x": jax.random.normal(ks[0], (BATCH, SEQ, D_MODEL), f32),
        "attn_norm_w": gain(ks[1], D_MODEL),
        "w_in": jax.random.normal(ks[2], (DEPTH, D_MODEL, D_IN), f32) * D_MODEL ** -0.5,
        "q_norm_w": gain(ks[3], HEAD_DIM),
        "k_norm_w": gain(ks[4], HEAD_DIM),
        "rel_bias": 0.1 * jax.random.normal(ks[5], (DEPTH, N_HEADS_CH, 2 * REL_CLIP + 1), f32),
        "conv_w": jax.random.normal(ks[6], (DEPTH, CONV_WIDTH, CONV_CH), f32) * CONV_WIDTH ** -0.5,
        "out_norm_w": gain(ks[7], D_MIX),
        "w_out": jax.random.normal(ks[8], (DEPTH, D_MIX, D_MODEL), f32) * D_MIX ** -0.5,
        "ffn_norm_w": gain(ks[9], D_MODEL),
        "w_gate": jax.random.normal(ks[10], (DEPTH, D_MODEL, D_FF), f32) * D_MODEL ** -0.5,
        "w_up": jax.random.normal(ks[11], (DEPTH, D_MODEL, D_FF), f32) * D_MODEL ** -0.5,
        "w_down": jax.random.normal(ks[12], (DEPTH, D_FF, D_MODEL), f32) * D_FF ** -0.5,
    }

def first_block(x, attn_norm_w, w_in, q_norm_w, k_norm_w, rel_bias, conv_w, out_norm_w,
              w_out, ffn_norm_w, w_gate, w_up, w_down):
    widths = [D_SB] * 3 + [D_CH] * 3 + [CONV_CH] * 3
    split_points = [int(v) for v in np.cumsum(widths)[:-1]]
    for l in range(DEPTH):
        h = rmsnorm(x, attn_norm_w[l])
        proj = h @ w_in[l]
        (q_a, k_a, v_a, q_b, k_b, v_b, g_b, g_c, x_c) = jnp.split(proj, split_points, axis=-1)
        y_sb = from_heads(stick_breaking_attention(to_heads(q_a), to_heads(k_a), to_heads(v_a)))
        qh = rmsnorm(to_heads(q_b), q_norm_w[l])
        kh = rmsnorm(to_heads(k_b), k_norm_w[l])
        y_ch = from_heads(chunked_relpos_attention(qh, kh, to_heads(v_b), rel_bias[l]))
        y_cv = short_conv_mixer(g_b, g_c, x_c, conv_w[l])
        y = group_rmsnorm(jnp.concatenate([y_sb, y_ch, y_cv], axis=-1), out_norm_w[l])
        x = x + y @ w_out[l]
        x = x + swiglu(rmsnorm(x, ffn_norm_w[l]), w_gate[l], w_up[l], w_down[l])
    return x


CONV_DIM = 1024
CONV_KERNEL = 31
CONV_PAD = (CONV_KERNEL - 1) // 2
N_HEADS = 16
N_KV_HEADS = 4
ATTN_DIM = N_HEADS * HEAD_DIM
KV_DIM = N_KV_HEADS * HEAD_DIM
WINDOW = 128
BLOCK = 128
NEG_INF = -1e30
N_BRANCH = 2
IN_DIM = 2 * CONV_DIM + ATTN_DIM + 2 * KV_DIM + N_BRANCH * D_MODEL
PEER_HEADS = 8
PEER_KEY_DIM = 256
PEER_HALF = PEER_KEY_DIM // 2
N_KEYS = 128
N_EXPERTS = N_KEYS * N_KEYS
PEER_TOPK = 16
TOKEN_CHUNK = 128


def rmsnorm_2(x, g):
    xf = x.astype(jnp.float32)
    y = xf * lax.rsqrt(jnp.mean(xf * xf, axis=-1, keepdims=True) + EPS)
    return (y * g.astype(jnp.float32)).astype(x.dtype)

def layernorm(x, g, b):
    xf = x.astype(jnp.float32)
    mu = jnp.mean(xf, axis=-1, keepdims=True)
    var = jnp.mean(jnp.square(xf - mu), axis=-1, keepdims=True)
    y = (xf - mu) * lax.rsqrt(var + EPS)
    return (y * g.astype(jnp.float32) + b.astype(jnp.float32)).astype(x.dtype)

def conformer_conv(a_in, dw_w, dw_b, ln_g, ln_b, w_pw):
    u = a_in[..., :CONV_DIM] * jax.nn.sigmoid(a_in[..., CONV_DIM:])
    u = lax.conv_general_dilated(
        u, dw_w[:, None, :], window_strides=(1,), padding=[(CONV_PAD, CONV_PAD)],
        dimension_numbers=('NWC', 'WIO', 'NWC'), feature_group_count=CONV_DIM) + dw_b
    u = layernorm(u, ln_g, ln_b)
    u = jax.nn.silu(u)
    return u @ w_pw

def windowed_gqa(q, k, v, sink):
    b, s = q.shape[0], q.shape[1]
    nb = s // BLOCK
    grp = N_HEADS // N_KV_HEADS
    span = BLOCK + 2 * WINDOW
    kp = jnp.pad(k, ((0, 0), (WINDOW, WINDOW), (0, 0), (0, 0)))
    vp = jnp.pad(v, ((0, 0), (WINDOW, WINDOW), (0, 0), (0, 0)))
    qb = q.reshape(b, nb, BLOCK, N_KV_HEADS, grp, HEAD_DIM).transpose(1, 0, 2, 3, 4, 5)
    slopes = jnp.exp2(-8.0 * jnp.arange(1, N_HEADS + 1, dtype=jnp.float32) / N_HEADS)
    slopes = slopes.reshape(N_KV_HEADS, grp)
    r = jnp.arange(BLOCK)[:, None]
    c = jnp.arange(span)[None, :]
    dist = jnp.abs(r + WINDOW - c)
    bias = -slopes[:, :, None, None] * dist.astype(jnp.float32)[None, None]
    in_window = dist <= WINDOW
    sink_f = sink.astype(jnp.float32).reshape(N_KV_HEADS, grp)[None, :, :, None]
    scale = HEAD_DIM ** -0.5

    def block_fn(args):
        i, qi = args
        start = i * BLOCK
        ks = lax.dynamic_slice_in_dim(kp, start, span, axis=1)
        vs = lax.dynamic_slice_in_dim(vp, start, span, axis=1)
        key_pos = start - WINDOW + jnp.arange(span)
        valid = in_window & ((key_pos >= 0) & (key_pos < s))[None, :]
        logits = jnp.einsum('bqkgd,bskd->bkgqs', qi, ks).astype(jnp.float32) * scale + bias
        logits = jnp.where(valid, logits, NEG_INF)
        m = jnp.maximum(logits.max(-1), sink_f)
        p = jnp.exp(logits - m[..., None])
        denom = p.sum(-1) + jnp.exp(sink_f - m)
        o = jnp.einsum('bkgqs,bskd->bqkgd', p, vs.astype(jnp.float32))
        o = o / denom.transpose(0, 3, 1, 2)[..., None]
        return o.astype(q.dtype)

    out = lax.map(block_fn, (jnp.arange(nb), qb))
    return out.transpose(1, 0, 2, 3, 4, 5).reshape(b, s, ATTN_DIM)

def peer_ffn(h, w_query, sub_keys, expert_u, expert_v):
    b, s, d = h.shape
    hc_all = h.reshape((b * s) // TOKEN_CHUNK, TOKEN_CHUNK, d)

    def chunk_fn(hc):
        q = (hc @ w_query).reshape(TOKEN_CHUNK, PEER_HEADS, 2, PEER_HALF)
        sc = jnp.einsum('thpd,pnd->thpn', q, sub_keys).astype(jnp.float32)
        vals, idx = lax.top_k(sc, PEER_TOPK)
        cand = vals[:, :, 0, :, None] + vals[:, :, 1, None, :]
        cand_idx = idx[:, :, 0, :, None] * N_KEYS + idx[:, :, 1, None, :]
        cand = cand.reshape(TOKEN_CHUNK, PEER_HEADS, PEER_TOPK * PEER_TOPK)
        cand_idx = cand_idx.reshape(TOKEN_CHUNK, PEER_HEADS, PEER_TOPK * PEER_TOPK)
        top_s, pos = lax.top_k(cand, PEER_TOPK)
        expert_idx = jnp.take_along_axis(cand_idx, pos, axis=-1)
        gate = jax.nn.softmax(top_s, axis=-1)
        u = expert_u[expert_idx]
        act = jax.nn.gelu(jnp.einsum('thkd,td->thk', u, hc).astype(jnp.float32), approximate=False)
        vv = expert_v[expert_idx]
        return jnp.einsum('thk,thkd->td', (gate * act).astype(hc.dtype), vv)

    return lax.map(chunk_fn, hc_all).reshape(b, s, d)

def second_inputs(seed: int = 0) -> dict:
    key = jax.random.key(seed)
    ks = jax.random.split(key, 18)
    f32 = jnp.float32
    nrm = lambda k, shape, sc: jax.random.normal(k, shape, f32) * sc
    return {
        "x": nrm(ks[0], (BATCH, SEQ, D_MODEL), 1.0),
        "norm1_g": 1.0 + nrm(ks[1], (DEPTH, D_MODEL), 0.02),
        "w_in": nrm(ks[2], (DEPTH, D_MODEL, IN_DIM), D_MODEL ** -0.5),
        "conv_dw_w": nrm(ks[3], (DEPTH, CONV_KERNEL, CONV_DIM), CONV_KERNEL ** -0.5),
        "conv_dw_b": nrm(ks[4], (DEPTH, CONV_DIM), 0.02),
        "conv_ln_g": 1.0 + nrm(ks[5], (DEPTH, CONV_DIM), 0.02),
        "conv_ln_b": nrm(ks[6], (DEPTH, CONV_DIM), 0.02),
        "conv_w_pw": nrm(ks[7], (DEPTH, CONV_DIM, D_MODEL), CONV_DIM ** -0.5),
        "attn_sink": nrm(ks[8], (DEPTH, N_HEADS), 0.5),
        "attn_w_o": nrm(ks[9], (DEPTH, ATTN_DIM, D_MODEL), ATTN_DIM ** -0.5),
        "w_out": nrm(ks[10], (DEPTH, D_MODEL, D_MODEL), D_MODEL ** -0.5),
        "norm2_g": 1.0 + nrm(ks[11], (DEPTH, D_MODEL), 0.02),
        "peer_w_query": nrm(ks[12], (DEPTH, D_MODEL, PEER_HEADS * PEER_KEY_DIM), D_MODEL ** -0.5),
        "peer_sub_keys": nrm(ks[13], (DEPTH, 2, N_KEYS, PEER_HALF), PEER_HALF ** -0.5),
        "peer_u": nrm(ks[14], (DEPTH, N_EXPERTS, D_MODEL), D_MODEL ** -0.5),
        "peer_v": nrm(ks[15], (DEPTH, N_EXPERTS, D_MODEL), 0.25),
        "final_g": 1.0 + nrm(ks[16], (D_MODEL,), 0.02),
    }

def second_block(x, norm1_g, w_in, conv_dw_w, conv_dw_b, conv_ln_g, conv_ln_b, conv_w_pw,
              attn_sink, attn_w_o, w_out, norm2_g, peer_w_query, peer_sub_keys,
              peer_u, peer_v, final_g):
    b, s, d = x.shape
    o_conv = 2 * CONV_DIM
    o_q = o_conv + ATTN_DIM
    o_k = o_q + KV_DIM
    o_v = o_k + KV_DIM
    for l in range(DEPTH):
        h = rmsnorm_2(x, norm1_g[l])
        z = h @ w_in[l]
        conv_in = z[..., :o_conv]
        q = z[..., o_conv:o_q].reshape(b, s, N_HEADS, HEAD_DIM)
        k = z[..., o_q:o_k].reshape(b, s, N_KV_HEADS, HEAD_DIM)
        v = z[..., o_k:o_v].reshape(b, s, N_KV_HEADS, HEAD_DIM)
        gates = jax.nn.sigmoid(z[..., o_v:].astype(jnp.float32)).astype(x.dtype)
        gates = gates.reshape(b, s, N_BRANCH, d)
        conv_out = conformer_conv(conv_in, conv_dw_w[l], conv_dw_b[l], conv_ln_g[l],
                                  conv_ln_b[l], conv_w_pw[l])
        attn_out = windowed_gqa(q, k, v, attn_sink[l]) @ attn_w_o[l]
        merged = gates[:, :, 0, :] * conv_out + gates[:, :, 1, :] * attn_out
        x = x + merged @ w_out[l]
        h2 = rmsnorm_2(x, norm2_g[l])
        x = x + peer_ffn(h2, peer_w_query[l], peer_sub_keys[l], peer_u[l], peer_v[l])
    return rmsnorm_2(x, final_g)


def setup_inputs(seed=0):
    out = dict(first_inputs(seed))
    for name, value in second_inputs(seed + 1).items():
        if name != "x":
            out[name + "_2"] = value
    return out


def reference(
    x, attn_norm_w, w_in, q_norm_w, k_norm_w, rel_bias, conv_w, out_norm_w, w_out, ffn_norm_w,
    w_gate, w_up, w_down, norm1_g_2, w_in_2, conv_dw_w_2, conv_dw_b_2, conv_ln_g_2, conv_ln_b_2,
    conv_w_pw_2, attn_sink_2, attn_w_o_2, w_out_2, norm2_g_2, peer_w_query_2, peer_sub_keys_2,
    peer_u_2, peer_v_2, final_g_2,
):
    x = first_block(
        x, attn_norm_w, w_in, q_norm_w, k_norm_w, rel_bias, conv_w, out_norm_w, w_out,
        ffn_norm_w, w_gate, w_up, w_down,
    )
    return second_block(
        x, norm1_g_2, w_in_2, conv_dw_w_2, conv_dw_b_2, conv_ln_g_2, conv_ln_b_2, conv_w_pw_2,
        attn_sink_2, attn_w_o_2, w_out_2, norm2_g_2, peer_w_query_2, peer_sub_keys_2, peer_u_2,
        peer_v_2, final_g_2,
    )


_drawn_inputs = setup_inputs


def setup_inputs(seed=0):
    import zlib

    import numpy as np

    out = dict(_drawn_inputs(seed))
    spreads = {}
    factors = {'q_norm_w': 3.619,
     'k_norm_w': 4.307,
     'out_norm_w': 3.01,
     'ffn_norm_w': 3.867,
     'norm1_g_2': 6.158,
     'conv_dw_b_2': 38.358,
     'conv_ln_g_2': 56.776,
     'conv_ln_b_2': 63.544,
     'attn_sink_2': 7.041,
     'norm2_g_2': 35.8,
     'final_g_2': 7.461}
    for name, (base, spread) in spreads.items():
        noise = np.random.default_rng([zlib.crc32(name.encode()), seed]).standard_normal(out[name].shape)
        drawn = base * np.exp(spread * noise) if base else spread * noise
        out[name] = __import__('jax').numpy.asarray(drawn.astype(out[name].dtype))
    for name, factor in factors.items():
        out[name] = (out[name] * factor).astype(out[name].dtype)
    return out
```

```python
from contextlib import ExitStack

import numpy as np

import concourse.bass as bass
from concourse import mybir

F32 = mybir.dt.float32
F32R = mybir.dt.float32r
BF16 = mybir.dt.bfloat16
U32 = mybir.dt.uint32
U16 = mybir.dt.uint16
ALU = mybir.AluOpType
ACT = mybir.ActivationFunctionType
AX_X = mybir.AxisListType.X

P = 128
D = 1024
KD = D // P
T = 512
TT = T // P
HD = 64
EPS = 1e-6
QSCALE = HD ** -0.5
NEG = -1e30

H_SB, H_CH = 4, 8
FF = 2816
KF = FF // P
KF_PAD = 24
CONV_TAPS = 31
REL = T + P
CONV_PAD = 15
UW = T + 2 * CONV_PAD
N_HEADS = 16
PH, TOPK, NKEY = 8, 16, 128
RING = 4
AHEAD = 2

N_IN, N_OUT, N_GU, N_DOWN = 24, 8, 2 * KF, 3 * KD
N_IN2, N_Q = 44, 16
S_IN = 0
S_OUT = S_IN + N_IN
S_GU = S_OUT + N_OUT
S_DOWN = S_GU + N_GU
S_IN2 = S_DOWN + N_DOWN
S_PW = S_IN2 + N_IN2
S_WO = S_PW + KD
S_WO2 = S_WO + KD
S_Q = S_WO2 + KD
S_PEER = S_Q + N_Q
N_SLOTS = S_PEER + 2 * NKEY
T_IN = 0
T_OUT = T_IN + N_IN
T_GU = T_OUT + N_OUT
T_DOWN = T_GU + N_GU
T_IN2 = T_DOWN + KD
T_PW = T_IN2 + N_IN2
T_WO = T_PW + KD
T_WO2 = T_WO + KD
T_Q = T_WO2 + KD

GC = {}
_at = 0
for _name, _n in (("attn", KD), ("out", KD), ("ffn", KD), ("norm1", KD), ("norm2", KD), ("final", KD),
                  ("ln_g", KD), ("ln_b", KD), ("dw_b", KD), ("dw", KD * CONV_TAPS), ("conv", 6),
                  ("qn", 1), ("kn", 1), ("sink", N_HEADS), ("eps", 1)):
    GC[_name] = _at
    _at += _n
N_GC = _at

CC = {"ident": 0, "ones": 128, "blk": 256, "tri": 384, "mask": 512, "neg": 640, "iota": 768}
N_CC = 784
GRP = 16
PAIRS = GRP // 2
N_GRP = NKEY // GRP
TB = 16
SLICE = T // PAIRS
NB = T // TB


class Chain:

    def __init__(self, eng, sem):
        self.eng, self.sem, self.n, self.loops = eng, sem, 0, []

    def loop(self, i, lo, hi, per):
        self.loops.append((i, lo, hi, per, self.n))

    def end(self):
        _, lo, hi, per, n = self.loops.pop()
        assert self.n == n + per, (self.n - n, per)
        self.n = n + (hi - lo) * per

    def mark(self, ins):
        ins.then_inc(self.sem, 1)
        self.n += 1
        value = self.n
        for i, lo, _, per, _ in self.loops:
            value = i * per + (value - lo * per) if isinstance(value, int) else value + i * per + (-lo * per)
        return value

    def wait(self, value):
        self.eng.wait_ge(self.sem, value)

    def __call__(self, ins):
        self.wait(self.mark(ins))


def program(nc, x, stream, gains, consts, rel, gqa, keys, ohc, out):
    ctx = ExitStack()
    with ctx:
        at = [16512]

        def fixed(name, shape, dt=F32):
            size = int(np.prod(shape[1:])) * (2 if dt == BF16 else 4)
            t = nc.alloc_sbuf_tensor_at(name, shape, dt, offset=at[0])
            at[0] += -(-size // 32) * 32
            return t

        def sem(name):
            return ctx.enter_context(nc.semaphore(name))

        xT = fixed("xT", [P, KD, T])
        inH = fixed("inH", [P, KD, T], F32R)
        inL = fixed("inL", [P, KD, T], F32R)
        raw = fixed("raw", [P, RING, D])
        hi = fixed("hi", [P, RING, D], F32R)
        lo = fixed("lo", [P, RING, D], F32R)
        gn = fixed("gn", [P, N_GC])
        cs = fixed("cs", [P, N_CC])
        sq_at = at[0]
        sq = fixed("sq", [P, 2, T])
        rt = fixed("rt", [P, 2, T])
        res = fixed("res", [P, T])
        arena = at[0]

        def phase():
            at[0] = arena

        phase()
        qk1 = fixed("qk1", [P, 12, T])
        cv1 = fixed("cv1", [P, 6, T])
        v1 = fixed("v1", [P, TT, 768])
        y1 = fixed("y1", [P, KD, T])
        tbl1 = fixed("tbl1", [P, 2, T])
        shared = at[0]
        lr = fixed("lr", [P, TT, T])
        ez = fixed("ez", [P, 2, T])
        mz = fixed("mz", [P, 2, T])
        wz = fixed("wz", [P, 2, T])
        at[0] = shared
        lg1 = fixed("lg1", [P, 2, T])
        pr1 = fixed("pr1", [P, 2, T])
        pT1 = fixed("pT1", [P, 2, T])
        sm1 = fixed("sm1", [P, 2, 8])
        phase()
        actH = fixed("actH", [P, KF, T], F32R)
        actL = fixed("actL", [P, KF, T], F32R)
        phase()
        u2 = fixed("u2", [P, KD, UW])
        qk2 = fixed("qk2", [P, 10, T])
        v2 = fixed("v2", [P, TT, 256])
        gate2 = fixed("gate2", [P, 16, T])
        c2_at = at[0]
        c2 = fixed("c2", [P, KD, T])
        at[0] = c2_at
        lg2 = fixed("lg2", [P, 2, T])
        pr2 = fixed("pr2", [P, 2, T])
        pT2 = fixed("pT2", [P, 2, T])
        tbl2 = fixed("tbl2", [P, 2, 384])
        sm2 = fixed("sm2", [P, 2, 8])
        m2 = u2
        phase()
        gpart = fixed("gpart", [P, 3, T], BF16)
        i1T = fixed("i1T", [P, T], BF16)
        i2T = fixed("i2T", [P, T], BF16)
        iota2 = fixed("iota2", [P, NKEY, TB], BF16)
        peer_at = at[0]
        qp = fixed("qp", [P, N_Q, T])
        key_sb = fixed("key_sb", [P, 2, NKEY])
        sc = fixed("sc", [P, N_Q, NKEY])
        scb = fixed("scb", [P, 2, NKEY])
        cand = fixed("cand", [P, PH, TOPK * TOPK])
        candb = fixed("candb", [P, TOPK * TOPK])
        eq = fixed("eq", [P, PH * TOPK, TOPK])
        vals = fixed("vals", [P, N_Q, TOPK])
        idx = fixed("idx", [P, N_Q, TOPK], U32)
        idxf = fixed("idxf", [P, N_Q, TOPK])
        top = fixed("top", [P, PH, TOPK])
        pos = fixed("pos", [P, PH, TOPK], U32)
        posb = fixed("posb", [P, 2, PH * TOPK], U32)
        posf = fixed("posf", [P, 2, PH * TOPK])
        sel = fixed("sel", [P, 3, PH * TOPK])
        den = fixed("den", [P, 2, PH])
        gT = fixed("gT", [P, T])
        at[0] = peer_at
        Gd = fixed("Gd", [P, 2, GRP, T])
        WH = fixed("WH", [P, 2, 2, T], F32R)
        WL = fixed("WL", [P, 2, 2, T], F32R)
        oh2 = fixed("oh2", [P, 2, NKEY, TB], BF16)
        assert at[0] <= 229344, at[0]
        at[0] = sq_at
        iota1 = fixed("iota1", [P, GRP, TB], BF16)
        oh1 = fixed("oh1", [P, GRP, TB], BF16)
        ohg = fixed("ohg", [P, 2, 3, GRP, TB], BF16)
        assert at[0] <= sq_at + 2 * T * 4

        B = [ctx.enter_context(nc.psum_tensor(f"bank{i}", [P, T], F32)) for i in range(8)]

        loaded = [sem(f"loaded{r}") for r in range(RING)]
        hi_done = sem("hi_done")
        lo_done = sem("lo_done")
        slot_used = sem("slot_used")
        evac = sem("evac")
        small_in = sem("small_in")
        squares = sem("squares")
        sums = sem("sums")
        roots = sem("roots")
        in_ready = sem("in_ready")
        dve_steps = sem("dve_steps")
        act_steps = sem("act_steps")
        z_done = sem("z_done")
        z_abs = sem("z_abs")
        z_soft = sem("z_soft")
        z_min = sem("z_min")
        lr_ready = sem("lr_ready")
        s_done = sem("s_done")
        s_masked = sem("s_masked")
        w_exp = sem("w_exp")
        w_ready = sem("w_ready")
        sb_out = sem("sb_out")
        att = [{n: sem(f"{n}{a}") for n in ("score", "logit", "maxed", "probs", "normed", "turned",
                                           "turned_sb", "mixed", "head_out", "tbl_free")} for a in (1, 2)]
        tbl_in = [[sem(f"tbl_in{a}{b}") for b in (0, 1)] for a in (1, 2)]
        y_sb = sem("y_sb")
        conv_done = sem("conv_done")
        mean_done = sem("mean_done")
        silu_ready = sem("silu_ready")
        peer_in = sem("peer_in")
        sc_done = sem("sc_done")
        sc_copied = sem("sc_copied")
        sc_used = sem("sc_used")
        top_ready = sem("top_ready")
        gexp = sem("gexp")
        sel_ready = sem("sel_ready")
        selT_done = sem("selT_done")
        selT_copied = sem("selT_copied")
        oh_ready = sem("oh_ready")
        g_built = sem("g_built")
        g_evac = sem("g_evac")
        gelu_done = sem("gelu_done")
        w_done = sem("w_done")
        y_done = sem("y_done")
        y_added = sem("y_added")
        out_done = sem("out_done")
        final_done = sem("final_done")
        u_done = sem("u_done")
        gate_act = sem("gate_act")
        sig_act = sem("sig_act")

        ident = cs[:, CC["ident"]:CC["ident"] + P]
        ones = cs[:, CC["ones"]:CC["ones"] + P]
        blk = cs[:, CC["blk"]:CC["blk"] + P]
        tri = cs[:, CC["tri"]:CC["tri"] + P]
        mask = cs[:, CC["mask"]:CC["mask"] + P]
        neg = cs[:, CC["neg"]:CC["neg"] + P]
        iota16 = cs[:, CC["iota"]:CC["iota"] + TOPK]

        def gain(name, k=0):
            return gn[:, GC[name] + k:GC[name] + k + 1]


        units1 = []
        for h in range(H_CH):
            for i in range(TT):
                units1.append(dict(q=4 + h // 2, k=8 + h // 2, row=HD * (h % 2), i=i, k0=0, n=(i + 1) * P,
                                   c0=(TT - 1 - i) * P, head=h, sink=None, v=256 + HD * h, pair=h // 2, dst=2 + h // 2))
        units2 = []
        for j in range(N_HEADS // 2):
            for half in (0, 1):
                kv = 2 * (j // 4) + half
                head = 4 * kv + j % 4
                for i in range(TT):
                    first, last = max(i - 1, 0), min(i + 1, TT - 1)
                    units2.append(dict(q=j, k=8 + kv // 2, row=HD * half, i=i, k0=first * P,
                                       n=(last - first + 1) * P, c0=(first - i + 1) * P, head=head,
                                       sink=head, v=HD * kv, pair=j, dst=j))
        stage1 = dict(units=units1, qk=qk1, v=v1, tbl=tbl1, lg=lg1, pr=pr1, pT=pT1, sm=sm1, s=att[0], tbl_in=tbl_in[0],
                      dst=y1)
        stage2 = dict(units=units2, qk=qk2, v=v2, tbl=tbl2, lg=lg2, pr=pr2, pT=pT2, sm=sm2, s=att[1], tbl_in=tbl_in[1],
                      dst=qk2)


        block = ctx.enter_context(nc.Block())

        @block.sync
        def _(sp):
            def load(n, r):
                sp.dma_start(raw[:, r, :], stream[bass.ds(n, 1)].rearrange("a p n -> (a p) n")).then_inc(loaded[r], 16)

            sp.dma_start(gn[:, :], gains).then_inc(small_in, 16)
            sp.dma_start(cs[:, :], consts).then_inc(small_in, 16)
            sp.dma_start(xT[:, :, :], x).then_inc(small_in, 16)
            for r in range(RING):
                load(r, r)
            with sp.Fori(1, N_SLOTS // RING) as i:
                for r in range(RING):
                    sp.wait_ge(lo_done, i * RING + (r - RING + 1))
                    load(i * RING + r, r)
            for n in range(N_SLOTS // RING * RING, N_SLOTS):
                sp.wait_ge(lo_done, n - RING + 1)
                load(n, n % RING)

        @block.gpsimd
        def _(pool):
            def low(n, r):
                pool.wait_ge(hi_done, n + 1)
                pool.tensor_tensor(lo[:, r, :], raw[:, r, :], hi[:, r, :].bitcast(F32), ALU.subtract).then_inc(lo_done, 1)

            with pool.Fori(0, N_SLOTS // RING) as i:
                for r in range(RING):
                    low(i * RING + r, r)
            for n in range(N_SLOTS // RING * RING, N_SLOTS):
                low(n, n % RING)

        @block.scalar
        def _(act):
            chain = Chain(act, act_steps)

            def high(n0, i, r, first=False):
                n = i * RING + (n0 + r)
                act.wait_ge(loaded[r % RING], i * 16 + 16 * ((n0 + r) // RING + 1))
                if not first:
                    act.wait_ge(slot_used, n - RING + 1)
                act.activation(hi[:, r % RING, :], raw[:, r % RING, :], ACT.Copy).then_inc(hi_done, 1)

            def highs(s0, n, epilogue=None):
                with act.Fori(0, n // RING) as i:
                    for r in range(RING):
                        high(s0, i, r + AHEAD)
                        if epilogue:
                            epilogue(i, r)

            def root_of(bank, dst, scale, n_sums, n_sq):
                act.wait_ge(sums, n_sums)
                if n_sq:
                    act.wait_ge(*n_sq)
                act.activation(dst, bank, ACT.Sqrt, bias=gain("eps"), scale=scale).then_inc(roots, 1)

            def group_roots(nth_sum):
                for k in range(KD):
                    root_of(B[4 + k % 4][:, :], rt[:, k % 2, :], 1.0 / HD, nth_sum + k + 1, None)

            def table(st, head):
                src = (bass.AP(tensor=rel.tensor, offset=head * P * REL + P - 1, ap=[[REL - 1, P], [1, T]]) if st is stage1
                       else gqa[head])
                act.dma_start(st["tbl"][:, head % 2, :], src).then_inc(st["tbl_in"][head % 2], 16)

            def attention(st):
                s, units = st["s"], st["units"]
                n = len(units)
                for u in range(n + 3):
                    if 0 < u < n and u % TT == 0 and u // TT + 1 < n // TT:
                        act.wait_ge(s["maxed"], u)
                        table(st, u // TT + 1)
                    if u < n:
                        w = units[u]
                        lg, pr, sm = st["lg"][:, u % 2, :w["n"]], st["pr"][:, u % 2, :w["n"]], st["sm"][:, u % 2, :]
                        act.wait_ge(s["maxed"], u + 1)
                        if u >= 2:
                            act.wait_ge(s["turned"], u - 1)
                        e = act.activation(pr, lg, ACT.Exp, bias=sm[:, 1:2], accum_out=sm[:, 2:3])
                        if w["sink"] is None:
                            e.then_inc(s["probs"], 1)
                        else:
                            act.activation(sm[:, 3:4], gain("sink", w["sink"]), ACT.Exp, bias=sm[:, 1:2]).then_inc(s["probs"], 1)
                    if 1 <= u <= n:
                        v = u - 1
                        w = units[v]
                        act.wait_ge(s["turned"], v + 1)
                        if v >= 2:
                            act.wait_ge(s["mixed"], v - 1)
                        act.activation(st["pT"][:, v % 2, :w["n"]], B[6 + v % 2][:, :w["n"]], ACT.Copy).then_inc(s["turned_sb"], 1)
                    v = u - 3
                    if v >= 0 and (v == n - 1 or units[v + 1]["pair"] != units[v]["pair"]):
                        pair = units[v]["pair"]
                        act.wait_ge(s["mixed"], v + 1)
                        act.activation(st["dst"][:, units[v]["dst"], :], B[2 + pair % 2][:, :], ACT.Copy).then_inc(s["head_out"], 1)

            table(stage1, 0)
            table(stage1, 1)
            act.wait_ge(small_in, 48)
            for n in range(AHEAD):
                high(0, 0, n, first=True)
            root_of(B[4][:, :], rt[:, 0, :], 1.0 / D, KD, None)
            n_sums = KD
            for r in range(RING):
                high(S_IN, 0, r + AHEAD, first=r + AHEAD < RING)
            with act.Fori(1, N_IN // RING) as i:
                for r in range(RING):
                    high(S_IN, i, r + AHEAD)
            n = 0
            for h in range(H_SB):
                for kb in reversed(range(TT)):
                    w = T - kb * P
                    act.wait_ge(z_done, n + 1)
                    if n >= 2:
                        act.wait_ge(lr_ready, n - 1)
                    act.activation(ez[:, n % 2, :w], B[2 + n % 2][:, :w], ACT.Abs).then_inc(z_abs, 1)
                    act.wait_ge(z_abs, n + 1)
                    chain(act.activation(ez[:, n % 2, :w], ez[:, n % 2, :w], ACT.Exp, scale=-1.0))
                    act.activation(ez[:, n % 2, :w], ez[:, n % 2, :w], ACT.Ln, bias=1.0).then_inc(z_soft, 1)
                    act.wait_ge(s_masked, n + 1)
                    if n >= 2:
                        act.wait_ge(sb_out, n - 1)
                    e = act.activation(wz[:, n % 2, :P], mz[:, n % 2, :P], ACT.Exp)
                    if w > P:
                        e = act.activation(wz[:, n % 2, P:w], B[4 + n % 2][:, P:w], ACT.Exp)
                    e.then_inc(w_exp, 1)
                    n += 1
                if h % 2:
                    act.wait_ge(sb_out, n)
                    act.activation(y1[:, h // 2, :], B[6 + h // 2][:, :], ACT.Copy).then_inc(y_sb, 1)
            group_roots(n_sums)
            n_sums += KD
            attention(stage1)
            group_roots(n_sums)
            n_sums += KD
            highs(S_OUT, N_OUT)
            root_of(B[4][:, :], rt[:, 0, :], 1.0 / D, n_sums + KD, None)
            n_sums += KD

            def silu(i, r):
                if r % 2 == 0:
                    act.wait_ge(evac, i * RING + (T_GU + r - 2))
                    act.wait_ge(slot_used, i * RING + (S_GU + r + 1))
                    act.activation(sq[:, r // 2, :], B[r][:, :], ACT.Silu).then_inc(gate_act, 1)

            highs(S_GU, N_GU, silu)
            highs(S_DOWN, N_DOWN)
            root_of(B[4][:, :], rt[:, 0, :], 1.0 / D, n_sums + KD, None)
            n_sums += KD

            def sigm(i, r):
                if r % 2 == 1:
                    act.wait_ge(evac, i * RING + (T_IN2 + r - 3))
                    act.wait_ge(slot_used, i * RING + (S_IN2 + r + 1))
                    act.activation(sq[:, r // 2, :], B[r][:, :], ACT.Sigmoid).then_inc(sig_act, 1)

            highs(S_IN2, 16, sigm)
            act.wait_ge(evac, T_IN2 + 16)
            for m in range(16, N_IN2):
                high(S_IN2, 0, m + AHEAD)
                act.wait_ge(slot_used, S_IN2 + m + 1)
                bank = B[m % RING]
                if m < 26:
                    e = act.activation(qk2[:, m - 16, :], bank[:, :], ACT.Copy)
                elif m < 42:
                    e = act.activation(gate2[:, m - 26, :], bank[:, :], ACT.Sigmoid)
                else:
                    e = act.activation(v2[:, :, (m - 42) * P:(m - 41) * P], bank[:, :].rearrange("p (t c) -> p t c", t=TT), ACT.Copy)
                e.then_inc(evac, 1)
            root_of(B[5][:, :], rt[:, 0, :], 1.0 / D, n_sums + KD, None)
            n_sums += KD
            for k in range(KD):
                act.wait_ge(conv_done, KD + k + 1)
                act.activation(sq[:, k % 2, :], c2[:, k, :], ACT.Silu).then_inc(silu_ready, 1)
            highs(S_PW, KD)
            act.wait_ge(in_ready, 6)
            table(stage2, 0)
            table(stage2, 1)
            attention(stage2)
            highs(S_WO, KD)
            highs(S_WO2, KD)
            root_of(B[4][:, :], rt[:, 0, :], 1.0 / D, n_sums + KD, None)
            n_sums += KD
            act.wait_ge(in_ready, 9)
            act.dma_start(iota2[:, :, :].bitcast(U16), ohc[:, 0:NKEY, :]).then_inc(peer_in, 16)
            act.dma_start(iota1[:, :, :].bitcast(U16), ohc[:, NKEY:NKEY + GRP, :]).then_inc(peer_in, 16)
            act.dma_start(key_sb[:, :, :], keys).then_inc(peer_in, 16)
            for m in range(N_Q):
                high(S_Q, 0, m + AHEAD)
                act.wait_ge(evac, T_Q + m)
                act.wait_ge(slot_used, S_Q + m + 1)
                act.activation(qp[:, m, :], B[m % RING][:, :], ACT.Copy).then_inc(evac, 1)
            for t in range(TT):
                if t:
                    act.wait_ge(sc_used, t)
                for b in range(4):
                    act.wait_ge(sc_done, 4 * t + b + 1)
                    act.activation(sc[:, 4 * b:4 * b + 4, :], B[4 + b][:, :], ACT.Copy).then_inc(sc_copied, 1)
                act.wait_ge(top_ready, t + 1)
                act.activation(sel[:, 0, :], sel[:, 0, :], ACT.Exp).then_inc(gexp, 1)
                act.wait_ge(selT_done, t + 1)
                act.activation(gT[:, t * P:(t + 1) * P], B[0][:, 0:P], ACT.Copy)
                act.activation(i1T[:, t * P:(t + 1) * P], B[0][:, P:2 * P], ACT.Copy)
                act.activation(i2T[:, t * P:(t + 1) * P], B[0][:, 2 * P:3 * P], ACT.Copy).then_inc(selT_copied, 1)

            def gelu(e, done):
                act.wait_ge(u_done, done)
                act.activation(B[e][:, :], B[e][:, :], ACT.Gelu).then_inc(gelu_done, 1)

            def high_peer(i, r, n_loads):
                act.wait_ge(loaded[r], i * 16 + n_loads * 16)
                act.wait_ge(small_in, 48)
                act.activation(hi[:, r, :], raw[:, r, :], ACT.Copy).then_inc(hi_done, 1)

            for e in (0, 1):
                high(S_PEER, 0, e + AHEAD)
                gelu(e, e + 1)
            def pair(j):
                for e in (0, 1):
                    act.wait_ge(*((u_done, 2) if isinstance(j, int) else (y_done, j * KD + (-KD))))
                    high_peer(j, e, S_PEER // RING + 1)
                    gelu(e, j * 2 + (e + 1))
                for e in (0, 1):
                    act.wait_ge(u_done, j * 2 + (e + 1))
                    high_peer(j, e + 2, S_PEER // RING + 1)

            pair(1)
            with act.Fori(2, NKEY // 2) as j:
                pair(j)
            root_of(B[2][:, :], rt[:, 0, :], 1.0 / D, n_sums + KD, None)
            for k in range(KD):
                act.wait_ge(final_done, k + 1)
                act.dma_start(out[:, k, :], xT[:, k, :]).then_inc(out_done, 16)
            act.wait_ge(out_done, 16 * KD)

        @block.vector
        def _(dve):
            chain = Chain(dve, dve_steps)

            def split(src, h, l):
                chain(dve.tensor_scalar(h, src, 1.0, None, ALU.mult))
                chain(dve.tensor_tensor(l, src, h.bitcast(F32), ALU.subtract))

            def square_sums(src, n):
                for k in range(KD):
                    if k >= 2:
                        dve.wait_ge(sums, n + k - 1)
                    dve.tensor_tensor(sq[:, k % 2, :], src(k), src(k), ALU.mult).then_inc(squares, 1)

            def norm(src, gname, n, nth_root):
                square_sums(src, n)
                dve.wait_ge(roots, nth_root)
                chain(dve.reciprocal(rt[:, 1, :], rt[:, 0, :]))
                for k in range(KD):
                    chain(dve.scalar_tensor_tensor(res[:, :], src(k), gain(gname, k), rt[:, 1, :], ALU.mult, ALU.mult))
                    split(res[:, :], inH[:, k, :], inL[:, k, :])

            def group_norm(src, gains_of, put, n, nth_root):
                def square(k):
                    if k >= 2:
                        dve.wait_ge(sums, n + k - 1)
                    dve.tensor_tensor(sq[:, k % 2, :], src(k), src(k), ALU.mult).then_inc(squares, 1)
                square(0)
                for k in range(KD):
                    if k + 1 < KD:
                        square(k + 1)
                    dve.wait_ge(roots, nth_root + k + 1)
                    chain(dve.reciprocal(rt[:, k % 2, :], rt[:, k % 2, :]))
                    put(k)

            def take(n, ins):
                ins.then_inc(evac, 1)

            def attention(st):
                s, units = st["s"], st["units"]
                n = len(units)
                for u in range(n + 1):
                    if u < n:
                        w = units[u]
                        lg, sm = st["lg"][:, u % 2, :w["n"]], st["sm"][:, u % 2, :]
                        hn = u // TT
                        if u % TT == 0:
                            dve.wait_ge(st["tbl_in"][hn % 2], 16 * (hn // 2 + 1))
                            if st is stage1:
                                chain(dve.memset(tbl1[0:HD, hn % 2, T - HD:T], NEG))
                        dve.wait_ge(s["score"], u + 1)
                        chain(dve.scalar_tensor_tensor(lg, B[4 + u % 2][:, :w["n"]], QSCALE,
                              st["tbl"][:, hn % 2, w["c0"]:w["c0"] + w["n"]], ALU.mult, ALU.add))
                        dve.reduce_max(sm[:, 0:1], lg, AX_X).then_inc(s["logit"], 1)
                        dve.wait_ge(s["logit"], u + 1)
                        if w["sink"] is None:
                            dve.tensor_scalar(sm[:, 1:2], sm[:, 0:1], -1.0, None, ALU.mult).then_inc(s["maxed"], 1)
                        else:
                            dve.tensor_scalar(sm[:, 1:2], sm[:, 0:1], gain("sink", w["sink"]), -1.0, ALU.max, ALU.mult).then_inc(s["maxed"], 1)
                    if u >= 1:
                        v = u - 1
                        w = units[v]
                        sm = st["sm"][:, v % 2, :]
                        pr = st["pr"][:, v % 2, :w["n"]]
                        dve.wait_ge(s["probs"], v + 1)
                        if w["sink"] is not None:
                            chain(dve.tensor_tensor(sm[:, 2:3], sm[:, 2:3], sm[:, 3:4], ALU.add))
                        chain(dve.reciprocal(sm[:, 4:5], sm[:, 2:3]))
                        dve.tensor_scalar(pr, pr, sm[:, 4:5], None, ALU.mult).then_inc(s["normed"], 1)


            x_of = lambda k: xT[:, k, :]
            dve.wait_ge(small_in, 48)
            n_sums, n_root = 0, 0
            norm(x_of, "attn", n_sums, n_root + 1)
            dve.sem_inc(in_ready, 1)
            n_sums += KD
            n_root += 1
            for m in range(N_IN):
                dve.wait_ge(slot_used, S_IN + m + 1)
                bank = B[m % RING]
                if m < 12:
                    take(m, dve.tensor_scalar(qk1[:, m, :], bank[:, :], QSCALE if m < 2 else 1.0, None, ALU.mult))
                elif m < 18:
                    take(m, dve.tensor_copy(cv1[:, m - 12, :], bank[:, :]))
                else:
                    take(m, dve.tensor_copy(v1[:, :, (m - 18) * P:(m - 17) * P], bank[:, :].rearrange("p (t c) -> p t c", t=TT)))
            dve.wait_ge(evac, T_OUT)
            n = 0
            for h in range(H_SB):
                for kb in reversed(range(TT)):
                    w = T - kb * P
                    dve.wait_ge(z_abs, n + 1)
                    chain(dve.tensor_scalar(lr[:, kb, :w], B[2 + n % 2][:, :w], -1.0, 0.0, ALU.mult, ALU.min))
                    dve.wait_ge(z_soft, n + 1)
                    i = dve.tensor_tensor(lr[:, kb, :w], lr[:, kb, :w], ez[:, n % 2, :w], ALU.subtract)
                    chain(i)
                    dve.tensor_tensor(lr[:, kb, :P], lr[:, kb, :P], mask, ALU.mult).then_inc(lr_ready, 1)
                    dve.wait_ge(s_done, n + 1)
                    if n >= 2:
                        dve.wait_ge(w_exp, n - 1)
                    dve.tensor_tensor(mz[:, n % 2, :P], B[4 + n % 2][:, :P], neg, ALU.add).then_inc(s_masked, 1)
                    n += 1
            for m in range(2):
                gb, gc, xc = cv1[:, m, :], cv1[:, 2 + m, :], cv1[:, 4 + m, :]
                tap = [gain("conv", 3 * m + j) for j in range(3)]
                chain(dve.tensor_tensor(gc, gc, xc, ALU.mult))
                chain(dve.tensor_scalar(xc, gc, tap[2], None, ALU.mult))
                chain(dve.scalar_tensor_tensor(xc[:, 1:], gc[:, :T - 1], tap[1], xc[:, 1:], ALU.mult, ALU.add))
                chain(dve.scalar_tensor_tensor(xc[:, 2:], gc[:, :T - 2], tap[0], xc[:, 2:], ALU.mult, ALU.add))
                chain(dve.tensor_tensor(y1[:, 6 + m, :], xc, gb, ALU.mult))
            def put_qk(k):
                t = qk1[:, 4 + k, :]
                chain(dve.scalar_tensor_tensor(t, t, gain("qn" if k < 4 else "kn"), rt[:, k % 2, :], ALU.mult, ALU.mult))
            group_norm(lambda k: qk1[:, 4 + k, :], None, put_qk, n_sums, n_root)
            dve.sem_inc(in_ready, 1)
            n_sums += KD
            n_root += KD
            attention(stage1)
            dve.wait_ge(att[0]["head_out"], 4)

            def put_y(k):
                chain(dve.scalar_tensor_tensor(res[:, :], y1[:, k, :], gain("out", k), rt[:, k % 2, :], ALU.mult, ALU.mult))
                split(res[:, :], inH[:, k, :], inL[:, k, :])
            dve.wait_ge(y_sb, 2)
            group_norm(lambda k: y1[:, k, :], None, put_y, n_sums, n_root)
            dve.sem_inc(in_ready, 1)
            n_sums += KD
            n_root += KD

            def add_x(s_last, k):
                dve.wait_ge(slot_used, s_last)
                take(None, dve.tensor_tensor(xT[:, k, :], xT[:, k, :], B[k % RING][:, :], ALU.add))

            for k in range(KD):
                add_x(S_OUT + k + 1, k)
            dve.wait_ge(evac, T_GU)
            norm(x_of, "ffn", n_sums, n_root + 1)
            dve.sem_inc(in_ready, 1)
            n_sums += KD
            n_root += 1
            with dve.Fori(0, N_GU // RING) as i:
                chain.loop(i, 0, N_GU // RING, 4)
                for r in (0, 1):
                    dve.wait_ge(gate_act, i * 2 + (r + 1))
                    dve.wait_ge(slot_used, i * RING + (S_GU + 2 * r + 2))
                    chain(dve.tensor_tensor(rt[:, r, :], sq[:, r, :], B[2 * r + 1][:, :], ALU.mult))
                    h, l = actH[:, bass.ds(i * 2 + r, 1), :], actL[:, bass.ds(i * 2 + r, 1), :]
                    src = rt[:, r:r + 1, :]
                    chain(dve.tensor_scalar(h, src, 1.0, None, ALU.mult))
                    dve.tensor_tensor(l, src, h.bitcast(F32), ALU.subtract).then_inc(evac, 2)
                chain.end()
            for k in range(KD):
                add_x(S_DOWN + 3 * (k + 1), k)
            dve.wait_ge(evac, T_IN2)
            norm(x_of, "norm1", n_sums, n_root + 1)
            chain(dve.memset(u2[:, :, 0:CONV_PAD], 0.0))
            chain(dve.memset(u2[:, :, CONV_PAD + T:UW], 0.0))
            dve.sem_inc(in_ready, 1)
            n_sums += KD
            n_root += 1
            def taps(k):
                t = c2[:, k, :]
                chain(dve.tensor_scalar(t, u2[:, k, 0:T], gain("dw", k * CONV_TAPS), gain("dw_b", k), ALU.mult, ALU.add))
                for j in range(1, CONV_TAPS):
                    ins = dve.scalar_tensor_tensor(t, u2[:, k, j:j + T], gain("dw", k * CONV_TAPS + j), t, ALU.mult, ALU.add)
                    if j < CONV_TAPS - 1:
                        chain(ins)
                    else:
                        ins.then_inc(conv_done, 1)
            for k in range(KD):
                dve.wait_ge(sig_act, k + 1)
                dve.wait_ge(slot_used, S_IN2 + 2 * k + 2)
                dve.tensor_tensor(u2[:, k, CONV_PAD:CONV_PAD + T], B[2 * k % RING][:, :], sq[:, k % 2, :], ALU.mult).then_inc(evac, 2)
            dve.wait_ge(evac, T_IN2 + 16)
            for k in range(KD):
                taps(k)
            dve.wait_ge(mean_done, KD)
            dve.wait_ge(conv_done, KD)
            chain(dve.tensor_scalar(rt[:, 1, :], B[4][:, :], 1.0 / D, None, ALU.mult))
            for k in range(KD):
                chain(dve.tensor_tensor(c2[:, k, :], c2[:, k, :], rt[:, 1, :], ALU.subtract))
            square_sums(lambda k: c2[:, k, :], n_sums)
            dve.wait_ge(roots, n_root + 1)
            chain(dve.reciprocal(rt[:, 1, :], rt[:, 0, :]))
            n_sums += KD
            n_root += 1
            for k in range(KD):
                t = c2[:, k, :]
                chain(dve.scalar_tensor_tensor(t, t, gain("ln_g", k), rt[:, 1, :], ALU.mult, ALU.mult))
                dve.tensor_scalar(t, t, gain("ln_b", k), None, ALU.add).then_inc(conv_done, 1)
                if k >= 1:
                    dve.wait_ge(silu_ready, k)
                    split(sq[:, (k - 1) % 2, :], inH[:, k - 1, :], inL[:, k - 1, :])
            dve.wait_ge(silu_ready, KD)
            split(sq[:, (KD - 1) % 2, :], inH[:, KD - 1, :], inL[:, KD - 1, :])
            dve.sem_inc(in_ready, 1)
            for k in range(KD):
                dve.wait_ge(slot_used, S_PW + k + 1)
                take(None, dve.tensor_tensor(m2[:, k, :T], gate2[:, k, :], B[k % RING][:, :], ALU.mult))
            attention(stage2)
            dve.wait_ge(att[1]["head_out"], 8)
            for k in range(KD):
                split(qk2[:, k, :], inH[:, k, :], inL[:, k, :])
            dve.sem_inc(in_ready, 1)
            for k in range(KD):
                dve.wait_ge(slot_used, S_WO + k + 1)
                dve.tensor_tensor(sq[:, k % 2, :], gate2[:, KD + k, :], B[k % RING][:, :], ALU.mult).then_inc(evac, 1)
                dve.wait_ge(evac, T_WO + k + 1)
                chain(dve.tensor_tensor(m2[:, k, :T], m2[:, k, :T], sq[:, k % 2, :], ALU.add))
            for k in range(KD):
                split(m2[:, k, :T], inH[:, k, :], inL[:, k, :])
            dve.sem_inc(in_ready, 1)
            for k in range(KD):
                add_x(S_WO2 + k + 1, k)
            dve.wait_ge(evac, T_Q)
            norm(x_of, "norm2", n_sums, n_root + 1)
            n_sums += KD
            n_root += 1
            dve.sem_inc(in_ready, 1)
            dve.wait_ge(peer_in, 48)
            for t in range(TT):
                dve.wait_ge(sc_copied, 4 * t + 4)
                for g in range(N_Q):
                    s, b = sc[:, g, :], scb[:, g % 2, :]
                    chain(dve.max(out=vals[:, g, 0:8], in_=s))
                    dve.max_index(out=idx[:, g, 0:8], in_max=vals[:, g, 0:8], in_values=s)
                    chain(dve.match_replace(out=b, in_to_replace=vals[:, g, 0:8], in_values=s, imm_value=-3.0e38))
                    chain(dve.max(out=vals[:, g, 8:16], in_=b))
                    dve.max_index(out=idx[:, g, 8:16], in_max=vals[:, g, 8:16], in_values=b)
                dve.sem_inc(sc_used, 1)
                v4 = vals[:, :, :].rearrange("p (h s) k -> p h s k", s=2)
                for h in range(PH):
                    c = cand[:, h, :]
                    chain(dve.tensor_tensor(c.rearrange("p (a b) -> p a b", a=TOPK),
                                            v4[:, h, 0, :].unsqueeze(2).broadcast_to([P, TOPK, TOPK]),
                                            v4[:, h, 1, :].unsqueeze(1).broadcast_to([P, TOPK, TOPK]), ALU.add))
                    chain(dve.max(out=top[:, h, 0:8], in_=c))
                    dve.max_index(out=pos[:, h, 0:8], in_max=top[:, h, 0:8], in_values=c)
                    chain(dve.match_replace(out=candb[:, :], in_to_replace=top[:, h, 0:8], in_values=c, imm_value=-3.0e38))
                    chain(dve.max(out=top[:, h, 8:16], in_=candb[:, :]))
                    chain(dve.max_index(out=pos[:, h, 8:16], in_max=top[:, h, 8:16], in_values=candb[:, :]))
                if t:
                    dve.wait_ge(selT_copied, t)
                s0 = sel[:, 0, :].rearrange("p (h k) -> p h k", h=PH)
                dve.tensor_tensor(s0, top[:, :, :], top[:, :, 0:1].broadcast_to([P, PH, TOPK]), ALU.subtract).then_inc(top_ready, 1)
                pf = pos[:, :, :].rearrange("p h k -> p (h k)")
                chain(dve.tensor_scalar(posb[:, 0, :], pf, 4, None, ALU.logical_shift_right))
                chain(dve.tensor_scalar(posb[:, 1, :], pf, 15, None, ALU.bitwise_and))
                chain(dve.tensor_copy(posf[:, :, :], posb[:, :, :]))
                chain(dve.tensor_copy(idxf[:, :, :], idx[:, :, :]))
                i4 = idxf[:, :, :].rearrange("p (h s) k -> p h s k", s=2)
                for s in (0, 1):
                    chain(dve.tensor_tensor(eq[:, :, :], posf[:, s, :].unsqueeze(2).broadcast_to([P, PH * TOPK, TOPK]),
                                            iota16.unsqueeze(1).broadcast_to([P, PH * TOPK, TOPK]), ALU.is_equal))
                    e4 = eq[:, :, :].rearrange("p (h k) a -> p h k a", h=PH)
                    chain(dve.tensor_tensor(e4, e4, i4[:, :, s, :].unsqueeze(2).broadcast_to([P, PH, TOPK, TOPK]), ALU.mult))
                    chain(dve.tensor_reduce(sel[:, 1 + s, :], eq[:, :, :], axis=AX_X, op=ALU.add))
                dve.wait_ge(gexp, t + 1)
                chain(dve.tensor_reduce(den[:, 0, :], s0, axis=AX_X, op=ALU.add))
                chain(dve.reciprocal(den[:, 1, :], den[:, 0, :]))
                dve.tensor_tensor(s0, s0, den[:, 1, :].unsqueeze(2).broadcast_to([P, PH, TOPK]), ALU.mult).then_inc(sel_ready, 1)
            dve.wait_ge(selT_copied, TT)
            chain(dve.tensor_copy(gpart[:, 0, :], gT[:, :]))
            chain(dve.tensor_tensor(gT[:, :], gT[:, :], gpart[:, 0, :], ALU.subtract))
            chain(dve.tensor_copy(gpart[:, 1, :], gT[:, :]))
            chain(dve.tensor_tensor(gT[:, :], gT[:, :], gpart[:, 1, :], ALU.subtract))
            chain(dve.tensor_copy(gpart[:, 2, :], gT[:, :]))

            def onehots(b, t0):
                r = b % 2
                tok = bass.ds(t0, TB)
                dve.tensor_tensor(oh2[:, r, :, :], i2T[:, tok].unsqueeze(1).broadcast_to([P, NKEY, TB]), iota2[:, :, :], ALU.is_equal)
                chain(dve.tensor_tensor(oh1[:, :, :], i1T[:, tok].unsqueeze(1).broadcast_to([P, GRP, TB]), iota1[:, :, :], ALU.is_equal))
                for s in range(3):
                    o = dve.tensor_tensor(ohg[:, r, s, :, :], oh1[:, :, :],
                                          gpart[:, s, tok].unsqueeze(1).broadcast_to([P, GRP, TB]), ALU.mult)
                chain(o)
                dve.sem_inc(oh_ready, 1)

            def gates(par, t0, built):
                for half in (0, 1):
                    dve.wait_ge(g_built, built + (half + 1))
                    dve.wait_ge(small_in, 48)
                    src = B[2 + half][:, 0:8 * 3 * GRP].rearrange("p (t s i) -> p i t s", s=3, i=GRP)
                    dve.tensor_reduce(Gd[:, par, :, bass.ds(t0 + 8 * half, 8)], src, axis=AX_X, op=ALU.add).then_inc(g_evac, 1)

            def next_group():
                chain(dve.tensor_scalar(iota1[:, :, :], iota1[:, :, :], float(GRP), None, ALU.add))
                dve.memset(res[:, 0:8], 0.0)

            with dve.Fori(0, NB // 2) as i:
                chain.loop(i, 0, NB // 2, 4)
                for r in (0, 1):
                    onehots(r, i * 2 * TB + r * TB)
                    gates(0, i * 2 * TB + r * TB, i * 4 + 2 * r)
                chain.end()
            next_group()

            def pair(par, p, j, wpar, build, first=False):
                built = j * 8 + 2 * NB

                def oh(b):
                    if build:
                        dve.wait_ge(g_built, built + (2 * b - 2))
                        onehots(b, p * SLICE + b * TB)

                def ev(b):
                    if build:
                        gates(1 - par, p * SLICE + b * TB, built + 2 * b)

                def weigh(e):
                    dve.wait_ge(gelu_done, j * 2 + (e + 1))
                    g = Gd[:, par, bass.ds(p * 2 + e, 1), :].rearrange("p a t -> p (a t)")
                    chain(dve.tensor_tensor(B[e][:, :], B[e][:, :], g, ALU.mult))
                    h, l = WH[:, wpar, e, :], WL[:, wpar, e, :]
                    chain(dve.tensor_scalar(h, B[e][:, :], 1.0, None, ALU.mult))
                    dve.tensor_tensor(l, B[e][:, :], h.bitcast(F32), ALU.subtract).then_inc(w_done, 1)

                def adds(k0, k1):
                    for k in range(k0, k1):
                        if not first:
                            dve.wait_ge(y_done, (j - 1) * KD + (k + 1))
                            dve.tensor_tensor(xT[:, k, :], xT[:, k, :], B[4 + k % 4][:, :], ALU.add).then_inc(y_added, 1)

                oh(0)
                oh(1)
                dve.wait_ge(g_evac, built if build else 2 * NB * N_GRP)
                weigh(0)
                ev(0)
                ev(1)
                oh(2)
                weigh(1)
                oh(3)
                ev(2)
                adds(0, 4)
                ev(3)
                adds(4, KD)

            steps = 2 * (4 * 2 + 2 * 2)
            pair(0, 0, 0, 0, True, first=True)
            pair(0, 1, 1, 1, True)
            with dve.Fori(1, PAIRS // 2) as i:
                chain.loop(i, 1, PAIRS // 2, steps)
                for q in (0, 1):
                    pair(0, i * 2 + q, i * 2 + q, q, True)
                chain.end()
            next_group()
            with dve.Fori(0, (N_GRP - 2) // 2) as g:
                chain.loop(g, 0, (N_GRP - 2) // 2, 2 * (PAIRS // 2 * steps + 1))
                for par in (1, 0):
                    with dve.Fori(0, PAIRS // 2) as i:
                        chain.loop(i, 0, PAIRS // 2, steps)
                        for q in (0, 1):
                            pair(par, i * 2 + q, g * (2 * PAIRS) + i * 2 + (PAIRS * (2 - par) + q), q, True)
                        chain.end()
                    next_group()
                chain.end()
            with dve.Fori(0, PAIRS // 2) as i:
                chain.loop(i, 0, PAIRS // 2, 2 * 2 * 2)
                for q in (0, 1):
                    pair(1, i * 2 + q, i * 2 + ((N_GRP - 1) * PAIRS + q), q, False)
                chain.end()
            for k in range(KD):
                dve.wait_ge(y_done, (NKEY // 2 - 1) * KD + k + 1)
                dve.tensor_tensor(xT[:, k, :], xT[:, k, :], B[4 + k % 4][:, :], ALU.add).then_inc(y_added, 1)
            dve.wait_ge(y_added, NKEY // 2 * KD)
            square_sums(x_of, n_sums)
            dve.wait_ge(roots, n_root + 1)
            chain(dve.reciprocal(rt[:, 1, :], rt[:, 0, :]))
            for k in range(KD):
                dve.scalar_tensor_tensor(xT[:, k, :], xT[:, k, :], gain("final", k), rt[:, 1, :], ALU.mult, ALU.mult).then_inc(final_done, 1)

        @block.tensor
        def _(pe):
            def mm3(bank, wh, wl, xh, xl, start, stop_):
                pe.matmul(bank, wh, xh, start=start, stop=False)
                pe.matmul(bank, wh, xl, start=False, stop=False)
                return pe.matmul(bank, wl, xh, start=False, stop=stop_)

            def tile(r, bank, signal=slot_used):
                for k in range(KD):
                    c = slice(k * P, (k + 1) * P)
                    m = mm3(bank, hi[:, r, c], lo[:, r, c], inH[:, k, :], inL[:, k, :], k == 0, k == KD - 1)
                m.then_inc(signal, 1)

            def tile_by_token(r, bank):
                for t in range(TT):
                    tok = slice(t * P, (t + 1) * P)
                    for k in range(KD):
                        c = slice(k * P, (k + 1) * P)
                        m = mm3(bank[:, tok], inH[:, k, tok], inL[:, k, tok], hi[:, r, c], lo[:, r, c], k == 0, k == KD - 1)
                m.then_inc(slot_used, 1)

            def linear(s0, t0, n, lo_=0):
                with pe.Fori(lo_, n // RING) as i:
                    for r in range(RING):
                        pe.wait_ge(evac, i * RING + (t0 + r - RING + 1))
                        pe.wait_ge(lo_done, i * RING + (s0 + r + 1))
                        tile(r, B[r][:, :])

            def sum_squares(n, bank, w):
                for k in range(KD):
                    pe.wait_ge(squares, n + k + 1)
                    pe.matmul(bank, w, sq[:, k % 2, :], start=k == 0, stop=k == KD - 1).then_inc(sums, 1)

            def group_sums(n):
                for k in range(KD):
                    pe.wait_ge(squares, n + k + 1)
                    if k >= 4:
                        pe.wait_ge(roots, group_roots_before[0] + k - 3)
                    pe.matmul(B[4 + k % 4][:, :], blk, sq[:, k % 2, :], start=True, stop=True).then_inc(sums, 1)

            group_roots_before = [0]

            def attention(st):
                s, units = st["s"], st["units"]
                n = len(units)
                for u in range(n + 2):
                    if u < n:
                        w = units[u]
                        rows = slice(w["row"], w["row"] + HD)
                        if u >= 2:
                            pe.wait_ge(s["logit"], u - 1)
                        pe.matmul(B[4 + u % 2][:, :w["n"]], st["qk"][rows, w["q"], w["i"] * P:(w["i"] + 1) * P],
                                  st["qk"][rows, w["k"], w["k0"]:w["k0"] + w["n"]], start=True, stop=True).then_inc(s["score"], 1)
                    if 1 <= u <= n:
                        v = u - 1
                        w = units[v]
                        pe.wait_ge(s["normed"], v + 1)
                        if v >= 2:
                            pe.wait_ge(s["turned_sb"], v - 1)
                        for b in range(w["n"] // P):
                            c = slice(b * P, (b + 1) * P)
                            m = pe.transpose(B[6 + v % 2][:, c], st["pr"][:, v % 2, c], ident)
                        m.then_inc(s["turned"], 1)
                    if u >= 2:
                        v = u - 2
                        w = units[v]
                        pe.wait_ge(s["turned_sb"], v + 1)
                        if w["pair"] >= 2 and (v == 0 or units[v - 1]["pair"] != w["pair"]):
                            pe.wait_ge(s["head_out"], w["pair"] - 1)
                        nb = w["n"] // P
                        for b in range(nb):
                            m = pe.matmul(B[2 + w["pair"] % 2][w["row"]:w["row"] + HD, w["i"] * P:(w["i"] + 1) * P],
                                          st["v"][:, w["k0"] // P + b, w["v"]:w["v"] + HD],
                                          st["pT"][:, v % 2, b * P:(b + 1) * P], start=b == 0, stop=b == nb - 1)
                        m.then_inc(s["mixed"], 1)


            pe.wait_ge(small_in, 48)
            n_sq, n_rt = 0, 0
            sum_squares(n_sq, B[4][:, :], ones)
            n_sq += KD
            n_rt += 1
            pe.wait_ge(in_ready, 1)
            for r in range(RING):
                pe.wait_ge(lo_done, r + 1)
                tile(r, B[r][:, :])
            linear(S_IN, T_IN, 16, 1)
            for m in range(16, N_IN):
                pe.wait_ge(evac, m - RING + 1)
                pe.wait_ge(lo_done, m + 1)
                (tile if m < 18 else tile_by_token)(m % RING, B[m % RING][:, :])
            pe.wait_ge(evac, T_OUT)
            n = 0
            for h in range(H_SB):
                rows = slice(HD * (h % 2), HD * (h % 2) + HD)
                q, k = qk1[rows, h // 2, :], qk1[rows, 2 + h // 2, :]
                for kb in reversed(range(TT)):
                    w = T - kb * P
                    if n >= 2:
                        pe.wait_ge(lr_ready, n - 1)
                    kt = k[:, kb * P:(kb + 1) * P]
                    pe.matmul(B[2 + n % 2][:, :w], kt, q[:, kb * P:], start=True, stop=True).then_inc(z_done, 1)
                    pe.wait_ge(lr_ready, n + 1)
                    if n >= 2:
                        pe.wait_ge(w_exp, n - 1)
                        pe.wait_ge(s_masked, n - 1)
                    s = B[4 + n % 2]
                    pe.matmul(s[:, :w], kt, q[:, kb * P:], start=True, stop=False)
                    m = pe.matmul(s[:, :w], tri, lr[:, kb, :w], start=False, stop=kb == TT - 1)
                    for nb in range(kb + 1, TT):
                        m = pe.matmul(s[:, (nb - kb) * P:w], ones, lr[:, nb, :T - nb * P], start=False, stop=nb == TT - 1)
                    m.then_inc(s_done, 1)
                    pe.wait_ge(w_exp, n + 1)
                    o = B[6 + h // 2]
                    v = v1[:, kb, HD * h:HD * h + HD]
                    pe.matmul(o[rows, kb * P:], v, wz[:, n % 2, :w], start=kb == TT - 1, stop=kb == 0,
                              skip_group_check=True).then_inc(sb_out, 1)
                    n += 1
            group_roots_before[0] = n_rt
            pe.wait_ge(y_sb, 2)
            pe.wait_ge(w_exp, n)
            group_sums(n_sq)
            n_sq += KD
            n_rt += KD
            pe.wait_ge(in_ready, 2)
            attention(stage1)
            group_roots_before[0] = n_rt
            group_sums(n_sq)
            n_sq += KD
            n_rt += KD
            pe.wait_ge(in_ready, 3)
            linear(S_OUT, T_OUT, N_OUT)
            pe.wait_ge(roots, n_rt)
            sum_squares(n_sq, B[4][:, :], ones)
            n_sq += KD
            n_rt += 1
            pe.wait_ge(in_ready, 4)
            linear(S_GU, T_GU, N_GU)
            pe.wait_ge(evac, T_DOWN)
            with pe.Fori(0, 2) as i:
                for m in range(RING):
                    pe.wait_ge(evac, i * RING + (T_DOWN + m - RING + 1))
                    for k in range(KF):
                        s, r = k // KD, (3 * m + k // KD) % RING
                        if k % KD == 0:
                            pe.wait_ge(lo_done, i * 12 + (S_DOWN + 3 * m + s + 1))
                        c = slice(k % KD * P, (k % KD + 1) * P)
                        mm = mm3(B[m][:, :], hi[:, r, c], lo[:, r, c], actH[:, k, :], actL[:, k, :], k == 0, k == KF - 1)
                        if k % KD == KD - 1 or k == KF - 1:
                            mm.then_inc(slot_used, 1)
            sum_squares(n_sq, B[4][:, :], ones)
            n_sq += KD
            n_rt += 1
            pe.wait_ge(in_ready, 5)
            linear(S_IN2, T_IN2, 40)
            for m in range(40, N_IN2):
                pe.wait_ge(evac, T_IN2 + m - RING + 1)
                pe.wait_ge(lo_done, S_IN2 + m + 1)
                (tile if m < 42 else tile_by_token)(m % RING, B[m % RING][:, :])
            for k in range(KD):
                pe.wait_ge(conv_done, k + 1)
                pe.matmul(B[4][:, :], ones, c2[:, k, :], start=k == 0, stop=k == KD - 1).then_inc(mean_done, 1)
            sum_squares(n_sq, B[5][:, :], ones)
            n_sq += KD
            n_rt += 1
            pe.wait_ge(in_ready, 6)
            linear(S_PW, T_PW, KD)
            pe.wait_ge(evac, T_WO)
            attention(stage2)
            pe.wait_ge(in_ready, 7)
            linear(S_WO, T_WO, KD)
            pe.wait_ge(in_ready, 8)
            linear(S_WO2, T_WO2, KD)
            sum_squares(n_sq, B[4][:, :], ones)
            n_sq += KD
            n_rt += 1
            pe.wait_ge(in_ready, 9)
            linear(S_Q, T_Q, N_Q)
            pe.wait_ge(peer_in, 48)
            pe.wait_ge(evac, T_Q + N_Q)
            for t in range(TT):
                for b in range(4):
                    if t:
                        pe.wait_ge(sc_copied, 4 * (t - 1) + b + 1)
                    for g in range(4):
                        m = pe.matmul(B[4 + b][:, g * P:(g + 1) * P], qp[:, 4 * b + g, t * P:(t + 1) * P],
                                      key_sb[:, g % 2, :], start=True, stop=True)
                    m.then_inc(sc_done, 1)
                pe.wait_ge(sel_ready, t + 1)
                if t:
                    pe.wait_ge(selT_copied, t)
                for j in range(3):
                    m = pe.transpose(B[0][:, j * P:(j + 1) * P], sel[:, j, :], ident)
                m.then_inc(selT_done, 1)

            def build(r, n_oh, n_built):
                pe.wait_ge(oh_ready, n_oh)
                for half in (0, 1):
                    pe.wait_ge(g_evac, n_built + half - 1)
                    for t in range(8):
                        tok = half * 8 + t
                        m = pe.matmul(B[2 + half][:, t * 3 * GRP:(t + 1) * 3 * GRP], oh2[:, r, :, tok],
                                      ohg[:, r, :, :, tok], start=True, stop=True)
                    m.then_inc(g_built, 1)

            pe.wait_ge(selT_copied, TT)
            pe.wait_ge(oh_ready, 1)
            for half in (0, 1):
                for t in range(8):
                    tok = half * 8 + t
                    m = pe.matmul(B[2 + half][:, t * 3 * GRP:(t + 1) * 3 * GRP], oh2[:, 0, :, tok],
                                  ohg[:, 0, :, :, tok], start=True, stop=True)
                m.then_inc(g_built, 1)
            build(1, 2, 2)
            with pe.Fori(1, NB // 2) as i:
                for r in (0, 1):
                    build(r, i * 2 + (r + 1), i * 4 + 2 * r)

            def a_tile(e, r, n, j):
                pe.wait_ge(lo_done, n)
                if j is not None:
                    pe.wait_ge(w_done, j * 2 + (e - 1))
                tile(r, B[e][:, :], u_done)

            def y_tiles(k0, k1, wpar, j, r0):
                if k0 == 0:
                    pe.wait_ge(lo_done, j * 4 + (S_PEER + 6))
                    pe.wait_ge(w_done, j * 2 + 2)
                for k in range(k0, k1):
                    pe.wait_ge(y_added, j * KD + (k - 3)) if not (isinstance(j, int) and j * KD + k - 3 <= 0) else None
                    c = slice(k * P, (k + 1) * P)
                    for e in (0, 1):
                        m = mm3(B[4 + k % 4][:, :], hi[:, r0 + e, c], lo[:, r0 + e, c], WH[:, wpar, e, :], WL[:, wpar, e, :],
                                e == 0, e == 1)
                    m.then_inc(y_done, 1)

            def body(j, q, build_next, first=False, one=False):
                if first:
                    a_tile(0, 0, S_PEER + 1, None)
                else:
                    a_tile(0, 2, j * 4 + (S_PEER - 2 + 1), j)
                ob, gb = j * 4 + NB, j * 8 + 2 * NB
                if build_next:
                    build(0, ob + 1, gb)
                    build(1, ob + 2, gb + 2)
                if first:
                    a_tile(1, 1, S_PEER + 2, None)
                else:
                    a_tile(1, 3, j * 4 + (S_PEER - 2 + 2), j)
                if build_next:
                    build(0, ob + 3, gb + 4)
                if not first:
                    y_tiles(0, 4, 1 - q, j - 1, 0)
                if build_next:
                    build(1, ob + 4, gb + 6)
                if not first:
                    y_tiles(4, KD, 1 - q, j - 1, 0)

            body(0, 0, True, first=True)
            body(1, 1, True)
            with pe.Fori(1, (N_GRP - 1) * PAIRS // 2) as i:
                for q in (0, 1):
                    body(i * 2 + q, q, True)
            with pe.Fori((N_GRP - 1) * PAIRS // 2, NKEY // 4) as i:
                for q in (0, 1):
                    body(i * 2 + q, q, False)
            last = NKEY // 2 - 1
            pe.wait_ge(lo_done, N_SLOTS)
            pe.wait_ge(w_done, 2 * last + 2)
            for k in range(KD):
                pe.wait_ge(y_added, last * KD + k - 3)
                c = slice(k * P, (k + 1) * P)
                for e in (0, 1):
                    m = mm3(B[4 + k % 4][:, :], hi[:, 2 + e, c], lo[:, 2 + e, c], WH[:, 1, e, :], WL[:, 1, e, :], e == 0, e == 1)
                m.then_inc(y_done, 1)
            sum_squares(n_sq, B[2][:, :], ones)

        return None


def lay_out(i):
    f = lambda a: np.asarray(a)

    def blocks(w):
        k, m = w.shape[0] // P, w.shape[1] // P
        return w.reshape(k, P, m, P).transpose(2, 1, 0, 3)

    def slots(w):
        b = blocks(w)
        return b.reshape(b.shape[0], P, D)

    w_in = f(i["w_in"])[0]
    o = np.cumsum([0, 256, 256, 256, 512, 512, 512, 256, 256, 256])
    part = lambda n: w_in[:, o[n]:o[n + 1]]
    win = slots(np.concatenate([part(n) for n in (0, 1, 3, 4, 6, 7, 8, 2, 5)], 1))
    wg, wu = slots(f(i["w_gate"])[0]), slots(f(i["w_up"])[0])
    gu = np.stack([wg, wu], 1).reshape(N_GU, P, D)
    wd = np.zeros((KD, P, KF_PAD, P), np.float32)
    wd[:, :, :KF] = blocks(f(i["w_down"])[0])
    wd = wd.reshape(KD, P, 3, D).transpose(0, 2, 1, 3).reshape(N_DOWN, P, D)
    w2 = f(i["w_in_2"])[0]
    a, b = slots(w2[:, :D]), slots(w2[:, D:2 * D])
    ab = np.stack([a, b], 1).reshape(16, P, D)
    heads = [4 * (2 * (j // 4) + half) + j % 4 for j in range(8) for half in (0, 1)]
    q2 = w2[:, 2048:3072].reshape(D, N_HEADS, HD)[:, heads].reshape(D, D)
    k2, vv2, g2 = w2[:, 3072:3328], w2[:, 3328:3584], w2[:, 3584:5632]
    win2 = np.concatenate([ab, slots(q2), slots(k2), slots(g2), slots(vv2)])
    wo = f(i["attn_w_o_2"])[0].reshape(N_HEADS, HD, D)[heads].reshape(D, D)
    eu = f(i["peer_u_2"])[0].reshape(NKEY, NKEY, KD, P).transpose(0, 3, 2, 1).reshape(NKEY, P, D)
    ev = f(i["peer_v_2"])[0].reshape(NKEY, NKEY, D)
    stream = np.empty((N_SLOTS, P, D), np.float32)
    n = 0
    for w in (win, slots(f(i["w_out"])[0]), gu, wd, win2, slots(f(i["conv_w_pw_2"])[0]), slots(wo),
              slots(f(i["w_out_2"])[0]), slots(f(i["peer_w_query_2"])[0])):
        stream[n:n + len(w)] = w
        n += len(w)
    assert n == S_PEER
    stream[n:n + 2] = eu[0:2]
    rest = stream[n + 2:n + 2 + 4 * (NKEY // 2 - 1)].reshape(NKEY // 2 - 1, 4, P, D)
    rest[:, 0:2] = eu[2:].reshape(NKEY // 2 - 1, 2, P, D)
    rest[:, 2:4] = ev[:-2].reshape(NKEY // 2 - 1, 2, P, D)
    stream[-2:] = ev[-2:]

    gains = np.empty((P, N_GC), np.float32)

    def put(name, a):
        gains[:, GC[name]:GC[name] + a.shape[1]] = a

    feat = lambda a: f(a).reshape(-1, P).T
    put("attn", feat(i["attn_norm_w"]))
    put("out", feat(i["out_norm_w"]))
    put("ffn", feat(i["ffn_norm_w"]))
    put("norm1", feat(i["norm1_g_2"]))
    put("norm2", feat(i["norm2_g_2"]))
    put("final", feat(i["final_g_2"]))
    put("ln_g", feat(i["conv_ln_g_2"]))
    put("ln_b", feat(i["conv_ln_b_2"]))
    put("dw_b", feat(i["conv_dw_b_2"]))
    put("dw", f(i["conv_dw_w_2"])[0].reshape(CONV_TAPS, KD, P).transpose(2, 1, 0).reshape(P, KD * CONV_TAPS))
    put("conv", f(i["conv_w"])[0].reshape(3, 2, P).transpose(2, 1, 0).reshape(P, 6))
    put("qn", np.concatenate([f(i["q_norm_w"])[0]] * 2)[:, None])
    put("kn", np.concatenate([f(i["k_norm_w"])[0]] * 2)[:, None])
    put("sink", np.broadcast_to(f(i["attn_sink_2"])[0][None], (P, N_HEADS)))
    put("eps", np.full((P, 1), EPS, np.float32))

    rel = f(i["rel_bias"])[0][:, np.clip(T - 1 - np.arange(REL), -P, P) + P]
    rel = np.tile(rel, (1, P))

    keys = np.ascontiguousarray(f(i["peer_sub_keys_2"])[0].transpose(2, 0, 1))
    x = np.ascontiguousarray(f(i["x"])[0].reshape(T, KD, P).transpose(2, 1, 0))
    return dict(x=x, stream=stream, gains=gains, rel=np.ascontiguousarray(rel), keys=keys)


def constants():
    r = np.arange(P)
    c = np.zeros((P, N_CC), np.float32)
    c[:, CC["ident"]:CC["ident"] + P] = np.eye(P)
    c[:, CC["ones"]:CC["ones"] + P] = 1
    c[:, CC["blk"]:CC["blk"] + P] = (r[:, None] // HD == r[None] // HD)
    c[:, CC["tri"]:CC["tri"] + P] = r[:, None] >= r[None]
    c[:, CC["mask"]:CC["mask"] + P] = r[:, None] < r[None]
    c[:, CC["neg"]:CC["neg"] + P] = np.where(r[:, None] < r[None], 0, NEG)
    c[:, CC["iota"]:CC["iota"] + TOPK] = np.arange(TOPK)
    dist = np.abs(r[:, None] + P - np.arange(3 * P)[None]).astype(np.float32)
    slopes = np.exp2(-8.0 * np.arange(1, N_HEADS + 1, dtype=np.float32) / N_HEADS).astype(np.float32)
    order = [4 * (2 * (j // 4) + half) + j % 4 for j in range(8) for half in (0, 1)]
    gqa = np.where(dist <= P, -slopes[order, None, None] * dist, np.float32(NEG)).astype(np.float32)
    ohc = np.empty((P, NKEY + GRP, TB), np.float32)
    ohc[:, :NKEY] = np.arange(NKEY)[None, :, None]
    ohc[:, NKEY:] = np.arange(GRP)[None, :, None]
    ohc = (ohc.view(np.uint32) >> 16).astype(np.uint16)
    return dict(consts=c, gqa=gqa, ohc=ohc)


def kernel(**inputs):
    import concourse.bacc as _bacc
    from concourse.bass_utils import run_bass_kernel_spmd as _run

    arrays = {**lay_out(inputs), **constants()}
    nc = _bacc.Bacc("TRN2", target_bir_lowering=False, num_devices=1)
    args = {n: nc.dram_tensor(n, a.shape, mybir.dt.from_np(a.dtype), kind="ExternalInput").ap() for n, a in arrays.items()}
    out = nc.dram_tensor("out", (P, KD, T), F32, kind="ExternalOutput").ap()
    program(nc, out=out, **args)
    r = _run(nc, [arrays], core_ids=[0])
    got = r.results[0]["out"]
    return got.transpose(2, 1, 0).reshape(1, T, D)
```

```python
from contextlib import ExitStack

import numpy as np

import concourse.bass as bass
from concourse import mybir

F32 = mybir.dt.float32
F32R = mybir.dt.float32r
BF16 = mybir.dt.bfloat16
U32 = mybir.dt.uint32
U16 = mybir.dt.uint16
ALU = mybir.AluOpType
ACT = mybir.ActivationFunctionType
AX_X = mybir.AxisListType.X

P = 128
D = 1024
KD = D // P
T = 512
TT = T // P
HD = 64
EPS = 1e-6
QSCALE = HD ** -0.5
NEG = -1e30

H_SB, H_CH = 4, 8
FF = 2816
KF = FF // P
KF_PAD = 24
CONV_TAPS = 31
REL = T + P
CONV_PAD = 15
UW = T + 2 * CONV_PAD
N_HEADS = 16
PH, TOPK, NKEY = 8, 16, 128
RING = 4
AHEAD = 2

N_IN, N_OUT, N_GU, N_DOWN = 24, 8, 2 * KF, 3 * KD
N_IN2, N_Q = 44, 16
S_IN = 0
S_OUT = S_IN + N_IN
S_GU = S_OUT + N_OUT
S_DOWN = S_GU + N_GU
S_IN2 = S_DOWN + N_DOWN
S_PW = S_IN2 + N_IN2
S_WO = S_PW + KD
S_WO2 = S_WO + KD
S_Q = S_WO2 + KD
S_PEER = S_Q + N_Q
N_SLOTS = S_PEER + 2 * NKEY
T_IN = 0
T_OUT = T_IN + N_IN
T_GU = T_OUT + N_OUT
T_DOWN = T_GU + N_GU
T_IN2 = T_DOWN + KD
T_PW = T_IN2 + N_IN2
T_WO = T_PW + KD
T_WO2 = T_WO + KD
T_Q = T_WO2 + KD

GC = {}
_at = 0
for _name, _n in (("attn", KD), ("out", KD), ("ffn", KD), ("norm1", KD), ("norm2", KD), ("final", KD),
                  ("ln_g", KD), ("ln_b", KD), ("dw_b", KD), ("dw", KD * CONV_TAPS), ("conv", 6),
                  ("qn", 1), ("kn", 1), ("sink", N_HEADS), ("eps", 1)):
    GC[_name] = _at
    _at += _n
N_GC = _at

CC = {"ident": 0, "ones": 128, "blk": 256, "tri": 384, "mask": 512, "neg": 640, "iota": 768}
N_CC = 784
GRP = 16
PAIRS = GRP // 2
N_GRP = NKEY // GRP
TB = 16
SLICE = T // PAIRS
NB = T // TB
N_GRPS = D // HD


class Chain:

    def __init__(self, eng, sem):
        self.eng, self.sem, self.n, self.loops = eng, sem, 0, []

    def loop(self, i, lo, hi, per):
        self.loops.append((i, lo, hi, per, self.n))

    def end(self):
        _, lo, hi, per, n = self.loops.pop()
        assert self.n == n + per, (self.n - n, per)
        self.n = n + (hi - lo) * per

    def mark(self, ins):
        ins.then_inc(self.sem, 1)
        self.n += 1
        value = self.n
        for i, lo, _, per, _ in self.loops:
            value = i * per + (value - lo * per) if isinstance(value, int) else value + i * per + (-lo * per)
        return value

    def wait(self, value):
        self.eng.wait_ge(self.sem, value)

    def __call__(self, ins):
        self.wait(self.mark(ins))


def program(nc, x, stream, gains, consts, rel, gqa, keys, ohc, out):
    ctx = ExitStack()
    with ctx:
        at = [16512]

        def fixed(name, shape, dt=F32):
            size = int(np.prod(shape[1:])) * (2 if dt == BF16 else 4)
            t = nc.alloc_sbuf_tensor_at(name, shape, dt, offset=at[0])
            at[0] += -(-size // 32) * 32
            return t

        def sem(name):
            return ctx.enter_context(nc.semaphore(name))

        xT = fixed("xT", [P, KD, T])
        inH = fixed("inH", [P, KD, T], F32R)
        inL = fixed("inL", [P, KD, T], F32R)
        raw = fixed("raw", [P, RING, D])
        hi = fixed("hi", [P, RING, D], F32R)
        lo = fixed("lo", [P, RING, D], F32R)
        gn = fixed("gn", [P, N_GC])
        cs = fixed("cs", [P, N_CC])
        sq_at = at[0]
        sq = fixed("sq", [P, 2, T])
        rt = fixed("rt", [P, 2, T])
        res = fixed("res", [P, T])
        rr = fixed("rr", [P, TT * N_GRPS])
        arena = at[0]

        def phase():
            at[0] = arena

        phase()
        qk1 = fixed("qk1", [P, 12, T])
        cv1 = fixed("cv1", [P, 6, T])
        v1 = fixed("v1", [P, TT, 768])
        y1 = fixed("y1", [P, KD, T])
        tbl1 = fixed("tbl1", [P, 2, T])
        shared = at[0]
        lr = fixed("lr", [P, 2, TT, T])
        ez = fixed("ez", [P, 2, T])
        mz = fixed("mz", [P, 2, T])
        wz = fixed("wz", [P, 2, T])
        at[0] = shared
        pr1 = fixed("pr1", [P, 4, T])
        pT1 = fixed("pT1", [P, 2, T])
        sm1 = fixed("sm1", [P, 4, 8])
        phase()
        actH = fixed("actH", [P, KF, T], F32R)
        actL = fixed("actL", [P, KF, T], F32R)
        phase()
        u2 = fixed("u2", [P, KD, UW])
        qk2 = fixed("qk2", [P, 10, T])
        v2 = fixed("v2", [P, TT, 256])
        gate2 = fixed("gate2", [P, 16, T])
        c2_at = at[0]
        c2 = fixed("c2", [P, KD, T])
        at[0] = c2_at
        pr2 = fixed("pr2", [P, 4, 3 * P])
        pT2 = fixed("pT2", [P, 2, 3 * P])
        tbl2 = fixed("tbl2", [P, 2, 3 * P])
        sm2 = fixed("sm2", [P, 4, 8])
        m2 = u2
        phase()
        gpart = fixed("gpart", [P, 3, T], BF16)
        i1T = fixed("i1T", [P, T], BF16)
        i2T = fixed("i2T", [P, T], BF16)
        iota2 = fixed("iota2", [P, NKEY, TB], BF16)
        peer_at = at[0]
        qp = fixed("qp", [P, N_Q, T])
        key_sb = fixed("key_sb", [P, 2, NKEY])
        sc = fixed("sc", [P, N_Q, NKEY])
        scb = fixed("scb", [P, 2, NKEY])
        cand = fixed("cand", [P, PH, TOPK * TOPK])
        candb = fixed("candb", [P, TOPK * TOPK])
        eq = fixed("eq", [P, PH * TOPK, TOPK])
        vals = fixed("vals", [P, N_Q, TOPK])
        idx = fixed("idx", [P, N_Q, TOPK], U32)
        idxf = fixed("idxf", [P, N_Q, TOPK])
        top = fixed("top", [P, PH, TOPK])
        pos = fixed("pos", [P, PH, TOPK], U32)
        posb = fixed("posb", [P, 2, PH * TOPK], U32)
        posf = fixed("posf", [P, 2, PH * TOPK])
        sel = fixed("sel", [P, 3, PH * TOPK])
        den = fixed("den", [P, 2, PH])
        gT = fixed("gT", [P, T])
        at[0] = peer_at
        Gd = fixed("Gd", [P, 2, GRP, T])
        WH = fixed("WH", [P, 2, 2, T], F32R)
        WL = fixed("WL", [P, 2, 2, T], F32R)
        oh2 = fixed("oh2", [P, 2, NKEY, TB], BF16)
        assert at[0] <= 229344, at[0]
        at[0] = sq_at
        iota1 = fixed("iota1", [P, GRP, TB], BF16)
        oh1 = fixed("oh1", [P, 2, GRP, TB], BF16)
        ohg = fixed("ohg", [P, 2, 3, GRP, TB], BF16)
        assert at[0] <= sq_at + 4 * T * 4

        B = [ctx.enter_context(nc.psum_tensor(f"bank{i}", [P, T], F32)) for i in range(8)]

        loaded = [sem(f"loaded{r}") for r in range(RING)]
        hi_done = sem("hi_done")
        lo_done = sem("lo_done")
        slot_used = sem("slot_used")
        evac = sem("evac")
        small_in = sem("small_in")
        squares = sem("squares")
        sums = sem("sums")
        roots = sem("roots")
        recips = sem("recips")
        spread = sem("spread")
        spread_used = sem("spread_used")
        in_ready = sem("in_ready")
        dve_steps = sem("dve_steps")
        act_steps = sem("act_steps")
        z_done = sem("z_done")
        z_abs = sem("z_abs")
        z_soft = sem("z_soft")
        z_min = sem("z_min")
        lr_ready = sem("lr_ready")
        s_done = sem("s_done")
        s_masked = sem("s_masked")
        w_exp = sem("w_exp")
        w_ready = sem("w_ready")
        sb_out = sem("sb_out")
        att = [{n: sem(f"{n}{a}") for n in ("score", "logit", "maxed", "probs", "normed", "turned",
                                           "turned_sb", "mixed", "head_out", "tbl_free")} for a in (1, 2)]
        tbl_in = [[sem(f"tbl_in{a}{b}") for b in (0, 1)] for a in (1, 2)]
        y_sb = sem("y_sb")
        conv_done = sem("conv_done")
        mean_done = sem("mean_done")
        silu_ready = sem("silu_ready")
        peer_in = sem("peer_in")
        sc_done = sem("sc_done")
        sc_copied = sem("sc_copied")
        sc_used = sem("sc_used")
        top_ready = sem("top_ready")
        gexp = sem("gexp")
        sel_ready = sem("sel_ready")
        selT_done = sem("selT_done")
        selT_copied = sem("selT_copied")
        oh_ready = sem("oh_ready")
        g_built = sem("g_built")
        g_evac = sem("g_evac")
        gelu_done = sem("gelu_done")
        w_done = sem("w_done")
        y_done = sem("y_done")
        y_added = sem("y_added")
        out_done = sem("out_done")
        final_done = sem("final_done")
        u_done = sem("u_done")
        gate_act = sem("gate_act")
        sig_act = sem("sig_act")

        ident = cs[:, CC["ident"]:CC["ident"] + P]
        ones = cs[:, CC["ones"]:CC["ones"] + P]
        blk = cs[:, CC["blk"]:CC["blk"] + P]
        tri = cs[:, CC["tri"]:CC["tri"] + P]
        mask = cs[:, CC["mask"]:CC["mask"] + P]
        neg = cs[:, CC["neg"]:CC["neg"] + P]
        iota16 = cs[:, CC["iota"]:CC["iota"] + TOPK]

        def gain(name, k=0):
            return gn[:, GC[name] + k:GC[name] + k + 1]


        units1 = []
        for h in range(H_CH):
            for i in range(TT):
                units1.append(dict(q=4 + h // 2, k=8 + h // 2, row=HD * (h % 2), i=i, k0=0, n=(i + 1) * P,
                                   c0=(TT - 1 - i) * P, head=h, sink=None, v=256 + HD * h, pair=h // 2, dst=2 + h // 2))
        units2 = []
        for j in range(N_HEADS // 2):
            for half in (0, 1):
                kv = 2 * (j // 4) + half
                head = 4 * kv + j % 4
                for i in range(TT):
                    first, last = max(i - 1, 0), min(i + 1, TT - 1)
                    units2.append(dict(q=j, k=8 + kv // 2, row=HD * half, i=i, k0=first * P,
                                       n=(last - first + 1) * P, c0=(first - i + 1) * P, head=head,
                                       sink=head, v=HD * kv, pair=j, dst=j))
        stage1 = dict(units=units1, qk=qk1, v=v1, tbl=tbl1, pr=pr1, pT=pT1, sm=sm1, s=att[0], tbl_in=tbl_in[0],
                      dst=y1)
        stage2 = dict(units=units2, qk=qk2, v=v2, tbl=tbl2, pr=pr2, pT=pT2, sm=sm2, s=att[1], tbl_in=tbl_in[1],
                      dst=qk2)


        blocks = [(h, kb, T - kb * P) for h in range(H_SB) for kb in reversed(range(TT))]

        block = ctx.enter_context(nc.Block())

        @block.sync
        def _(sp):
            def load(n, r):
                sp.dma_start(raw[:, r, :], stream[bass.ds(n, 1)].rearrange("a p n -> (a p) n")).then_inc(loaded[r], 16)

            sp.dma_start(gn[:, :], gains).then_inc(small_in, 16)
            sp.dma_start(cs[:, :], consts).then_inc(small_in, 16)
            sp.dma_start(xT[:, :, :], x).then_inc(small_in, 16)
            for r in range(RING):
                load(r, r)
            with sp.Fori(1, N_SLOTS // RING) as i:
                for r in range(RING):
                    sp.wait_ge(lo_done, i * RING + (r - RING + 1))
                    load(i * RING + r, r)
            for n in range(N_SLOTS // RING * RING, N_SLOTS):
                sp.wait_ge(lo_done, n - RING + 1)
                load(n, n % RING)

        @block.gpsimd
        def _(pool):
            def low(n, r):
                pool.wait_ge(hi_done, n + 1)
                pool.tensor_tensor(lo[:, r, :], raw[:, r, :], hi[:, r, :].bitcast(F32), ALU.subtract).then_inc(lo_done, 1)

            with pool.Fori(0, N_SLOTS // RING) as i:
                for r in range(RING):
                    low(i * RING + r, r)
            for n in range(N_SLOTS // RING * RING, N_SLOTS):
                low(n, n % RING)

        @block.scalar
        def _(act):
            chain = Chain(act, act_steps)

            def high(n0, i, r, first=False):
                n = i * RING + (n0 + r)
                act.wait_ge(loaded[r % RING], i * 16 + 16 * ((n0 + r) // RING + 1))
                if not first:
                    act.wait_ge(slot_used, n - RING + 1)
                act.activation(hi[:, r % RING, :], raw[:, r % RING, :], ACT.Copy).then_inc(hi_done, 1)

            def highs(s0, n, epilogue=None):
                with act.Fori(0, n // RING) as i:
                    for r in range(RING):
                        high(s0, i, r + AHEAD)
                        if epilogue:
                            epilogue(i, r)

            def root_of(width, scale, n_sums):
                act.wait_ge(sums, n_sums)
                act.activation(rr[:, :width], B[4][:, :width], ACT.Sqrt, bias=gain("eps"), scale=scale).then_inc(roots, 1)

            def table(st, head):
                src = (bass.AP(tensor=rel.tensor, offset=head * P * REL + P - 1, ap=[[REL - 1, P], [1, T]]) if st is stage1
                       else gqa[head])
                act.dma_start(st["tbl"][:, head % 2, :], src).then_inc(st["tbl_in"][head % 2], 16)

            def attention(st):
                s, units = st["s"], st["units"]
                n = len(units)
                for u in range(n + 4):
                    if 0 < u < n and u % TT == 0 and u // TT + 1 < n // TT:
                        act.wait_ge(s["maxed"], u)
                        table(st, u // TT + 1)
                    if u < n:
                        w = units[u]
                        pr, sm = st["pr"][:, u % 4, :w["n"]], st["sm"][:, u % 4, :]
                        act.wait_ge(s["maxed"], u + 1)
                        e = act.activation(pr, pr, ACT.Exp, bias=sm[:, 1:2], accum_out=sm[:, 2:3])
                        if w["sink"] is None:
                            e.then_inc(s["probs"], 1)
                        else:
                            act.activation(sm[:, 3:4], gain("sink", w["sink"]), ACT.Exp, bias=sm[:, 1:2]).then_inc(s["probs"], 1)
                    v = u - 2
                    if 0 <= v < n:
                        w = units[v]
                        act.wait_ge(s["turned"], v + 1)
                        if v >= 2:
                            act.wait_ge(s["mixed"], v - 1)
                        act.activation(st["pT"][:, v % 2, :w["n"]], B[6 + v % 2][:, :w["n"]], ACT.Copy).then_inc(s["turned_sb"], 1)
                    v = u - 4
                    if v >= 0 and (v == n - 1 or units[v + 1]["pair"] != units[v]["pair"]):
                        pair = units[v]["pair"]
                        act.wait_ge(s["mixed"], v + 1)
                        act.activation(st["dst"][:, units[v]["dst"], :], B[2 + pair % 2][:, :], ACT.Copy).then_inc(s["head_out"], 1)

            table(stage1, 0)
            table(stage1, 1)
            act.wait_ge(small_in, 48)
            for n in range(AHEAD):
                high(0, 0, n, first=True)
            root_of(TT, 1.0 / D, KD)
            n_sums = KD
            for r in range(RING):
                high(S_IN, 0, r + AHEAD, first=r + AHEAD < RING)
            with act.Fori(1, N_IN // RING) as i:
                for r in range(RING):
                    high(S_IN, i, r + AHEAD)
            act.preload_act_table_set("natural_log_exp_and_others")
            for n in range(-1, len(blocks)):
                if n + 1 < len(blocks):
                    m = n + 1
                    w = blocks[m][2]
                    act.wait_ge(z_done, m + 1)
                    if m >= 2:
                        act.wait_ge(lr_ready, m - 1)
                    act.activation(ez[:, m % 2, :w], B[2 + m % 2][:, :w], ACT.Abs).then_inc(z_abs, 1)
                    act.wait_ge(z_abs, m + 1)
                    chain(act.activation(ez[:, m % 2, :w], ez[:, m % 2, :w], ACT.Exp, scale=-1.0))
                    act.activation(ez[:, m % 2, :w], ez[:, m % 2, :w], ACT.Ln, bias=1.0).then_inc(z_soft, 1)
                if n < 0:
                    continue
                h, kb, w = blocks[n]
                act.wait_ge(s_masked, n + 1)
                if n >= 2:
                    act.wait_ge(sb_out, n - 1)
                e = act.activation(wz[:, n % 2, :P], mz[:, n % 2, :P], ACT.Exp)
                if w > P:
                    e = act.activation(wz[:, n % 2, P:w], B[4 + n % 2][:, P:w], ACT.Exp)
                e.then_inc(w_exp, 1)
                if h % 2 and kb == TT - 1 and h > 1 or n == len(blocks) - 1:
                    pair = H_SB // 2 - 1 if n == len(blocks) - 1 else h // 2 - 1
                    act.wait_ge(sb_out, len(blocks) if n == len(blocks) - 1 else (pair + 1) * 2 * TT)
                    act.activation(y1[:, pair, :], B[6 + pair][:, :], ACT.Copy).then_inc(y_sb, 1)
            root_of(TT * N_GRPS, 1.0 / HD, n_sums + KD)
            n_sums += KD
            attention(stage1)
            root_of(TT * N_GRPS, 1.0 / HD, n_sums + KD)
            n_sums += KD
            highs(S_OUT, N_OUT)
            root_of(TT, 1.0 / D, n_sums + KD)
            n_sums += KD

            def silu(i, r):
                if r % 2 == 0:
                    act.wait_ge(evac, i * RING + (T_GU + r - 2))
                    act.wait_ge(slot_used, i * RING + (S_GU + r + 1))
                    act.activation(sq[:, r // 2, :], B[r][:, :], ACT.Silu).then_inc(gate_act, 1)

            highs(S_GU, N_GU, silu)
            highs(S_DOWN, N_DOWN)
            root_of(TT, 1.0 / D, n_sums + KD)
            n_sums += KD

            def sigm(i, r):
                if r % 2 == 1:
                    act.wait_ge(evac, i * RING + (T_IN2 + r - 3))
                    act.wait_ge(slot_used, i * RING + (S_IN2 + r + 1))
                    act.activation(sq[:, r // 2, :], B[r][:, :], ACT.Sigmoid).then_inc(sig_act, 1)

            highs(S_IN2, 16, sigm)
            act.wait_ge(evac, T_IN2 + 16)
            for m in range(16, N_IN2):
                high(S_IN2, 0, m + AHEAD)
                act.wait_ge(slot_used, S_IN2 + m + 1)
                bank = B[m % RING]
                if m < 26:
                    e = act.activation(qk2[:, m - 16, :], bank[:, :], ACT.Copy, scale=QSCALE if m < 24 else 1.0)
                elif m < 42:
                    e = act.activation(gate2[:, m - 26, :], bank[:, :], ACT.Sigmoid)
                else:
                    e = act.activation(v2[:, :, (m - 42) * P:(m - 41) * P], bank[:, :].rearrange("p (t c) -> p t c", t=TT), ACT.Copy)
                e.then_inc(evac, 1)
            root_of(TT, 1.0 / D, n_sums + KD)
            n_sums += KD
            for k in range(KD):
                act.wait_ge(conv_done, KD + k + 1)
                act.activation(sq[:, k % 2, :], c2[:, k, :], ACT.Silu).then_inc(silu_ready, 1)
            highs(S_PW, KD)
            act.wait_ge(in_ready, 6)
            table(stage2, 0)
            table(stage2, 1)
            attention(stage2)
            highs(S_WO, KD)
            highs(S_WO2, KD)
            root_of(TT, 1.0 / D, n_sums + KD)
            n_sums += KD
            act.wait_ge(in_ready, 9)
            act.dma_start(iota2[:, :, :].bitcast(U16), ohc[:, 0:NKEY, :]).then_inc(peer_in, 16)
            act.dma_start(iota1[:, :, :].bitcast(U16), ohc[:, NKEY:NKEY + GRP, :]).then_inc(peer_in, 16)
            act.dma_start(key_sb[:, :, :], keys).then_inc(peer_in, 16)
            for m in range(N_Q):
                high(S_Q, 0, m + AHEAD)
                act.wait_ge(evac, T_Q + m)
                act.wait_ge(slot_used, S_Q + m + 1)
                act.activation(qp[:, m, :], B[m % RING][:, :], ACT.Copy).then_inc(evac, 1)
            for t in range(TT):
                if t:
                    act.wait_ge(sc_used, t)
                for b in range(4):
                    act.wait_ge(sc_done, 4 * t + b + 1)
                    act.activation(sc[:, 4 * b:4 * b + 4, :], B[4 + b][:, :], ACT.Copy).then_inc(sc_copied, 1)
                act.wait_ge(top_ready, t + 1)
                act.activation(sel[:, 0, :], sel[:, 0, :], ACT.Exp).then_inc(gexp, 1)
                act.wait_ge(selT_done, t + 1)
                act.activation(gT[:, t * P:(t + 1) * P], B[0][:, 0:P], ACT.Copy)
                act.activation(i1T[:, t * P:(t + 1) * P], B[0][:, P:2 * P], ACT.Copy)
                act.activation(i2T[:, t * P:(t + 1) * P], B[0][:, 2 * P:3 * P], ACT.Copy).then_inc(selT_copied, 1)

            def gelu(e, done):
                act.wait_ge(u_done, done)
                act.activation(B[e][:, :], B[e][:, :], ACT.Gelu).then_inc(gelu_done, 1)

            def high_peer(i, r, n_loads):
                act.wait_ge(loaded[r], i * 16 + n_loads * 16)
                act.wait_ge(small_in, 48)
                act.activation(hi[:, r, :], raw[:, r, :], ACT.Copy).then_inc(hi_done, 1)

            for e in (0, 1):
                high(S_PEER, 0, e + AHEAD)
                gelu(e, e + 1)
            def pair(j):
                for e in (0, 1):
                    act.wait_ge(*((u_done, 2) if isinstance(j, int) else (y_done, j * KD + (-KD))))
                    high_peer(j, e, S_PEER // RING + 1)
                    gelu(e, j * 2 + (e + 1))
                for e in (0, 1):
                    act.wait_ge(u_done, j * 2 + (e + 1))
                    high_peer(j, e + 2, S_PEER // RING + 1)

            pair(1)
            with act.Fori(2, NKEY // 2) as j:
                pair(j)
            root_of(TT, 1.0 / D, n_sums + KD)
            for k in range(KD):
                act.wait_ge(final_done, k + 1)
                act.dma_start(out[:, k, :], xT[:, k, :]).then_inc(out_done, 16)
            act.wait_ge(out_done, 16 * KD)

        @block.vector
        def _(dve):
            chain = Chain(dve, dve_steps)

            def split(src, h, l):
                chain(dve.tensor_scalar(h, src, 1.0, None, ALU.mult))
                chain(dve.tensor_tensor(l, src, h.bitcast(F32), ALU.subtract))

            def square_sums(src, n):
                for k in range(KD):
                    if k >= 2:
                        dve.wait_ge(sums, n + k - 1)
                    dve.tensor_tensor(sq[:, k % 2, :], src(k), src(k), ALU.mult).then_inc(squares, 1)

            def norm(src, gname, n, nth_root, n_spread):
                square_sums(src, n)
                over_root(TT, nth_root)
                dve.wait_ge(spread, n_spread + 1)
                for k in range(KD):
                    chain(dve.scalar_tensor_tensor(res[:, :], src(k), gain(gname, k), B[5][:, :], ALU.mult, ALU.mult))
                    split(res[:, :], inH[:, k, :], inL[:, k, :])

            def over_root(width, nth_root):
                dve.wait_ge(roots, nth_root)
                dve.reciprocal(rr[:, :width], rr[:, :width]).then_inc(recips, 1)

            def group_norm(src, put, n, nth_root, n_spread):
                square_sums(src, n)
                over_root(TT * N_GRPS, nth_root)
                for k in range(KD):
                    dve.wait_ge(spread, n_spread + k + 1)
                    put(k, B[5 + k % 2][:, :])

            def take(n, ins):
                ins.then_inc(evac, 1)

            def attention(st):
                s, units = st["s"], st["units"]
                n = len(units)
                for u in range(n + 1):
                    if u < n:
                        w = units[u]
                        pr, sm = st["pr"][:, u % 4, :w["n"]], st["sm"][:, u % 4, :]
                        hn = u // TT
                        if u % TT == 0:
                            dve.wait_ge(st["tbl_in"][hn % 2], 16 * (hn // 2 + 1))
                            if st is stage1:
                                chain(dve.memset(tbl1[0:HD, hn % 2, T - HD:T], NEG))
                        dve.wait_ge(s["score"], u + 1)
                        if u >= 4:
                            dve.wait_ge(s["turned"], u - 3)
                        dve.tensor_tensor_reduce(out=pr, in0=B[4 + u % 2][:, :w["n"]],
                                                 in1=st["tbl"][:, hn % 2, w["c0"]:w["c0"] + w["n"]], scale=1.0, scalar=-3.0e38,
                                                 op0=ALU.add, op1=ALU.max, accum_out=sm[:, 0:1]).then_inc(s["logit"], 1)
                        dve.wait_ge(s["logit"], u + 1)
                        if w["sink"] is None:
                            dve.tensor_scalar(sm[:, 1:2], sm[:, 0:1], -1.0, None, ALU.mult).then_inc(s["maxed"], 1)
                        else:
                            dve.tensor_scalar(sm[:, 1:2], sm[:, 0:1], gain("sink", w["sink"]), -1.0, ALU.max, ALU.mult).then_inc(s["maxed"], 1)
                    if u >= 1:
                        v = u - 1
                        w = units[v]
                        sm = st["sm"][:, v % 4, :]
                        pr = st["pr"][:, v % 4, :w["n"]]
                        dve.wait_ge(s["probs"], v + 1)
                        if w["sink"] is not None:
                            chain(dve.tensor_tensor(sm[:, 2:3], sm[:, 2:3], sm[:, 3:4], ALU.add))
                        chain(dve.reciprocal(sm[:, 4:5], sm[:, 2:3]))
                        dve.tensor_scalar(pr, pr, sm[:, 4:5], None, ALU.mult).then_inc(s["normed"], 1)


            x_of = lambda k: xT[:, k, :]
            dve.wait_ge(small_in, 48)
            n_sums, n_root, n_spread = 0, 0, 0
            norm(x_of, "attn", n_sums, n_root + 1, n_spread)
            n_spread += 1
            dve.sem_inc(in_ready, 1)
            n_sums += KD
            n_root += 1
            for m in range(N_IN):
                dve.wait_ge(slot_used, S_IN + m + 1)
                bank = B[m % RING]
                if m < 12:
                    take(m, dve.tensor_scalar(qk1[:, m, :], bank[:, :], QSCALE if m < 2 else 1.0, None, ALU.mult))
                elif m < 18:
                    take(m, dve.tensor_copy(cv1[:, m - 12, :], bank[:, :]))
                else:
                    take(m, dve.tensor_copy(v1[:, :, (m - 18) * P:(m - 17) * P], bank[:, :].rearrange("p (t c) -> p t c", t=TT)))
            dve.wait_ge(evac, T_OUT)
            for n in range(-1, len(blocks)):
                if n + 1 < len(blocks):
                    m = n + 1
                    h, kb, w = blocks[m]
                    l = lr[:, h % 2, kb, :]
                    dve.wait_ge(z_abs, m + 1)
                    chain(dve.tensor_scalar(l[:, :w], B[2 + m % 2][:, :w], -1.0, 0.0, ALU.mult, ALU.min))
                    dve.wait_ge(z_soft, m + 1)
                    chain(dve.tensor_tensor(l[:, :w], l[:, :w], ez[:, m % 2, :w], ALU.subtract))
                    dve.tensor_tensor(l[:, :P], l[:, :P], mask, ALU.mult).then_inc(lr_ready, 1)
                if n >= 0:
                    dve.wait_ge(s_done, n + 1)
                    if n >= 2:
                        dve.wait_ge(w_exp, n - 1)
                    dve.tensor_tensor(mz[:, n % 2, :P], B[4 + n % 2][:, :P], neg, ALU.add).then_inc(s_masked, 1)
            for m in range(2):
                gb, gc, xc = cv1[:, m, :], cv1[:, 2 + m, :], cv1[:, 4 + m, :]
                tap = [gain("conv", 3 * m + j) for j in range(3)]
                chain(dve.tensor_tensor(gc, gc, xc, ALU.mult))
                chain(dve.tensor_scalar(xc, gc, tap[2], None, ALU.mult))
                chain(dve.scalar_tensor_tensor(xc[:, 1:], gc[:, :T - 1], tap[1], xc[:, 1:], ALU.mult, ALU.add))
                chain(dve.scalar_tensor_tensor(xc[:, 2:], gc[:, :T - 2], tap[0], xc[:, 2:], ALU.mult, ALU.add))
                chain(dve.tensor_tensor(y1[:, 6 + m, :], xc, gb, ALU.mult))
            chain(dve.tensor_scalar(gain("qn"), gain("qn"), QSCALE, None, ALU.mult))

            def put_qk(k, r):
                t = qk1[:, 4 + k, :]
                dve.scalar_tensor_tensor(t, t, gain("qn" if k < 4 else "kn"), r, ALU.mult, ALU.mult).then_inc(spread_used, 1)
            group_norm(lambda k: qk1[:, 4 + k, :], put_qk, n_sums, n_root + 1, n_spread)
            n_spread += KD
            dve.wait_ge(spread_used, KD)
            dve.sem_inc(in_ready, 1)
            n_sums += KD
            n_root += 1
            attention(stage1)
            dve.wait_ge(att[0]["head_out"], 4)

            def put_y(k, r):
                dve.scalar_tensor_tensor(res[:, :], y1[:, k, :], gain("out", k), r, ALU.mult, ALU.mult).then_inc(spread_used, 1)
                dve.wait_ge(spread_used, KD + k + 1)
                split(res[:, :], inH[:, k, :], inL[:, k, :])
            dve.wait_ge(y_sb, 2)
            group_norm(lambda k: y1[:, k, :], put_y, n_sums, n_root + 1, n_spread)
            n_spread += KD
            dve.sem_inc(in_ready, 1)
            n_sums += KD
            n_root += 1

            def add_x(s_last, k):
                dve.wait_ge(slot_used, s_last)
                take(None, dve.tensor_tensor(xT[:, k, :], xT[:, k, :], B[k % RING][:, :], ALU.add))

            for k in range(KD):
                add_x(S_OUT + k + 1, k)
            dve.wait_ge(evac, T_GU)
            norm(x_of, "ffn", n_sums, n_root + 1, n_spread)
            n_spread += 1
            dve.sem_inc(in_ready, 1)
            n_sums += KD
            n_root += 1
            with dve.Fori(0, N_GU // RING) as i:
                chain.loop(i, 0, N_GU // RING, 4)
                for r in (0, 1):
                    dve.wait_ge(gate_act, i * 2 + (r + 1))
                    dve.wait_ge(slot_used, i * RING + (S_GU + 2 * r + 2))
                    chain(dve.tensor_tensor(rt[:, r, :], sq[:, r, :], B[2 * r + 1][:, :], ALU.mult))
                    h, l = actH[:, bass.ds(i * 2 + r, 1), :], actL[:, bass.ds(i * 2 + r, 1), :]
                    src = rt[:, r:r + 1, :]
                    chain(dve.tensor_scalar(h, src, 1.0, None, ALU.mult))
                    dve.tensor_tensor(l, src, h.bitcast(F32), ALU.subtract).then_inc(evac, 2)
                chain.end()
            for k in range(KD):
                add_x(S_DOWN + 3 * (k + 1), k)
            dve.wait_ge(evac, T_IN2)
            norm(x_of, "norm1", n_sums, n_root + 1, n_spread)
            n_spread += 1
            chain(dve.memset(u2[:, :, 0:CONV_PAD], 0.0))
            chain(dve.memset(u2[:, :, CONV_PAD + T:UW], 0.0))
            dve.sem_inc(in_ready, 1)
            n_sums += KD
            n_root += 1
            def taps(k):
                t = c2[:, k, :]
                chain(dve.tensor_scalar(t, u2[:, k, 0:T], gain("dw", k * CONV_TAPS), gain("dw_b", k), ALU.mult, ALU.add))
                for j in range(1, CONV_TAPS):
                    ins = dve.scalar_tensor_tensor(t, u2[:, k, j:j + T], gain("dw", k * CONV_TAPS + j), t, ALU.mult, ALU.add)
                    if j < CONV_TAPS - 1:
                        chain(ins)
                    else:
                        ins.then_inc(conv_done, 1)
            for k in range(KD):
                dve.wait_ge(sig_act, k + 1)
                dve.wait_ge(slot_used, S_IN2 + 2 * k + 2)
                dve.tensor_tensor(u2[:, k, CONV_PAD:CONV_PAD + T], B[2 * k % RING][:, :], sq[:, k % 2, :], ALU.mult).then_inc(evac, 2)
            dve.wait_ge(evac, T_IN2 + 16)
            for k in range(KD):
                taps(k)
            dve.wait_ge(mean_done, KD)
            dve.wait_ge(conv_done, KD)
            chain(dve.tensor_scalar(rt[:, 1, :], B[4][:, :], 1.0 / D, None, ALU.mult))
            for k in range(KD):
                chain(dve.tensor_tensor(c2[:, k, :], c2[:, k, :], rt[:, 1, :], ALU.subtract))
            square_sums(lambda k: c2[:, k, :], n_sums)
            over_root(TT, n_root + 1)
            dve.wait_ge(spread, n_spread + 1)
            n_sums += KD
            n_root += 1
            n_spread += 1
            for k in range(KD):
                t = c2[:, k, :]
                chain(dve.scalar_tensor_tensor(t, t, gain("ln_g", k), B[5][:, :], ALU.mult, ALU.mult))
                dve.tensor_scalar(t, t, gain("ln_b", k), None, ALU.add).then_inc(conv_done, 1)
                if k >= 1:
                    dve.wait_ge(silu_ready, k)
                    split(sq[:, (k - 1) % 2, :], inH[:, k - 1, :], inL[:, k - 1, :])
            dve.wait_ge(silu_ready, KD)
            split(sq[:, (KD - 1) % 2, :], inH[:, KD - 1, :], inL[:, KD - 1, :])
            dve.sem_inc(in_ready, 1)
            for k in range(KD):
                dve.wait_ge(slot_used, S_PW + k + 1)
                take(None, dve.tensor_tensor(m2[:, k, :T], gate2[:, k, :], B[k % RING][:, :], ALU.mult))
            attention(stage2)
            dve.wait_ge(att[1]["head_out"], 8)
            for k in range(KD):
                split(qk2[:, k, :], inH[:, k, :], inL[:, k, :])
            dve.sem_inc(in_ready, 1)
            for k in range(KD):
                dve.wait_ge(slot_used, S_WO + k + 1)
                dve.tensor_tensor(sq[:, k % 2, :], gate2[:, KD + k, :], B[k % RING][:, :], ALU.mult).then_inc(evac, 1)
                dve.wait_ge(evac, T_WO + k + 1)
                chain(dve.tensor_tensor(m2[:, k, :T], m2[:, k, :T], sq[:, k % 2, :], ALU.add))
            for k in range(KD):
                split(m2[:, k, :T], inH[:, k, :], inL[:, k, :])
            dve.sem_inc(in_ready, 1)
            for k in range(KD):
                add_x(S_WO2 + k + 1, k)
            dve.wait_ge(evac, T_Q)
            norm(x_of, "norm2", n_sums, n_root + 1, n_spread)
            n_spread += 1
            n_sums += KD
            n_root += 1
            dve.sem_inc(in_ready, 1)
            dve.wait_ge(peer_in, 48)
            for t in range(TT):
                dve.wait_ge(sc_copied, 4 * t + 4)
                for g in range(N_Q):
                    s, b = sc[:, g, :], scb[:, g % 2, :]
                    chain(dve.max(out=vals[:, g, 0:8], in_=s))
                    dve.max_index(out=idx[:, g, 0:8], in_max=vals[:, g, 0:8], in_values=s)
                    chain(dve.match_replace(out=b, in_to_replace=vals[:, g, 0:8], in_values=s, imm_value=-3.0e38))
                    chain(dve.max(out=vals[:, g, 8:16], in_=b))
                    dve.max_index(out=idx[:, g, 8:16], in_max=vals[:, g, 8:16], in_values=b)
                dve.sem_inc(sc_used, 1)
                v4 = vals[:, :, :].rearrange("p (h s) k -> p h s k", s=2)
                for h in range(PH):
                    c = cand[:, h, :]
                    chain(dve.tensor_tensor(c.rearrange("p (a b) -> p a b", a=TOPK),
                                            v4[:, h, 0, :].unsqueeze(2).broadcast_to([P, TOPK, TOPK]),
                                            v4[:, h, 1, :].unsqueeze(1).broadcast_to([P, TOPK, TOPK]), ALU.add))
                    chain(dve.max(out=top[:, h, 0:8], in_=c))
                    dve.max_index(out=pos[:, h, 0:8], in_max=top[:, h, 0:8], in_values=c)
                    chain(dve.match_replace(out=candb[:, :], in_to_replace=top[:, h, 0:8], in_values=c, imm_value=-3.0e38))
                    chain(dve.max(out=top[:, h, 8:16], in_=candb[:, :]))
                    chain(dve.max_index(out=pos[:, h, 8:16], in_max=top[:, h, 8:16], in_values=candb[:, :]))
                if t:
                    dve.wait_ge(selT_copied, t)
                s0 = sel[:, 0, :].rearrange("p (h k) -> p h k", h=PH)
                dve.tensor_tensor(s0, top[:, :, :], top[:, :, 0:1].broadcast_to([P, PH, TOPK]), ALU.subtract).then_inc(top_ready, 1)
                pf = pos[:, :, :].rearrange("p h k -> p (h k)")
                chain(dve.tensor_scalar(posb[:, 0, :], pf, 4, None, ALU.logical_shift_right))
                chain(dve.tensor_scalar(posb[:, 1, :], pf, 15, None, ALU.bitwise_and))
                chain(dve.tensor_copy(posf[:, :, :], posb[:, :, :]))
                chain(dve.tensor_copy(idxf[:, :, :], idx[:, :, :]))
                i4 = idxf[:, :, :].rearrange("p (h s) k -> p h s k", s=2)
                for s in (0, 1):
                    chain(dve.tensor_tensor(eq[:, :, :], posf[:, s, :].unsqueeze(2).broadcast_to([P, PH * TOPK, TOPK]),
                                            iota16.unsqueeze(1).broadcast_to([P, PH * TOPK, TOPK]), ALU.is_equal))
                    e4 = eq[:, :, :].rearrange("p (h k) a -> p h k a", h=PH)
                    chain(dve.tensor_tensor(e4, e4, i4[:, :, s, :].unsqueeze(2).broadcast_to([P, PH, TOPK, TOPK]), ALU.mult))
                    chain(dve.tensor_reduce(sel[:, 1 + s, :], eq[:, :, :], axis=AX_X, op=ALU.add))
                dve.wait_ge(gexp, t + 1)
                chain(dve.tensor_reduce(den[:, 0, :], s0, axis=AX_X, op=ALU.add))
                chain(dve.reciprocal(den[:, 1, :], den[:, 0, :]))
                dve.tensor_tensor(s0, s0, den[:, 1, :].unsqueeze(2).broadcast_to([P, PH, TOPK]), ALU.mult).then_inc(sel_ready, 1)
            dve.wait_ge(selT_copied, TT)
            chain(dve.tensor_copy(gpart[:, 0, :], gT[:, :]))
            chain(dve.tensor_tensor(gT[:, :], gT[:, :], gpart[:, 0, :], ALU.subtract))
            chain(dve.tensor_copy(gpart[:, 1, :], gT[:, :]))
            chain(dve.tensor_tensor(gT[:, :], gT[:, :], gpart[:, 1, :], ALU.subtract))
            chain(dve.tensor_copy(gpart[:, 2, :], gT[:, :]))

            def onehots(b, t0):
                r = b % 2
                tok = bass.ds(t0, TB)
                dve.tensor_tensor(oh2[:, r, :, :], i2T[:, tok].unsqueeze(1).broadcast_to([P, NKEY, TB]), iota2[:, :, :], ALU.is_equal)
                chain(dve.tensor_tensor(oh1[:, r, :, :], i1T[:, tok].unsqueeze(1).broadcast_to([P, GRP, TB]), iota1[:, :, :], ALU.is_equal))
                dve.tensor_tensor(ohg[:, r, :, :, :], oh1[:, r, :, :].unsqueeze(1).broadcast_to([P, 3, GRP, TB]),
                                  gpart[:, :, tok].unsqueeze(2).broadcast_to([P, 3, GRP, TB]), ALU.mult).then_inc(oh_ready, 1)

            def gates(par, t0, built):
                for half in (0, 1):
                    dve.wait_ge(g_built, built + (half + 1))
                    dve.wait_ge(small_in, 48)
                    src = B[2 + half][:, 0:8 * 3 * GRP].rearrange("p (t s i) -> p i t s", s=3, i=GRP)
                    dve.tensor_reduce(Gd[:, par, :, bass.ds(t0 + 8 * half, 8)], src, axis=AX_X, op=ALU.add).then_inc(g_evac, 1)

            def next_group():
                chain(dve.tensor_scalar(iota1[:, :, :], iota1[:, :, :], float(GRP), None, ALU.add))
                dve.memset(res[:, 0:8], 0.0)

            with dve.Fori(0, NB // 2) as i:
                chain.loop(i, 0, NB // 2, 2)
                for r in (0, 1):
                    onehots(r, i * 2 * TB + r * TB)
                    gates(0, i * 2 * TB + r * TB, i * 4 + 2 * r)
                chain.end()
            next_group()

            def pair(par, p, j, wpar, build, first=False):
                built = j * 8 + 2 * NB

                def oh(b):
                    if build:
                        dve.wait_ge(g_built, built + (2 * b - 2))
                        onehots(b, p * SLICE + b * TB)

                def ev(b):
                    if build:
                        gates(1 - par, p * SLICE + b * TB, built + 2 * b)

                def weigh(e):
                    dve.wait_ge(gelu_done, j * 2 + (e + 1))
                    g = Gd[:, par, bass.ds(p * 2 + e, 1), :].rearrange("p a t -> p (a t)")
                    chain(dve.tensor_tensor(B[e][:, :], B[e][:, :], g, ALU.mult))
                    h, l = WH[:, wpar, e, :], WL[:, wpar, e, :]
                    chain(dve.tensor_scalar(h, B[e][:, :], 1.0, None, ALU.mult))
                    dve.tensor_tensor(l, B[e][:, :], h.bitcast(F32), ALU.subtract).then_inc(w_done, 1)

                def adds(k0, k1):
                    for k in range(k0, k1):
                        if not first:
                            dve.wait_ge(y_done, (j - 1) * KD + (k + 1))
                            dve.tensor_tensor(xT[:, k, :], xT[:, k, :], B[4 + k % 4][:, :], ALU.add).then_inc(y_added, 1)

                oh(0)
                oh(1)
                dve.wait_ge(g_evac, built if build else 2 * NB * N_GRP)
                weigh(0)
                ev(0)
                oh(2)
                weigh(1)
                ev(1)
                oh(3)
                adds(0, 4)
                ev(2)
                adds(4, KD)
                ev(3)

            steps = 2 * (4 * 1 + 2 * 2)
            pair(0, 0, 0, 0, True, first=True)
            pair(0, 1, 1, 1, True)
            with dve.Fori(1, PAIRS // 2) as i:
                chain.loop(i, 1, PAIRS // 2, steps)
                for q in (0, 1):
                    pair(0, i * 2 + q, i * 2 + q, q, True)
                chain.end()
            next_group()
            with dve.Fori(0, (N_GRP - 2) // 2) as g:
                chain.loop(g, 0, (N_GRP - 2) // 2, 2 * (PAIRS // 2 * steps + 1))
                for par in (1, 0):
                    with dve.Fori(0, PAIRS // 2) as i:
                        chain.loop(i, 0, PAIRS // 2, steps)
                        for q in (0, 1):
                            pair(par, i * 2 + q, g * (2 * PAIRS) + i * 2 + (PAIRS * (2 - par) + q), q, True)
                        chain.end()
                    next_group()
                chain.end()
            with dve.Fori(0, PAIRS // 2) as i:
                chain.loop(i, 0, PAIRS // 2, 2 * 2 * 2)
                for q in (0, 1):
                    pair(1, i * 2 + q, i * 2 + ((N_GRP - 1) * PAIRS + q), q, False)
                chain.end()
            for k in range(KD):
                dve.wait_ge(y_done, (NKEY // 2 - 1) * KD + k + 1)
                dve.tensor_tensor(xT[:, k, :], xT[:, k, :], B[4 + k % 4][:, :], ALU.add).then_inc(y_added, 1)
            dve.wait_ge(y_added, NKEY // 2 * KD)
            square_sums(x_of, n_sums)
            over_root(TT, n_root + 1)
            dve.wait_ge(spread, n_spread + 1)
            for k in range(KD):
                dve.scalar_tensor_tensor(xT[:, k, :], xT[:, k, :], gain("final", k), B[5][:, :], ALU.mult, ALU.mult).then_inc(final_done, 1)

        @block.tensor
        def _(pe):
            def mm3(bank, wh, wl, xh, xl, start, stop_):
                pe.matmul(bank, wh, xh, start=start, stop=False)
                pe.matmul(bank, wh, xl, start=False, stop=False)
                return pe.matmul(bank, wl, xh, start=False, stop=stop_)

            def tile(r, bank, signal=slot_used):
                for k in range(KD):
                    c = slice(k * P, (k + 1) * P)
                    m = mm3(bank, hi[:, r, c], lo[:, r, c], inH[:, k, :], inL[:, k, :], k == 0, k == KD - 1)
                m.then_inc(signal, 1)

            def tile_by_token(r, bank):
                for t in range(TT):
                    tok = slice(t * P, (t + 1) * P)
                    for k in range(KD):
                        c = slice(k * P, (k + 1) * P)
                        m = mm3(bank[:, tok], inH[:, k, tok], inL[:, k, tok], hi[:, r, c], lo[:, r, c], k == 0, k == KD - 1)
                m.then_inc(slot_used, 1)

            def linear(s0, t0, n, lo_=0):
                with pe.Fori(lo_, n // RING) as i:
                    for r in range(RING):
                        pe.wait_ge(evac, i * RING + (t0 + r - RING + 1))
                        pe.wait_ge(lo_done, i * RING + (s0 + r + 1))
                        tile(r, B[r][:, :])

            def spread_roots(n, group, k):
                if group and k >= 2:
                    pe.wait_ge(spread_used, group - 1 + k - 1)
                for t in range(TT):
                    tok = slice(t * P, (t + 1) * P)
                    if group:
                        for g in range(2):
                            c = t * N_GRPS + 2 * k + g
                            m = pe.matmul(B[5 + k % 2][g * HD:(g + 1) * HD, tok], rr[:, c:c + 1].broadcast_to([P, HD]), ident,
                                          start=True, stop=True)
                    else:
                        m = pe.matmul(B[5 + k % 2][:, tok], rr[:, t:t + 1].broadcast_to([P, P]), ident, start=True, stop=True)
                m.then_inc(spread, 1)

            def full_norm(n, nth):
                for k in range(KD):
                    pe.wait_ge(squares, n + k + 1)
                    for t in range(TT):
                        m = pe.matmul(B[4][:, t:t + 1], sq[:, k % 2, t * P:(t + 1) * P], ones[:, 0:1],
                                      start=k == 0 and t == 0, stop=k == KD - 1, skip_group_check=True)
                    m.then_inc(sums, 1)
                pe.wait_ge(recips, nth)
                spread_roots(n, 0, 0)

            def group_norm(n, nth, used):
                for k in range(KD):
                    pe.wait_ge(squares, n + k + 1)
                    for t in range(TT):
                        c = t * N_GRPS + 2 * k
                        m = pe.matmul(B[4][:, c:c + 2], sq[:, k % 2, t * P:(t + 1) * P], blk[:, 0:P:HD], start=True, stop=True)
                    m.then_inc(sums, 1)
                pe.wait_ge(recips, nth)
                for k in range(KD):
                    spread_roots(n, used + 1, k)

            def attention(st):
                s, units = st["s"], st["units"]
                n = len(units)
                for u in range(n + 3):
                    if u < n:
                        w = units[u]
                        rows = slice(w["row"], w["row"] + HD)
                        if u >= 2:
                            pe.wait_ge(s["logit"], u - 1)
                        pe.matmul(B[4 + u % 2][:, :w["n"]], st["qk"][rows, w["q"], w["i"] * P:(w["i"] + 1) * P],
                                  st["qk"][rows, w["k"], w["k0"]:w["k0"] + w["n"]], start=True, stop=True).then_inc(s["score"], 1)
                    if 2 <= u <= n + 1:
                        v = u - 2
                        w = units[v]
                        pe.wait_ge(s["normed"], v + 1)
                        if v >= 2:
                            pe.wait_ge(s["turned_sb"], v - 1)
                        for b in range(w["n"] // P):
                            c = slice(b * P, (b + 1) * P)
                            m = pe.transpose(B[6 + v % 2][:, c], st["pr"][:, v % 4, c], ident)
                        m.then_inc(s["turned"], 1)
                    if u >= 3:
                        v = u - 3
                        w = units[v]
                        pe.wait_ge(s["turned_sb"], v + 1)
                        if w["pair"] >= 2 and (v == 0 or units[v - 1]["pair"] != w["pair"]):
                            pe.wait_ge(s["head_out"], w["pair"] - 1)
                        nb = w["n"] // P
                        for b in range(nb):
                            m = pe.matmul(B[2 + w["pair"] % 2][w["row"]:w["row"] + HD, w["i"] * P:(w["i"] + 1) * P],
                                          st["v"][:, w["k0"] // P + b, w["v"]:w["v"] + HD],
                                          st["pT"][:, v % 2, b * P:(b + 1) * P], start=b == 0, stop=b == nb - 1)
                        m.then_inc(s["mixed"], 1)


            pe.wait_ge(small_in, 48)
            n_sq, n_rt = 0, 0
            n_rt += 1
            full_norm(n_sq, n_rt)
            n_sq += KD
            pe.wait_ge(in_ready, 1)
            for r in range(RING):
                pe.wait_ge(lo_done, r + 1)
                tile(r, B[r][:, :])
            linear(S_IN, T_IN, 16, 1)
            for m in range(16, N_IN):
                pe.wait_ge(evac, m - RING + 1)
                pe.wait_ge(lo_done, m + 1)
                (tile if m < 18 else tile_by_token)(m % RING, B[m % RING][:, :])
            pe.wait_ge(evac, T_OUT)
            def z_of(m):
                h, kb, w = blocks[m]
                rows = slice(HD * (h % 2), HD * (h % 2) + HD)
                return qk1[rows, 2 + h // 2, kb * P:(kb + 1) * P], qk1[rows, h // 2, kb * P:]

            for n in range(-1, len(blocks) + 1):
                if n + 1 < len(blocks):
                    m = n + 1
                    if m >= 2:
                        pe.wait_ge(lr_ready, m - 1)
                    pe.matmul(B[2 + m % 2][:, :blocks[m][2]], *z_of(m), start=True, stop=True).then_inc(z_done, 1)
                if 0 <= n < len(blocks):
                    h, kb, w = blocks[n]
                    pe.wait_ge(lr_ready, n + 1)
                    if n >= 2:
                        pe.wait_ge(w_exp, n - 1)
                        pe.wait_ge(s_masked, n - 1)
                    s, l = B[4 + n % 2], lr[:, h % 2, :, :]
                    pe.matmul(s[:, :w], *z_of(n), start=True, stop=False)
                    m = pe.matmul(s[:, :w], tri, l[:, kb, :w], start=False, stop=kb == TT - 1)
                    for nb in range(kb + 1, TT):
                        m = pe.matmul(s[:, (nb - kb) * P:w], ones, l[:, nb, :T - nb * P], start=False, stop=nb == TT - 1)
                    m.then_inc(s_done, 1)
                if n >= 1:
                    v = n - 1
                    h, kb, w = blocks[v]
                    pe.wait_ge(w_exp, v + 1)
                    pe.matmul(B[6 + h // 2][HD * (h % 2):HD * (h % 2) + HD, kb * P:], v1[:, kb, HD * h:HD * h + HD],
                              wz[:, v % 2, :w], start=kb == TT - 1, stop=kb == 0, skip_group_check=True).then_inc(sb_out, 1)
            pe.wait_ge(y_sb, 2)
            n_rt += 1
            group_norm(n_sq, n_rt, 0)
            n_sq += KD
            pe.wait_ge(in_ready, 2)
            attention(stage1)
            n_rt += 1
            group_norm(n_sq, n_rt, KD)
            n_sq += KD
            pe.wait_ge(in_ready, 3)
            linear(S_OUT, T_OUT, N_OUT)
            n_rt += 1
            full_norm(n_sq, n_rt)
            n_sq += KD
            pe.wait_ge(in_ready, 4)
            linear(S_GU, T_GU, N_GU)
            pe.wait_ge(evac, T_DOWN)
            with pe.Fori(0, 2) as i:
                for m in range(RING):
                    pe.wait_ge(evac, i * RING + (T_DOWN + m - RING + 1))
                    for k in range(KF):
                        s, r = k // KD, (3 * m + k // KD) % RING
                        if k % KD == 0:
                            pe.wait_ge(lo_done, i * 12 + (S_DOWN + 3 * m + s + 1))
                        c = slice(k % KD * P, (k % KD + 1) * P)
                        mm = mm3(B[m][:, :], hi[:, r, c], lo[:, r, c], actH[:, k, :], actL[:, k, :], k == 0, k == KF - 1)
                        if k % KD == KD - 1 or k == KF - 1:
                            mm.then_inc(slot_used, 1)
            n_rt += 1
            full_norm(n_sq, n_rt)
            n_sq += KD
            pe.wait_ge(in_ready, 5)
            linear(S_IN2, T_IN2, 40)
            for m in range(40, N_IN2):
                pe.wait_ge(evac, T_IN2 + m - RING + 1)
                pe.wait_ge(lo_done, S_IN2 + m + 1)
                (tile if m < 42 else tile_by_token)(m % RING, B[m % RING][:, :])
            for k in range(KD):
                pe.wait_ge(conv_done, k + 1)
                pe.matmul(B[4][:, :], ones, c2[:, k, :], start=k == 0, stop=k == KD - 1).then_inc(mean_done, 1)
            n_rt += 1
            full_norm(n_sq, n_rt)
            n_sq += KD
            pe.wait_ge(in_ready, 6)
            linear(S_PW, T_PW, KD)
            pe.wait_ge(evac, T_WO)
            attention(stage2)
            pe.wait_ge(in_ready, 7)
            linear(S_WO, T_WO, KD)
            pe.wait_ge(in_ready, 8)
            linear(S_WO2, T_WO2, KD)
            n_rt += 1
            full_norm(n_sq, n_rt)
            n_sq += KD
            pe.wait_ge(in_ready, 9)
            linear(S_Q, T_Q, N_Q)
            pe.wait_ge(peer_in, 48)
            pe.wait_ge(evac, T_Q + N_Q)
            for t in range(TT):
                for b in range(4):
                    if t:
                        pe.wait_ge(sc_copied, 4 * (t - 1) + b + 1)
                    for g in range(4):
                        m = pe.matmul(B[4 + b][:, g * P:(g + 1) * P], qp[:, 4 * b + g, t * P:(t + 1) * P],
                                      key_sb[:, g % 2, :], start=True, stop=True)
                    m.then_inc(sc_done, 1)
                pe.wait_ge(sel_ready, t + 1)
                if t:
                    pe.wait_ge(selT_copied, t)
                for j in range(3):
                    m = pe.transpose(B[0][:, j * P:(j + 1) * P], sel[:, j, :], ident)
                m.then_inc(selT_done, 1)

            def build(r, n_oh, n_built):
                pe.wait_ge(oh_ready, n_oh)
                for half in (0, 1):
                    pe.wait_ge(g_evac, n_built + half - 1)
                    for t in range(8):
                        tok = half * 8 + t
                        m = pe.matmul(B[2 + half][:, t * 3 * GRP:(t + 1) * 3 * GRP], oh2[:, r, :, tok],
                                      ohg[:, r, :, :, tok], start=True, stop=True)
                    m.then_inc(g_built, 1)

            pe.wait_ge(selT_copied, TT)
            pe.wait_ge(oh_ready, 1)
            for half in (0, 1):
                for t in range(8):
                    tok = half * 8 + t
                    m = pe.matmul(B[2 + half][:, t * 3 * GRP:(t + 1) * 3 * GRP], oh2[:, 0, :, tok],
                                  ohg[:, 0, :, :, tok], start=True, stop=True)
                m.then_inc(g_built, 1)
            build(1, 2, 2)
            with pe.Fori(1, NB // 2) as i:
                for r in (0, 1):
                    build(r, i * 2 + (r + 1), i * 4 + 2 * r)

            def a_tile(e, r, n, j):
                pe.wait_ge(lo_done, n)
                if j is not None:
                    pe.wait_ge(w_done, j * 2 + (e - 1))
                tile(r, B[e][:, :], u_done)

            def y_tiles(k0, k1, wpar, j, r0):
                if k0 == 0:
                    pe.wait_ge(lo_done, j * 4 + (S_PEER + 6))
                    pe.wait_ge(w_done, j * 2 + 2)
                for k in range(k0, k1):
                    pe.wait_ge(y_added, j * KD + (k - 3)) if not (isinstance(j, int) and j * KD + k - 3 <= 0) else None
                    c = slice(k * P, (k + 1) * P)
                    for e in (0, 1):
                        m = mm3(B[4 + k % 4][:, :], hi[:, r0 + e, c], lo[:, r0 + e, c], WH[:, wpar, e, :], WL[:, wpar, e, :],
                                e == 0, e == 1)
                    m.then_inc(y_done, 1)

            def body(j, q, build_next, first=False, one=False):
                if first:
                    a_tile(0, 0, S_PEER + 1, None)
                else:
                    a_tile(0, 2, j * 4 + (S_PEER - 2 + 1), j)
                ob, gb = j * 4 + NB, j * 8 + 2 * NB
                if build_next:
                    build(0, ob + 1, gb)
                if first:
                    a_tile(1, 1, S_PEER + 2, None)
                else:
                    a_tile(1, 3, j * 4 + (S_PEER - 2 + 2), j)
                if build_next:
                    build(1, ob + 2, gb + 2)
                if not first:
                    y_tiles(0, 4, 1 - q, j - 1, 0)
                if build_next:
                    build(0, ob + 3, gb + 4)
                if not first:
                    y_tiles(4, KD, 1 - q, j - 1, 0)
                if build_next:
                    build(1, ob + 4, gb + 6)

            body(0, 0, True, first=True)
            body(1, 1, True)
            with pe.Fori(1, (N_GRP - 1) * PAIRS // 2) as i:
                for q in (0, 1):
                    body(i * 2 + q, q, True)
            with pe.Fori((N_GRP - 1) * PAIRS // 2, NKEY // 4) as i:
                for q in (0, 1):
                    body(i * 2 + q, q, False)
            last = NKEY // 2 - 1
            pe.wait_ge(lo_done, N_SLOTS)
            pe.wait_ge(w_done, 2 * last + 2)
            for k in range(KD):
                pe.wait_ge(y_added, last * KD + k - 3)
                c = slice(k * P, (k + 1) * P)
                for e in (0, 1):
                    m = mm3(B[4 + k % 4][:, :], hi[:, 2 + e, c], lo[:, 2 + e, c], WH[:, 1, e, :], WL[:, 1, e, :], e == 0, e == 1)
                m.then_inc(y_done, 1)
            full_norm(n_sq, n_rt + 1)

        return None


def lay_out(i):
    f = lambda a: np.asarray(a)

    def blocks(w):
        k, m = w.shape[0] // P, w.shape[1] // P
        return w.reshape(k, P, m, P).transpose(2, 1, 0, 3)

    def slots(w):
        b = blocks(w)
        return b.reshape(b.shape[0], P, D)

    w_in = f(i["w_in"])[0]
    o = np.cumsum([0, 256, 256, 256, 512, 512, 512, 256, 256, 256])
    part = lambda n: w_in[:, o[n]:o[n + 1]]
    win = slots(np.concatenate([part(n) for n in (0, 1, 3, 4, 6, 7, 8, 2, 5)], 1))
    wg, wu = slots(f(i["w_gate"])[0]), slots(f(i["w_up"])[0])
    gu = np.stack([wg, wu], 1).reshape(N_GU, P, D)
    wd = np.zeros((KD, P, KF_PAD, P), np.float32)
    wd[:, :, :KF] = blocks(f(i["w_down"])[0])
    wd = wd.reshape(KD, P, 3, D).transpose(0, 2, 1, 3).reshape(N_DOWN, P, D)
    w2 = f(i["w_in_2"])[0]
    a, b = slots(w2[:, :D]), slots(w2[:, D:2 * D])
    ab = np.stack([a, b], 1).reshape(16, P, D)
    heads = [4 * (2 * (j // 4) + half) + j % 4 for j in range(8) for half in (0, 1)]
    q2 = w2[:, 2048:3072].reshape(D, N_HEADS, HD)[:, heads].reshape(D, D)
    k2, vv2, g2 = w2[:, 3072:3328], w2[:, 3328:3584], w2[:, 3584:5632]
    win2 = np.concatenate([ab, slots(q2), slots(k2), slots(g2), slots(vv2)])
    wo = f(i["attn_w_o_2"])[0].reshape(N_HEADS, HD, D)[heads].reshape(D, D)
    eu = f(i["peer_u_2"])[0].reshape(NKEY, NKEY, KD, P).transpose(0, 3, 2, 1).reshape(NKEY, P, D)
    ev = f(i["peer_v_2"])[0].reshape(NKEY, NKEY, D)
    stream = np.empty((N_SLOTS, P, D), np.float32)
    n = 0
    for w in (win, slots(f(i["w_out"])[0]), gu, wd, win2, slots(f(i["conv_w_pw_2"])[0]), slots(wo),
              slots(f(i["w_out_2"])[0]), slots(f(i["peer_w_query_2"])[0])):
        stream[n:n + len(w)] = w
        n += len(w)
    assert n == S_PEER
    stream[n:n + 2] = eu[0:2]
    rest = stream[n + 2:n + 2 + 4 * (NKEY // 2 - 1)].reshape(NKEY // 2 - 1, 4, P, D)
    rest[:, 0:2] = eu[2:].reshape(NKEY // 2 - 1, 2, P, D)
    rest[:, 2:4] = ev[:-2].reshape(NKEY // 2 - 1, 2, P, D)
    stream[-2:] = ev[-2:]

    gains = np.empty((P, N_GC), np.float32)

    def put(name, a):
        gains[:, GC[name]:GC[name] + a.shape[1]] = a

    feat = lambda a: f(a).reshape(-1, P).T
    put("attn", feat(i["attn_norm_w"]))
    put("out", feat(i["out_norm_w"]))
    put("ffn", feat(i["ffn_norm_w"]))
    put("norm1", feat(i["norm1_g_2"]))
    put("norm2", feat(i["norm2_g_2"]))
    put("final", feat(i["final_g_2"]))
    put("ln_g", feat(i["conv_ln_g_2"]))
    put("ln_b", feat(i["conv_ln_b_2"]))
    put("dw_b", feat(i["conv_dw_b_2"]))
    put("dw", f(i["conv_dw_w_2"])[0].reshape(CONV_TAPS, KD, P).transpose(2, 1, 0).reshape(P, KD * CONV_TAPS))
    put("conv", f(i["conv_w"])[0].reshape(3, 2, P).transpose(2, 1, 0).reshape(P, 6))
    put("qn", np.concatenate([f(i["q_norm_w"])[0]] * 2)[:, None])
    put("kn", np.concatenate([f(i["k_norm_w"])[0]] * 2)[:, None])
    put("sink", np.broadcast_to(f(i["attn_sink_2"])[0][None], (P, N_HEADS)))
    put("eps", np.full((P, 1), EPS, np.float32))

    rel = f(i["rel_bias"])[0][:, np.clip(T - 1 - np.arange(REL), -P, P) + P]
    rel = np.tile(rel, (1, P))

    keys = np.ascontiguousarray(f(i["peer_sub_keys_2"])[0].transpose(2, 0, 1))
    x = np.ascontiguousarray(f(i["x"])[0].reshape(T, KD, P).transpose(2, 1, 0))
    return dict(x=x, stream=stream, gains=gains, rel=np.ascontiguousarray(rel), keys=keys)


def constants():
    r = np.arange(P)
    c = np.zeros((P, N_CC), np.float32)
    c[:, CC["ident"]:CC["ident"] + P] = np.eye(P)
    c[:, CC["ones"]:CC["ones"] + P] = 1
    c[:, CC["blk"]:CC["blk"] + P] = (r[:, None] // HD == r[None] // HD)
    c[:, CC["tri"]:CC["tri"] + P] = r[:, None] >= r[None]
    c[:, CC["mask"]:CC["mask"] + P] = r[:, None] < r[None]
    c[:, CC["neg"]:CC["neg"] + P] = np.where(r[:, None] < r[None], 0, NEG)
    c[:, CC["iota"]:CC["iota"] + TOPK] = np.arange(TOPK)
    dist = np.abs(r[:, None] + P - np.arange(3 * P)[None]).astype(np.float32)
    slopes = np.exp2(-8.0 * np.arange(1, N_HEADS + 1, dtype=np.float32) / N_HEADS).astype(np.float32)
    order = [4 * (2 * (j // 4) + half) + j % 4 for j in range(8) for half in (0, 1)]
    gqa = np.where(dist <= P, -slopes[order, None, None] * dist, np.float32(NEG)).astype(np.float32)
    ohc = np.empty((P, NKEY + GRP, TB), np.float32)
    ohc[:, :NKEY] = np.arange(NKEY)[None, :, None]
    ohc[:, NKEY:] = np.arange(GRP)[None, :, None]
    ohc = (ohc.view(np.uint32) >> 16).astype(np.uint16)
    return dict(consts=c, gqa=gqa, ohc=ohc)


def kernel(**inputs):
    import concourse.bacc as _bacc
    from concourse.bass_utils import run_bass_kernel_spmd as _run

    arrays = {**lay_out(inputs), **constants()}
    nc = _bacc.Bacc("TRN2", target_bir_lowering=False, num_devices=1)
    args = {n: nc.dram_tensor(n, a.shape, mybir.dt.from_np(a.dtype), kind="ExternalInput").ap() for n, a in arrays.items()}
    out = nc.dram_tensor("out", (P, KD, T), F32, kind="ExternalOutput").ap()
    program(nc, out=out, **args)
    r = _run(nc, [arrays], core_ids=[0])
    got = r.results[0]["out"]
    return got.transpose(2, 1, 0).reshape(1, T, D)
```

```python
from contextlib import ExitStack

import numpy as np

import concourse.bass as bass
from concourse import mybir

F32 = mybir.dt.float32
F32R = mybir.dt.float32r
BF16 = mybir.dt.bfloat16
U32 = mybir.dt.uint32
U16 = mybir.dt.uint16
ALU = mybir.AluOpType
ACT = mybir.ActivationFunctionType
AX_X = mybir.AxisListType.X

P = 128
D = 1024
KD = D // P
T = 512
TT = T // P
HD = 64
EPS = 1e-6
QSCALE = HD ** -0.5
NEG = -1e30

H_SB, H_CH = 4, 8
FF = 2816
KF = FF // P
KF_PAD = 24
CONV_TAPS = 31
REL = T + P
CONV_PAD = 15
UW = T + 2 * CONV_PAD
N_HEADS = 16
PH, TOPK, NKEY = 8, 16, 128
RING = 4
AHEAD = RING - 1

N_IN, N_OUT, N_GU, N_DOWN = 24, 8, 2 * KF, 3 * KD
N_IN2, N_Q = 44, 16
S_IN = 0
S_OUT = S_IN + N_IN
S_GU = S_OUT + N_OUT
S_DOWN = S_GU + N_GU
S_IN2 = S_DOWN + N_DOWN
S_PW = S_IN2 + N_IN2
S_WO = S_PW + KD
S_WO2 = S_WO + KD
S_Q = S_WO2 + KD
S_PEER = S_Q + N_Q
N_SLOTS = S_PEER + 2 * NKEY
T_IN = 0
T_OUT = T_IN + N_IN
T_GU = T_OUT + N_OUT
T_DOWN = T_GU + N_GU
T_IN2 = T_DOWN + KD
T_PW = T_IN2 + N_IN2
T_WO = T_PW + KD
T_WO2 = T_WO + KD
T_Q = T_WO2 + KD

GC = {}
_at = 0
for _name, _n in (("attn", KD), ("out", KD), ("ffn", KD), ("norm1", KD), ("norm2", KD), ("final", KD),
                  ("ln_g", KD), ("ln_b", KD), ("dw_b", KD), ("dw", KD * CONV_TAPS), ("conv", 6),
                  ("qn", 1), ("kn", 1), ("sink", N_HEADS), ("eps", 1)):
    GC[_name] = _at
    _at += _n
N_GC = _at

CC = {"ident": 0, "ones": 128, "blk": 256, "tri": 384, "mask": 512, "neg": 640, "iota": 768}
N_CC = 784
GRP = 16
PAIRS = GRP // 2
N_GRP = NKEY // GRP
TB = 16
SLICE = T // PAIRS
LN_TILE = 38
NB = T // TB
N_GRPS = D // HD


class Chain:

    def __init__(self, eng, sem):
        self.eng, self.sem, self.n, self.loops = eng, sem, 0, []

    def loop(self, i, lo, hi, per):
        self.loops.append((i, lo, hi, per, self.n))

    def end(self):
        _, lo, hi, per, n = self.loops.pop()
        assert self.n == n + per, (self.n - n, per)
        self.n = n + (hi - lo) * per

    def mark(self, ins):
        ins.then_inc(self.sem, 1)
        self.n += 1
        value = self.n
        for i, lo, _, per, _ in self.loops:
            value = i * per + (value - lo * per) if isinstance(value, int) else value + i * per + (-lo * per)
        return value

    def wait(self, value):
        self.eng.wait_ge(self.sem, value)

    def __call__(self, ins):
        self.wait(self.mark(ins))


def program(nc, x, stream, gains, consts, rel, gqa, keys, ohc, out):
    ctx = ExitStack()
    with ctx:
        at = [16512]

        def fixed(name, shape, dt=F32):
            size = int(np.prod(shape[1:])) * (2 if dt == BF16 else 4)
            t = nc.alloc_sbuf_tensor_at(name, shape, dt, offset=at[0])
            at[0] += -(-size // 32) * 32
            return t

        def sem(name):
            return ctx.enter_context(nc.semaphore(name))

        xT = fixed("xT", [P, KD, T])
        inH = fixed("inH", [P, KD, T], F32R)
        inL = fixed("inL", [P, KD, T], F32R)
        raw = fixed("raw", [P, RING, D])
        hi = fixed("hi", [P, RING, D], F32R)
        lo = fixed("lo", [P, RING, D], F32R)
        gn = fixed("gn", [P, N_GC])
        cs = fixed("cs", [P, N_CC])
        sq_at = at[0]
        sq = fixed("sq", [P, 2, T])
        rt = fixed("rt", [P, 2, T])
        res = fixed("res", [P, T])
        rr = fixed("rr", [P, TT * N_GRPS])
        arena = at[0]

        def phase():
            at[0] = arena

        phase()
        qk1 = fixed("qk1", [P, 12, T])
        cv1 = fixed("cv1", [P, 6, T])
        v1 = fixed("v1", [P, TT, 768])
        y1 = fixed("y1", [P, KD, T])
        tbl1 = fixed("tbl1", [P, 2, T])
        shared = at[0]
        lr = fixed("lr", [P, 2, TT, T])
        ez = fixed("ez", [P, 2, T])
        mz = fixed("mz", [P, 2, T])
        wz = fixed("wz", [P, 2, T])
        at[0] = shared
        pr1 = fixed("pr1", [P, 4, T])
        pT1 = fixed("pT1", [P, 2, T])
        sm1 = fixed("sm1", [P, 4, 8])
        phase()
        actH = fixed("actH", [P, KF, T], F32R)
        actL = fixed("actL", [P, KF, T], F32R)
        phase()
        u2 = fixed("u2", [P, KD, UW])
        qk2 = fixed("qk2", [P, 10, T])
        v2 = fixed("v2", [P, TT, 256])
        gate2 = fixed("gate2", [P, 16, T])
        c2_at = at[0]
        c2 = fixed("c2", [P, KD, T])
        at[0] = c2_at
        pr2 = fixed("pr2", [P, 4, 3 * P])
        pT2 = fixed("pT2", [P, 2, 3 * P])
        tbl2 = fixed("tbl2", [P, 2, 3 * P])
        sm2 = fixed("sm2", [P, 4, 8])
        m2 = u2
        phase()
        gpart = fixed("gpart", [P, 3, T], BF16)
        i1T = fixed("i1T", [P, T], BF16)
        i2T = fixed("i2T", [P, T], BF16)
        iota2 = fixed("iota2", [P, NKEY, TB], BF16)
        peer_at = at[0]
        qp = fixed("qp", [P, RING, T])
        key_sb = fixed("key_sb", [P, 2, NKEY])
        sc = fixed("sc", [P, 2, TT, NKEY])
        scb = fixed("scb", [P, TT, NKEY])
        cand = fixed("cand", [P, TT, TOPK * TOPK])
        candb = fixed("candb", [P, TT, TOPK * TOPK])
        eq = fixed("eq", [P, PH * TOPK, TOPK], BF16)
        iota_rank = fixed("iota_rank", [P, TOPK], BF16)
        vals = fixed("vals", [P, TT, N_Q, TOPK])
        idx = fixed("idx", [P, TT, N_Q, TOPK], U32)
        idxf = fixed("idxf", [P, N_Q, TOPK], BF16)
        top = fixed("top", [P, TT, PH, TOPK])
        pos = fixed("pos", [P, TT, PH, TOPK], U32)
        posb = fixed("posb", [P, 2, PH * TOPK], U32)
        posf = fixed("posf", [P, 2, PH * TOPK], BF16)
        sel = fixed("sel", [P, 2, 3, PH * TOPK])
        den = fixed("den", [P, 2, PH])
        gT = fixed("gT", [P, T])
        at[0] = peer_at
        Gd = fixed("Gd", [P, 2, GRP, T])
        WH = fixed("WH", [P, 2, 2, T], F32R)
        WL = fixed("WL", [P, 2, 2, T], F32R)
        oh2 = fixed("oh2", [P, 2, NKEY, TB], BF16)
        assert at[0] <= 229344, at[0]
        at[0] = sq_at
        iota1 = fixed("iota1", [P, GRP, TB], BF16)
        oh1 = fixed("oh1", [P, 2, GRP, TB], BF16)
        ohg = fixed("ohg", [P, 2, 3, GRP, TB], BF16)
        assert at[0] <= sq_at + 4 * T * 4

        B = [ctx.enter_context(nc.psum_tensor(f"bank{i}", [P, T], F32)) for i in range(8)]

        loaded = [sem(f"loaded{r}") for r in range(RING)]
        hi_done = sem("hi_done")
        lo_done = sem("lo_done")
        slot_used = sem("slot_used")
        evac = sem("evac")
        small_in = sem("small_in")
        squares = sem("squares")
        sums = sem("sums")
        roots = sem("roots")
        recips = sem("recips")
        spread = sem("spread")
        spread_used = sem("spread_used")
        in_ready = sem("in_ready")
        in_part = sem("in_part")
        dve_steps = sem("dve_steps")
        act_steps = sem("act_steps")
        z_done = sem("z_done")
        z_abs = sem("z_abs")
        z_soft = sem("z_soft")
        z_min = sem("z_min")
        lr_ready = sem("lr_ready")
        s_done = sem("s_done")
        s_masked = sem("s_masked")
        w_exp = sem("w_exp")
        w_ready = sem("w_ready")
        sb_out = sem("sb_out")
        att = [{n: sem(f"{n}{a}") for n in ("score", "logit", "maxed", "probs", "normed", "turned",
                                           "turned_sb", "mixed", "head_out", "tbl_free")} for a in (1, 2)]
        tbl_in = [[sem(f"tbl_in{a}{b}") for b in (0, 1)] for a in (1, 2)]
        y_sb = sem("y_sb")
        conv_done = sem("conv_done")
        mean_done = sem("mean_done")
        silu_ready = sem("silu_ready")
        peer_in = sem("peer_in")
        sc_done = sem("sc_done")
        sc_copied = sem("sc_copied")
        sc_used = sem("sc_used")
        top_ready = sem("top_ready")
        gexp = sem("gexp")
        sel_ready = sem("sel_ready")
        selT_done = sem("selT_done")
        selT_copied = sem("selT_copied")
        oh_ready = sem("oh_ready")
        g_built = sem("g_built")
        g_evac = sem("g_evac")
        gelu_done = sem("gelu_done")
        w_done = sem("w_done")
        y_done = sem("y_done")
        y_added = sem("y_added")
        out_done = sem("out_done")
        final_done = sem("final_done")
        u_done = sem("u_done")
        gate_act = sem("gate_act")
        glu_done = sem("glu_done")

        ident = cs[:, CC["ident"]:CC["ident"] + P]
        ones = cs[:, CC["ones"]:CC["ones"] + P]
        blk = cs[:, CC["blk"]:CC["blk"] + P]
        tri = cs[:, CC["tri"]:CC["tri"] + P]
        mask = cs[:, CC["mask"]:CC["mask"] + P]
        neg = cs[:, CC["neg"]:CC["neg"] + P]
        iota16 = cs[:, CC["iota"]:CC["iota"] + TOPK]

        def by_token(v, m, n):
            return v[:, 2 * (m % 2):2 * (m % 2) + 2, n // 2 * 2 * P:(n // 2 + 1) * 2 * P]

        def gain(name, k=0):
            return gn[:, GC[name] + k:GC[name] + k + 1]


        units1 = []
        for h in range(H_CH):
            for i in range(TT):
                units1.append(dict(q=4 + h // 2, k=8 + h // 2, row=HD * (h % 2), i=i, k0=0, n=(i + 1) * P,
                                   c0=(TT - 1 - i) * P, head=h, sink=None, v=256 + HD * h, pair=h // 2, dst=2 + h // 2))
        units2 = []
        for j in range(N_HEADS // 2):
            for half in (0, 1):
                kv = 2 * (j // 4) + half
                head = 4 * kv + j % 4
                for i in range(TT):
                    first, last = max(i - 1, 0), min(i + 1, TT - 1)
                    units2.append(dict(q=j, k=8 + kv // 2, row=HD * half, i=i, k0=first * P,
                                       n=(last - first + 1) * P, c0=(first - i + 1) * P, head=head,
                                       sink=head, v=HD * kv, pair=j, dst=j))
        stage1 = dict(units=units1, qk=qk1, v=v1, tbl=tbl1, pr=pr1, pT=pT1, sm=sm1, s=att[0], tbl_in=tbl_in[0],
                      dst=y1)
        stage2 = dict(units=units2, qk=qk2, v=v2, tbl=tbl2, pr=pr2, pT=pT2, sm=sm2, s=att[1], tbl_in=tbl_in[1],
                      dst=qk2)


        blocks = [(h, kb, T - kb * P) for h in range(H_SB) for kb in reversed(range(TT))]

        block = ctx.enter_context(nc.Block())

        @block.sync
        def _(sp):
            def load(n, r):
                sp.dma_start(raw[:, r, :], stream[bass.ds(n, 1)].rearrange("a p n -> (a p) n")).then_inc(loaded[r], 16)

            sp.dma_start(gn[:, :], gains).then_inc(small_in, 16)
            sp.dma_start(cs[:, :], consts).then_inc(small_in, 16)
            sp.dma_start(xT[:, :, :], x).then_inc(small_in, 16)
            for r in range(RING):
                load(r, r)
            with sp.Fori(1, N_SLOTS // RING) as i:
                for r in range(RING):
                    sp.wait_ge(lo_done, i * RING + (r - RING + 1))
                    load(i * RING + r, r)
            for n in range(N_SLOTS // RING * RING, N_SLOTS):
                sp.wait_ge(lo_done, n - RING + 1)
                load(n, n % RING)

        @block.gpsimd
        def _(pool):
            def low(n, r):
                pool.wait_ge(hi_done, n + 1)
                pool.tensor_tensor(lo[:, r, :], raw[:, r, :], hi[:, r, :].bitcast(F32), ALU.subtract).then_inc(lo_done, 1)

            with pool.Fori(0, N_SLOTS // RING) as i:
                for r in range(RING):
                    low(i * RING + r, r)
            for n in range(N_SLOTS // RING * RING, N_SLOTS):
                low(n, n % RING)

        @block.scalar
        def _(act):
            chain = Chain(act, act_steps)

            def high(n0, i, r, first=False):
                n = i * RING + (n0 + r)
                act.wait_ge(loaded[r % RING], i * 16 + 16 * ((n0 + r) // RING + 1))
                if not first:
                    act.wait_ge(slot_used, n - RING + 1)
                act.activation(hi[:, r % RING, :], raw[:, r % RING, :], ACT.Copy).then_inc(hi_done, 1)

            def highs(s0, n, epilogue=None):
                with act.Fori(0, n // RING) as i:
                    for r in range(RING):
                        high(s0, i, r + AHEAD)
                        if epilogue:
                            epilogue(i, r)

            def root_of(width, scale, n_sums):
                act.wait_ge(sums, n_sums)
                act.activation(rr[:, :width], B[4][:, :width], ACT.Sqrt, bias=gain("eps"), scale=scale).then_inc(roots, 1)

            def table(st, head):
                src = (bass.AP(tensor=rel.tensor, offset=head * P * REL + P - 1, ap=[[REL - 1, P], [1, T]]) if st is stage1
                       else gqa[head])
                act.dma_start(st["tbl"][:, head % 2, :], src).then_inc(st["tbl_in"][head % 2], 16)

            def attention(st):
                s, units = st["s"], st["units"]
                n = len(units)
                for u in range(n + 4):
                    if 0 < u < n and u % TT == 0 and u // TT + 1 < n // TT:
                        act.wait_ge(s["maxed"], u)
                        table(st, u // TT + 1)
                    if u < n:
                        w = units[u]
                        pr, sm = st["pr"][:, u % 4, :w["n"]], st["sm"][:, u % 4, :]
                        act.wait_ge(s["maxed"], u + 1)
                        e = act.activation(pr, pr, ACT.Exp, bias=sm[:, 1:2], accum_out=sm[:, 2:3])
                        if w["sink"] is None:
                            e.then_inc(s["probs"], 1)
                        else:
                            act.activation(sm[:, 3:4], gain("sink", w["sink"]), ACT.Exp, bias=sm[:, 1:2]).then_inc(s["probs"], 1)
                    v = u - 2
                    if 0 <= v < n:
                        w = units[v]
                        act.wait_ge(s["turned"], v + 1)
                        if v >= 2:
                            act.wait_ge(s["mixed"], v - 1)
                        act.activation(st["pT"][:, v % 2, :w["n"]], B[6 + v % 2][:, :w["n"]], ACT.Copy).then_inc(s["turned_sb"], 1)
                    v = u - 4
                    if v >= 0 and (v == n - 1 or units[v + 1]["pair"] != units[v]["pair"]):
                        pair = units[v]["pair"]
                        act.wait_ge(s["mixed"], v + 1)
                        act.activation(st["dst"][:, units[v]["dst"], :], B[2 + pair % 2][:, :], ACT.Copy).then_inc(s["head_out"], 1)

            table(stage1, 0)
            table(stage1, 1)
            act.wait_ge(small_in, 48)
            for n in range(AHEAD):
                high(0, 0, n, first=True)
            root_of(TT, 1.0 / D, KD)
            n_sums = KD
            for r in range(RING):
                high(S_IN, 0, r + AHEAD, first=r + AHEAD < RING)
            with act.Fori(1, N_IN // RING) as i:
                for r in range(RING):
                    high(S_IN, i, r + AHEAD)
            act.preload_act_table_set("natural_log_exp_and_others")
            for n in range(-1, len(blocks)):
                if n + 1 < len(blocks):
                    m = n + 1
                    w = blocks[m][2]
                    act.wait_ge(z_done, m + 1)
                    if m >= 2:
                        act.wait_ge(lr_ready, m - 1)
                    act.activation(ez[:, m % 2, :w], B[2 + m % 2][:, :w], ACT.Abs).then_inc(z_abs, 1)
                    act.wait_ge(z_abs, m + 1)
                    chain(act.activation(ez[:, m % 2, :w], ez[:, m % 2, :w], ACT.Exp, scale=-1.0))
                    act.activation(ez[:, m % 2, :w], ez[:, m % 2, :w], ACT.Ln, bias=1.0).then_inc(z_soft, 1)
                if n < 0:
                    continue
                h, kb, w = blocks[n]
                act.wait_ge(s_masked, n + 1)
                if n >= 2:
                    act.wait_ge(sb_out, n - 1)
                e = act.activation(wz[:, n % 2, :P], mz[:, n % 2, :P], ACT.Exp)
                if w > P:
                    e = act.activation(wz[:, n % 2, P:w], B[4 + n % 2][:, P:w], ACT.Exp)
                e.then_inc(w_exp, 1)
                if h % 2 and kb == TT - 1 and h > 1 or n == len(blocks) - 1:
                    pair = H_SB // 2 - 1 if n == len(blocks) - 1 else h // 2 - 1
                    act.wait_ge(sb_out, len(blocks) if n == len(blocks) - 1 else (pair + 1) * 2 * TT)
                    act.activation(y1[:, pair, :], B[6 + pair][:, :], ACT.Copy).then_inc(y_sb, 1)
            root_of(TT * N_GRPS, 1.0 / HD, n_sums + KD)
            n_sums += KD
            attention(stage1)
            root_of(TT * N_GRPS, 1.0 / HD, n_sums + KD)
            n_sums += KD
            highs(S_OUT, N_OUT)
            root_of(TT, 1.0 / D, n_sums + KD)
            n_sums += KD

            def silu(i, r):
                if r % 2 == 0:
                    act.wait_ge(evac, i * RING + (T_GU + r - 2))
                    act.wait_ge(slot_used, i * RING + (S_GU + r + 1))
                    act.activation(sq[:, r // 2, :], B[r][:, :], ACT.Silu).then_inc(gate_act, 1)

            highs(S_GU, N_GU, silu)
            highs(S_DOWN, N_DOWN)
            root_of(TT, 1.0 / D, n_sums + KD)
            n_sums += KD

            def silu_conv(k):
                act.wait_ge(conv_done, KD + k + 1)
                act.activation(c2[:, k, :], c2[:, k, :], ACT.Silu).then_inc(silu_ready, 1)

            for m in range(N_IN2):
                if m == LN_TILE:
                    root_of(TT, 1.0 / D, n_sums + KD)
                    n_sums += KD
                high(S_IN2, 0, m + AHEAD)
                g, r = m // 4, m % 4
                bank = B[m % RING]
                act.wait_ge(slot_used, S_IN2 + m + 1)
                o = 2 * g + r - 2 if m < 4 * KD else m - 2 * KD
                if m < 4 * KD and r == 0:
                    e = act.activation(u2[:, g, CONV_PAD:CONV_PAD + T], bank[:, :], ACT.Copy)
                elif m < 4 * KD and r == 1:
                    if g >= 2:
                        act.wait_ge(glu_done, g - 1)
                    e = act.activation(sq[:, g % 2, :], bank[:, :], ACT.Sigmoid)
                elif o < 10:
                    e = act.activation(qk2[:, o, :], bank[:, :], ACT.Copy, scale=QSCALE if o < 8 else 1.0)
                elif o < 26:
                    e = act.activation(gate2[:, o - 10, :], bank[:, :], ACT.Sigmoid)
                else:
                    e = act.activation(by_token(v2, m, o - 26), bank[:, :].rearrange("p (t c) -> p t c", t=2), ACT.Copy)
                e.then_inc(evac, 1)
                if LN_TILE < m < LN_TILE + 5:
                    silu_conv(2 * (m - LN_TILE) - 2)
                    silu_conv(2 * (m - LN_TILE) - 1)
            highs(S_PW, KD)
            act.wait_ge(in_ready, 6)
            table(stage2, 0)
            table(stage2, 1)
            attention(stage2)
            highs(S_WO, KD)
            highs(S_WO2, KD)
            root_of(TT, 1.0 / D, n_sums + KD)
            n_sums += KD
            act.wait_ge(in_ready, 9)
            act.dma_start(iota2[:, :, :].bitcast(U16), ohc[:, 0:NKEY, :]).then_inc(peer_in, 16)
            act.dma_start(iota1[:, :, :].bitcast(U16), ohc[:, NKEY:NKEY + GRP, :]).then_inc(peer_in, 16)
            act.dma_start(key_sb[:, :, :], keys).then_inc(peer_in, 16)
            def scores_out(m):
                if m >= 2:
                    act.wait_ge(sc_used, m - 1)
                act.wait_ge(sc_done, m + 1)
                act.activation(sc[:, m % 2, :, :], B[4 + m % 2][:, :].rearrange("p (t k) -> p t k", t=TT), ACT.Copy).then_inc(sc_copied, 1)

            for m in range(N_Q):
                if m + AHEAD < N_Q + 2:
                    high(S_Q, 0, m + AHEAD)
                act.wait_ge(evac, T_Q + m)
                act.wait_ge(slot_used, S_Q + m + 1)
                if m >= RING:
                    act.wait_ge(sc_done, m - RING + 1)
                act.activation(qp[:, m % RING, :], B[m % RING][:, :], ACT.Copy).then_inc(evac, 1)
                if m:
                    scores_out(m - 1)
            scores_out(N_Q - 1)
            for t in range(TT):
                act.wait_ge(top_ready, t + 1)
                act.activation(sel[:, t % 2, 0, :], sel[:, t % 2, 0, :], ACT.Exp).then_inc(gexp, 1)
                act.wait_ge(selT_done, t + 1)
                act.activation(gT[:, t * P:(t + 1) * P], B[6 + t % 2][:, 0:P], ACT.Copy)
                act.activation(i1T[:, t * P:(t + 1) * P], B[6 + t % 2][:, P:2 * P], ACT.Copy)
                act.activation(i2T[:, t * P:(t + 1) * P], B[6 + t % 2][:, 2 * P:3 * P], ACT.Copy).then_inc(selT_copied, 1)

            with act.Fori(0, NB // 2) as i:
                for r in (0, 1):
                    act.wait_ge(g_built, i * 2 + (r + 1))
                    act.wait_ge(small_in, 48)
                    act.activation(Gd[:, 0, :, bass.ds(i * 2 * TB + r * TB, TB)],
                                   B[2 + r][:, :TB * GRP].rearrange("p (t i) -> p i t", i=GRP), ACT.Copy).then_inc(g_evac, 1)

            def gelu(e, done):
                act.wait_ge(u_done, done)
                act.activation(B[e][:, :], B[e][:, :], ACT.Gelu).then_inc(gelu_done, 1)

            def high_peer(i, r, n_loads):
                act.wait_ge(loaded[r], i * 16 + n_loads * 16)
                act.wait_ge(small_in, 48)
                act.activation(hi[:, r, :], raw[:, r, :], ACT.Copy).then_inc(hi_done, 1)

            for e in (0, 1):
                high(S_PEER, 0, e + 2)
                gelu(e, e + 1)
            def pair(j):
                for e in (0, 1):
                    act.wait_ge(*((u_done, 2) if isinstance(j, int) else (y_done, j * KD + (-KD))))
                    high_peer(j, e, S_PEER // RING + 1)
                    gelu(e, j * 2 + (e + 1))
                for e in (0, 1):
                    act.wait_ge(u_done, j * 2 + (e + 1))
                    high_peer(j, e + 2, S_PEER // RING + 1)

            pair(1)
            with act.Fori(2, NKEY // 2) as j:
                pair(j)
            root_of(TT, 1.0 / D, n_sums + KD)
            for k in range(KD):
                act.wait_ge(final_done, k + 1)
                act.dma_start(out[:, k, :], xT[:, k, :]).then_inc(out_done, 16)
            act.wait_ge(out_done, 16 * KD)

        @block.vector
        def _(dve):
            chain = Chain(dve, dve_steps)

            parts = [0]

            def split(src, h, l):
                chain(dve.tensor_scalar(h, src, 1.0, None, ALU.mult))
                dve.tensor_tensor(l, src, h.bitcast(F32), ALU.subtract).then_inc(in_part, 1)
                parts[0] += 1
                dve.wait_ge(in_part, parts[0])

            def square_sums(src, n):
                for k in range(KD):
                    if k >= 2:
                        dve.wait_ge(sums, n + k - 1)
                    dve.tensor_tensor(sq[:, k % 2, :], src(k), src(k), ALU.mult).then_inc(squares, 1)

            def square(x, k):
                if k == 0:
                    chain(dve.tensor_tensor(sq[:, 0, :], x, x, ALU.mult))
                    return
                chain(dve.tensor_tensor(sq[:, 1, :], x, x, ALU.mult))
                ins = dve.tensor_tensor(sq[:, 0, :], sq[:, 0, :], sq[:, 1, :], ALU.add)
                if k < KD - 1:
                    chain(ins)
                else:
                    ins.then_inc(squares, KD)

            def norm(src, gname, nth_root, n_spread):
                over_root(TT, nth_root)
                dve.wait_ge(spread, n_spread + 1)
                for k in range(KD):
                    chain(dve.scalar_tensor_tensor(res[:, :], src(k), gain(gname, k), B[5][:, :], ALU.mult, ALU.mult))
                    split(res[:, :], inH[:, k, :], inL[:, k, :])

            def over_root(width, nth_root):
                dve.wait_ge(roots, nth_root)
                dve.reciprocal(rr[:, :width], rr[:, :width]).then_inc(recips, 1)

            def group_norm(src, put, n, nth_root, n_spread):
                square_sums(src, n)
                over_root(TT * N_GRPS, nth_root)
                for k in range(KD):
                    dve.wait_ge(spread, n_spread + k + 1)
                    put(k, B[5 + k % 2][:, :])

            def take(n, ins):
                ins.then_inc(evac, 1)

            def attention(st):
                s, units = st["s"], st["units"]
                n = len(units)
                for u in range(n + 1):
                    if u < n:
                        w = units[u]
                        pr, sm = st["pr"][:, u % 4, :w["n"]], st["sm"][:, u % 4, :]
                        hn = u // TT
                        if u % TT == 0:
                            dve.wait_ge(st["tbl_in"][hn % 2], 16 * (hn // 2 + 1))
                            if st is stage1:
                                chain(dve.memset(tbl1[0:HD, hn % 2, T - HD:T], NEG))
                        dve.wait_ge(s["score"], u + 1)
                        if u >= 4:
                            dve.wait_ge(s["turned"], u - 3)
                        dve.tensor_tensor_reduce(out=pr, in0=B[4 + u % 2][:, :w["n"]],
                                                 in1=st["tbl"][:, hn % 2, w["c0"]:w["c0"] + w["n"]], scale=1.0, scalar=-3.0e38,
                                                 op0=ALU.add, op1=ALU.max, accum_out=sm[:, 0:1]).then_inc(s["logit"], 1)
                        dve.wait_ge(s["logit"], u + 1)
                        if w["sink"] is None:
                            dve.tensor_scalar(sm[:, 1:2], sm[:, 0:1], -1.0, None, ALU.mult).then_inc(s["maxed"], 1)
                        else:
                            dve.tensor_scalar(sm[:, 1:2], sm[:, 0:1], gain("sink", w["sink"]), -1.0, ALU.max, ALU.mult).then_inc(s["maxed"], 1)
                    if u >= 1:
                        v = u - 1
                        w = units[v]
                        sm = st["sm"][:, v % 4, :]
                        pr = st["pr"][:, v % 4, :w["n"]]
                        dve.wait_ge(s["probs"], v + 1)
                        if w["sink"] is not None:
                            chain(dve.tensor_tensor(sm[:, 2:3], sm[:, 2:3], sm[:, 3:4], ALU.add))
                        chain(dve.reciprocal(sm[:, 4:5], sm[:, 2:3]))
                        dve.tensor_scalar(pr, pr, sm[:, 4:5], None, ALU.mult).then_inc(s["normed"], 1)


            x_of = lambda k: xT[:, k, :]
            dve.wait_ge(small_in, 48)
            n_sums, n_root, n_spread = 0, 0, 0
            for k in range(KD):
                square(x_of(k), k)
            norm(x_of, "attn", n_root + 1, n_spread)
            n_spread += 1
            dve.sem_inc(in_ready, 1)
            n_sums += KD
            n_root += 1
            for m in range(N_IN):
                dve.wait_ge(slot_used, S_IN + m + 1)
                bank = B[m % RING]
                if m < 12:
                    take(m, dve.tensor_scalar(qk1[:, m, :], bank[:, :], QSCALE if m < 2 else 1.0, None, ALU.mult))
                elif m < 18:
                    take(m, dve.tensor_copy(cv1[:, m - 12, :], bank[:, :]))
                else:
                    take(m, dve.tensor_copy(by_token(v1, m, m - 18), bank[:, :].rearrange("p (t c) -> p t c", t=2)))
            dve.wait_ge(evac, T_OUT)
            for n in range(-1, len(blocks)):
                if n + 1 < len(blocks):
                    m = n + 1
                    h, kb, w = blocks[m]
                    l = lr[:, h % 2, kb, :]
                    dve.wait_ge(z_abs, m + 1)
                    chain(dve.tensor_scalar(l[:, :w], B[2 + m % 2][:, :w], -1.0, 0.0, ALU.mult, ALU.min))
                    dve.wait_ge(z_soft, m + 1)
                    chain(dve.tensor_tensor(l[:, :w], l[:, :w], ez[:, m % 2, :w], ALU.subtract))
                    dve.tensor_tensor(l[:, :P], l[:, :P], mask, ALU.mult).then_inc(lr_ready, 1)
                if n >= 0:
                    dve.wait_ge(s_done, n + 1)
                    if n >= 2:
                        dve.wait_ge(w_exp, n - 1)
                    dve.tensor_tensor(mz[:, n % 2, :P], B[4 + n % 2][:, :P], neg, ALU.add).then_inc(s_masked, 1)
            for m in range(2):
                gb, gc, xc = cv1[:, m, :], cv1[:, 2 + m, :], cv1[:, 4 + m, :]
                tap = [gain("conv", 3 * m + j) for j in range(3)]
                chain(dve.tensor_tensor(gc, gc, xc, ALU.mult))
                chain(dve.tensor_scalar(xc, gc, tap[2], None, ALU.mult))
                chain(dve.scalar_tensor_tensor(xc[:, 1:], gc[:, :T - 1], tap[1], xc[:, 1:], ALU.mult, ALU.add))
                chain(dve.scalar_tensor_tensor(xc[:, 2:], gc[:, :T - 2], tap[0], xc[:, 2:], ALU.mult, ALU.add))
                chain(dve.tensor_tensor(y1[:, 6 + m, :], xc, gb, ALU.mult))
            chain(dve.tensor_scalar(gain("qn"), gain("qn"), QSCALE, None, ALU.mult))

            def put_qk(k, r):
                t = qk1[:, 4 + k, :]
                dve.scalar_tensor_tensor(t, t, gain("qn" if k < 4 else "kn"), r, ALU.mult, ALU.mult).then_inc(spread_used, 1)
            group_norm(lambda k: qk1[:, 4 + k, :], put_qk, n_sums, n_root + 1, n_spread)
            n_spread += KD
            dve.wait_ge(spread_used, KD)
            dve.sem_inc(in_ready, 1)
            n_sums += KD
            n_root += 1
            attention(stage1)
            dve.wait_ge(att[0]["head_out"], 4)

            def put_y(k, r):
                dve.scalar_tensor_tensor(res[:, :], y1[:, k, :], gain("out", k), r, ALU.mult, ALU.mult).then_inc(spread_used, 1)
                dve.wait_ge(spread_used, KD + k + 1)
                split(res[:, :], inH[:, k, :], inL[:, k, :])
            dve.wait_ge(y_sb, 2)
            group_norm(lambda k: y1[:, k, :], put_y, n_sums, n_root + 1, n_spread)
            n_spread += KD
            dve.sem_inc(in_ready, 1)
            n_sums += KD
            n_root += 1

            def add_x(s_last, k):
                dve.wait_ge(slot_used, s_last)
                take(None, dve.tensor_tensor(xT[:, k, :], xT[:, k, :], B[k % RING][:, :], ALU.add))

            for k in range(KD):
                add_x(S_OUT + k + 1, k)
                dve.wait_ge(evac, T_OUT + k + 1)
                square(x_of(k), k)
            dve.wait_ge(evac, T_GU)
            norm(x_of, "ffn", n_root + 1, n_spread)
            n_spread += 1
            dve.sem_inc(in_ready, 1)
            n_sums += KD
            n_root += 1
            with dve.Fori(0, N_GU // RING) as i:
                chain.loop(i, 0, N_GU // RING, 4)
                for r in (0, 1):
                    dve.wait_ge(gate_act, i * 2 + (r + 1))
                    dve.wait_ge(slot_used, i * RING + (S_GU + 2 * r + 2))
                    chain(dve.tensor_tensor(rt[:, r, :], sq[:, r, :], B[2 * r + 1][:, :], ALU.mult))
                    h, l = actH[:, bass.ds(i * 2 + r, 1), :], actL[:, bass.ds(i * 2 + r, 1), :]
                    src = rt[:, r:r + 1, :]
                    chain(dve.tensor_scalar(h, src, 1.0, None, ALU.mult))
                    dve.tensor_tensor(l, src, h.bitcast(F32), ALU.subtract).then_inc(evac, 2)
                chain.end()
            for k in range(KD):
                add_x(S_DOWN + 3 * (k + 1), k)
                dve.wait_ge(evac, T_DOWN + k + 1)
                square(x_of(k), k)
            dve.wait_ge(evac, T_IN2)
            norm(x_of, "norm1", n_root + 1, n_spread)
            n_spread += 1
            chain(dve.memset(u2[:, :, 0:CONV_PAD], 0.0))
            chain(dve.memset(u2[:, :, CONV_PAD + T:UW], 0.0))
            dve.sem_inc(in_ready, 1)
            n_sums += KD
            n_root += 1
            def taps(k):
                def tap(j):
                    return u2[:, k, j:j + T], gain("dw", k * CONV_TAPS + j)
                t, odd = c2[:, k, :], res[:, :]
                done = [chain.mark(dve.tensor_scalar(t, *tap(0), gain("dw_b", k), ALU.mult, ALU.add)),
                        chain.mark(dve.tensor_scalar(odd, *tap(1), None, ALU.mult))]
                for j in range(2, CONV_TAPS):
                    chain.wait(done[j - 2])
                    d = odd if j % 2 else t
                    done.append(chain.mark(dve.scalar_tensor_tensor(d, *tap(j), d, ALU.mult, ALU.add)))
                chain.wait(done[-1])
                dve.tensor_tensor(t, t, odd, ALU.add).then_inc(conv_done, 1)
                dve.wait_ge(conv_done, k + 1)

            for k in range(KD):
                u = u2[:, k, CONV_PAD:CONV_PAD + T]
                dve.wait_ge(evac, T_IN2 + 4 * k + 2)
                dve.tensor_tensor(u, u, sq[:, k % 2, :], ALU.mult).then_inc(glu_done, 1)
                dve.wait_ge(glu_done, k + 1)
                taps(k)
            dve.wait_ge(mean_done, KD)
            dve.wait_ge(conv_done, KD)
            chain(dve.tensor_scalar(rt[:, 1, :], B[4][:, :], 1.0 / D, None, ALU.mult))
            centred = [chain.mark(dve.tensor_tensor(c2[:, k, :], c2[:, k, :], rt[:, 1, :], ALU.subtract)) for k in range(KD)]
            chain.wait(centred[-1])
            for k in range(KD):
                square(c2[:, k, :], k)
            over_root(TT, n_root + 1)
            dve.wait_ge(spread, n_spread + 1)
            n_sums += KD
            n_root += 1
            n_spread += 1
            normed = []

            def shift(k):
                chain.wait(normed[k])
                dve.tensor_scalar(c2[:, k, :], c2[:, k, :], gain("ln_b", k), None, ALU.add).then_inc(conv_done, 1)

            for k in range(KD):
                t = c2[:, k, :]
                normed.append(chain.mark(dve.scalar_tensor_tensor(t, t, gain("ln_g", k), B[5][:, :], ALU.mult, ALU.mult)))
                if k:
                    shift(k - 1)
            shift(KD - 1)
            dve.wait_ge(evac, T_PW)
            for k in range(KD):
                dve.wait_ge(silu_ready, k + 1)
                split(c2[:, k, :], inH[:, k, :], inL[:, k, :])
            dve.sem_inc(in_ready, 1)
            for k in range(KD):
                dve.wait_ge(slot_used, S_PW + k + 1)
                take(None, dve.tensor_tensor(m2[:, k, :T], gate2[:, k, :], B[k % RING][:, :], ALU.mult))
            attention(stage2)
            dve.wait_ge(att[1]["head_out"], KD)
            for k in range(KD):
                split(qk2[:, k, :], inH[:, k, :], inL[:, k, :])
            dve.sem_inc(in_ready, 1)
            for k in range(KD):
                dve.wait_ge(slot_used, S_WO + k + 1)
                dve.tensor_tensor(sq[:, k % 2, :], gate2[:, KD + k, :], B[k % RING][:, :], ALU.mult).then_inc(evac, 1)
                dve.wait_ge(evac, T_WO + k + 1)
                chain(dve.tensor_tensor(m2[:, k, :T], m2[:, k, :T], sq[:, k % 2, :], ALU.add))
            for k in range(KD):
                split(m2[:, k, :T], inH[:, k, :], inL[:, k, :])
            dve.sem_inc(in_ready, 1)
            for k in range(KD):
                add_x(S_WO2 + k + 1, k)
                dve.wait_ge(evac, T_WO2 + k + 1)
                square(x_of(k), k)
            dve.wait_ge(evac, T_Q)
            norm(x_of, "norm2", n_root + 1, n_spread)
            n_spread += 1
            n_sums += KD
            n_root += 1
            dve.sem_inc(in_ready, 1)
            dve.wait_ge(peer_in, 48)
            chain(dve.tensor_copy(iota_rank[:, :], iota16))

            def best(srcs, rests, tops, places):
                first = [chain.mark(dve.max(out=t[:, 0:8], in_=s)) for s, t in zip(srcs, tops)]
                left = []
                for s, b, t, p, done in zip(srcs, rests, tops, places, first):
                    chain.wait(done)
                    dve.max_index(out=p[:, 0:8], in_max=t[:, 0:8], in_values=s)
                    left.append(chain.mark(dve.match_replace(out=b, in_to_replace=t[:, 0:8], in_values=s, imm_value=-3.0e38)))
                second = []
                for b, t, done in zip(rests, tops, left):
                    chain.wait(done)
                    second.append(chain.mark(dve.max(out=t[:, 8:16], in_=b)))
                for b, t, p, done in zip(rests, tops, places, second):
                    chain.wait(done)
                    last = chain.mark(dve.max_index(out=p[:, 8:16], in_max=t[:, 8:16], in_values=b))
                return last

            for m in range(N_Q):
                dve.wait_ge(sc_copied, m + 1)
                last = best([sc[:, m % 2, t, :] for t in range(TT)], [scb[:, t, :] for t in range(TT)],
                            [vals[:, t, m, :] for t in range(TT)], [idx[:, t, m, :] for t in range(TT)])
                chain.wait(last)
                dve.sem_inc(sc_used, 1)
                if m % 2:
                    h = m // 2
                    chain(dve.tensor_tensor(cand[:, :, :].rearrange("p t (a b) -> p t a b", a=TOPK),
                                            vals[:, :, m - 1, :].unsqueeze(3).broadcast_to([P, TT, TOPK, TOPK]),
                                            vals[:, :, m, :].unsqueeze(2).broadcast_to([P, TT, TOPK, TOPK]), ALU.add))
                    last = best([cand[:, t, :] for t in range(TT)], [candb[:, t, :] for t in range(TT)],
                                [top[:, t, h, :] for t in range(TT)], [pos[:, t, h, :] for t in range(TT)])
            chain.wait(last)
            for t in range(TT):
                if t >= 2:
                    dve.wait_ge(selT_copied, t - 1)
                s0 = sel[:, t % 2, 0, :].rearrange("p (h k) -> p h k", h=PH)
                dve.tensor_tensor(s0, top[:, t, :, :], top[:, t, :, 0:1].broadcast_to([P, PH, TOPK]), ALU.subtract).then_inc(top_ready, 1)
                pf = pos[:, t, :, :].rearrange("p h k -> p (h k)")
                chain(dve.tensor_scalar(posb[:, 0, :], pf, 4, None, ALU.logical_shift_right))
                chain(dve.tensor_scalar(posb[:, 1, :], pf, 15, None, ALU.bitwise_and))
                chain(dve.tensor_copy(posf[:, :, :], posb[:, :, :]))
                chain(dve.tensor_copy(idxf[:, :, :], idx[:, t, :, :]))
                i4 = idxf[:, :, :].rearrange("p (h s) k -> p h s k", s=2)
                for s in (0, 1):
                    chain(dve.tensor_tensor(eq[:, :, :], posf[:, s, :].unsqueeze(2).broadcast_to([P, PH * TOPK, TOPK]),
                                            iota_rank[:, :].unsqueeze(1).broadcast_to([P, PH * TOPK, TOPK]), ALU.is_equal))
                    e4 = eq[:, :, :].rearrange("p (h k) a -> p h k a", h=PH)
                    chain(dve.tensor_tensor(e4, e4, i4[:, :, s, :].unsqueeze(2).broadcast_to([P, PH, TOPK, TOPK]), ALU.mult))
                    chain(dve.tensor_reduce(sel[:, t % 2, 1 + s, :], eq[:, :, :], axis=AX_X, op=ALU.add))
                dve.wait_ge(gexp, t + 1)
                chain(dve.tensor_reduce(den[:, 0, :], s0, axis=AX_X, op=ALU.add))
                chain(dve.reciprocal(den[:, 1, :], den[:, 0, :]))
                dve.tensor_tensor(s0, s0, den[:, 1, :].unsqueeze(2).broadcast_to([P, PH, TOPK]), ALU.mult).then_inc(sel_ready, 1)
            dve.wait_ge(selT_copied, TT)
            chain(dve.tensor_copy(gpart[:, 0, :], gT[:, :]))
            chain(dve.tensor_tensor(gT[:, :], gT[:, :], gpart[:, 0, :], ALU.subtract))
            chain(dve.tensor_copy(gpart[:, 1, :], gT[:, :]))
            chain(dve.tensor_tensor(gT[:, :], gT[:, :], gpart[:, 1, :], ALU.subtract))
            chain(dve.tensor_copy(gpart[:, 2, :], gT[:, :]))

            def onehots(b, t0):
                r = b % 2
                tok = bass.ds(t0, TB)
                narrow = chain.mark(dve.tensor_tensor(oh1[:, r, :, :], i1T[:, tok].unsqueeze(1).broadcast_to([P, GRP, TB]),
                                                      iota1[:, :, :], ALU.is_equal))
                dve.tensor_tensor(oh2[:, r, :, :], i2T[:, tok].unsqueeze(1).broadcast_to([P, NKEY, TB]), iota2[:, :, :], ALU.is_equal)
                chain.wait(narrow)
                dve.tensor_tensor(ohg[:, r, :, :, :], oh1[:, r, :, :].unsqueeze(1).broadcast_to([P, 3, GRP, TB]),
                                  gpart[:, :, tok].unsqueeze(2).broadcast_to([P, 3, GRP, TB]), ALU.mult).then_inc(oh_ready, 1)

            def gates(par, t0, built):
                for half in (0, 1):
                    dve.wait_ge(g_built, built + (half + 1))
                    dve.wait_ge(small_in, 48)
                    src = B[2 + half][:, 0:8 * 3 * GRP].rearrange("p (t s i) -> p i t s", s=3, i=GRP)
                    dve.tensor_reduce(Gd[:, par, :, bass.ds(t0 + 8 * half, 8)], src, axis=AX_X, op=ALU.add).then_inc(g_evac, 1)

            def next_group():
                chain(dve.tensor_scalar(iota1[:, :, :], iota1[:, :, :], float(GRP), None, ALU.add))
                dve.memset(res[:, 0:8], 0.0)

            for r in (0, 1):
                onehots(r, r * TB)
            with dve.Fori(1, NB // 2) as i:
                chain.loop(i, 1, NB // 2, 2)
                for r in (0, 1):
                    dve.wait_ge(g_built, i * 2 + (r - 1))
                    onehots(r, i * 2 * TB + r * TB)
                chain.end()
            dve.wait_ge(g_built, NB)
            next_group()

            def pair(par, p, j, wpar, build, first=False):
                built = j * 8 + NB

                def oh(b):
                    if build:
                        dve.wait_ge(g_built, built + (2 * b - 2))
                        onehots(b, p * SLICE + b * TB)

                def ev(b):
                    if build:
                        gates(1 - par, p * SLICE + b * TB, built + 2 * b)

                def weigh(e):
                    dve.wait_ge(gelu_done, j * 2 + (e + 1))
                    g = Gd[:, par, bass.ds(p * 2 + e, 1), :].rearrange("p a t -> p (a t)")
                    chain(dve.tensor_tensor(B[e][:, :], B[e][:, :], g, ALU.mult))
                    h, l = WH[:, wpar, e, :], WL[:, wpar, e, :]
                    chain(dve.tensor_scalar(h, B[e][:, :], 1.0, None, ALU.mult))
                    dve.tensor_tensor(l, B[e][:, :], h.bitcast(F32), ALU.subtract).then_inc(w_done, 1)

                def adds(k0, k1):
                    for k in range(k0, k1):
                        if not first:
                            dve.wait_ge(y_done, (j - 1) * KD + (k + 1))
                            dve.tensor_tensor(xT[:, k, :], xT[:, k, :], B[4 + k % 4][:, :], ALU.add).then_inc(y_added, 1)

                oh(0)
                oh(1)
                dve.wait_ge(g_evac, built if build else NB * (2 * N_GRP - 1))
                weigh(0)
                ev(0)
                oh(2)
                weigh(1)
                ev(1)
                adds(0, 2)
                oh(3)
                adds(2, 4)
                ev(2)
                adds(4, KD)
                ev(3)

            steps = 2 * (4 * 1 + 2 * 2)
            pair(0, 0, 0, 0, True, first=True)
            pair(0, 1, 1, 1, True)
            with dve.Fori(1, PAIRS // 2) as i:
                chain.loop(i, 1, PAIRS // 2, steps)
                for q in (0, 1):
                    pair(0, i * 2 + q, i * 2 + q, q, True)
                chain.end()
            next_group()
            with dve.Fori(0, (N_GRP - 2) // 2) as g:
                chain.loop(g, 0, (N_GRP - 2) // 2, 2 * (PAIRS // 2 * steps + 1))
                for par in (1, 0):
                    with dve.Fori(0, PAIRS // 2) as i:
                        chain.loop(i, 0, PAIRS // 2, steps)
                        for q in (0, 1):
                            pair(par, i * 2 + q, g * (2 * PAIRS) + i * 2 + (PAIRS * (2 - par) + q), q, True)
                        chain.end()
                    next_group()
                chain.end()
            with dve.Fori(0, PAIRS // 2) as i:
                chain.loop(i, 0, PAIRS // 2, 2 * 2 * 2)
                for q in (0, 1):
                    pair(1, i * 2 + q, i * 2 + ((N_GRP - 1) * PAIRS + q), q, False)
                chain.end()
            for k in range(KD):
                dve.wait_ge(y_done, (NKEY // 2 - 1) * KD + k + 1)
                dve.tensor_tensor(xT[:, k, :], xT[:, k, :], B[4 + k % 4][:, :], ALU.add).then_inc(y_added, 1)
                dve.wait_ge(y_added, (NKEY // 2 - 1) * KD + k + 1)
                square(x_of(k), k)
            over_root(TT, n_root + 1)
            dve.wait_ge(spread, n_spread + 1)
            for k in range(KD):
                dve.scalar_tensor_tensor(xT[:, k, :], xT[:, k, :], gain("final", k), B[5][:, :], ALU.mult, ALU.mult).then_inc(final_done, 1)

        @block.tensor
        def _(pe):
            def mm3(bank, wh, wl, xh, xl, start, stop_):
                pe.matmul(bank, wh, xh, start=start, stop=False)
                pe.matmul(bank, wh, xl, start=False, stop=False)
                return pe.matmul(bank, wl, xh, start=False, stop=stop_)

            def tile(r, bank, signal=slot_used):
                for k in range(KD):
                    c = slice(k * P, (k + 1) * P)
                    m = mm3(bank, hi[:, r, c], lo[:, r, c], inH[:, k, :], inL[:, k, :], k == 0, k == KD - 1)
                m.then_inc(signal, 1)

            def tiles_by_token(s0, t0, m):
                r = m % RING
                pe.wait_ge(evac, t0 + m + 1 - RING + 1)
                pe.wait_ge(lo_done, s0 + m + 2)
                for t in range(TT):
                    tok = slice(t * P, (t + 1) * P)
                    out_cols = B[r + t // 2][:, t % 2 * 2 * P:(t % 2 + 1) * 2 * P]
                    for k in range(KD):
                        c = slice(k * P, (k + 1) * P)
                        mm = mm3(out_cols, inH[:, k, tok], inL[:, k, tok], hi[:, r:r + 2, c], lo[:, r:r + 2, c], k == 0, k == KD - 1)
                mm.then_inc(slot_used, 2)

            def linear(s0, t0, n, lo_=0):
                with pe.Fori(lo_, n // RING) as i:
                    for r in range(RING):
                        pe.wait_ge(evac, i * RING + (t0 + r - RING + 1))
                        pe.wait_ge(lo_done, i * RING + (s0 + r + 1))
                        tile(r, B[r][:, :])

            def first_tiles(s0, t0, nth, then=None):
                for m in range(AHEAD):
                    if t0:
                        pe.wait_ge(evac, t0 + m - RING + 1)
                    pe.wait_ge(lo_done, s0 + m + 1)
                for k in range(KD):
                    pe.wait_ge(in_part, nth * KD + k + 1)
                    c = slice(k * P, (k + 1) * P)
                    for m in range(AHEAD):
                        mm = mm3(B[m][:, :], hi[:, m, c], lo[:, m, c], inH[:, k, :], inL[:, k, :], k == 0, k == KD - 1)
                        if k == KD - 1:
                            mm.then_inc(slot_used, 1)
                if then:
                    then()
                for m in range(AHEAD, RING):
                    if t0:
                        pe.wait_ge(evac, t0 + m - RING + 1)
                    pe.wait_ge(lo_done, s0 + m + 1)
                    tile(m, B[m][:, :])

            def spread_roots(n, group, k):
                if group and k >= 2:
                    pe.wait_ge(spread_used, group - 1 + k - 1)
                for t in range(TT):
                    tok = slice(t * P, (t + 1) * P)
                    if group:
                        for g in range(2):
                            c = t * N_GRPS + 2 * k + g
                            m = pe.matmul(B[5 + k % 2][g * HD:(g + 1) * HD, tok], rr[:, c:c + 1].broadcast_to([P, HD]), ident,
                                          start=True, stop=True)
                    else:
                        m = pe.matmul(B[5 + k % 2][:, tok], rr[:, t:t + 1].broadcast_to([P, P]), ident, start=True, stop=True)
                m.then_inc(spread, 1)

            def square_sums(n):
                pe.wait_ge(squares, n + KD)
                for t in range(TT):
                    m = pe.matmul(B[4][:, t:t + 1], sq[:, 0, t * P:(t + 1) * P], ones[:, 0:1], start=True, stop=True)
                m.then_inc(sums, KD)

            def full_norm(n, nth):
                square_sums(n)
                pe.wait_ge(recips, nth)
                spread_roots(n, 0, 0)

            def group_norm(n, nth, used):
                for k in range(KD):
                    pe.wait_ge(squares, n + k + 1)
                    for t in range(TT):
                        c = t * N_GRPS + 2 * k
                        m = pe.matmul(B[4][:, c:c + 2], sq[:, k % 2, t * P:(t + 1) * P], blk[:, 0:P:HD], start=True, stop=True)
                    m.then_inc(sums, 1)
                pe.wait_ge(recips, nth)
                for k in range(KD):
                    spread_roots(n, used + 1, k)

            def attention(st):
                s, units = st["s"], st["units"]
                n = len(units)
                for u in range(n + 3):
                    if u < n:
                        w = units[u]
                        rows = slice(w["row"], w["row"] + HD)
                        if u >= 2:
                            pe.wait_ge(s["logit"], u - 1)
                        pe.matmul(B[4 + u % 2][:, :w["n"]], st["qk"][rows, w["q"], w["i"] * P:(w["i"] + 1) * P],
                                  st["qk"][rows, w["k"], w["k0"]:w["k0"] + w["n"]], start=True, stop=True).then_inc(s["score"], 1)
                    if 2 <= u <= n + 1:
                        v = u - 2
                        w = units[v]
                        pe.wait_ge(s["normed"], v + 1)
                        if v >= 2:
                            pe.wait_ge(s["turned_sb"], v - 1)
                        for b in range(w["n"] // P):
                            c = slice(b * P, (b + 1) * P)
                            m = pe.transpose(B[6 + v % 2][:, c], st["pr"][:, v % 4, c], ident)
                        m.then_inc(s["turned"], 1)
                    if u >= 3:
                        v = u - 3
                        w = units[v]
                        pe.wait_ge(s["turned_sb"], v + 1)
                        if w["pair"] >= 2 and (v == 0 or units[v - 1]["pair"] != w["pair"]):
                            pe.wait_ge(s["head_out"], w["pair"] - 1)
                        nb = w["n"] // P
                        for b in range(nb):
                            m = pe.matmul(B[2 + w["pair"] % 2][w["row"]:w["row"] + HD, w["i"] * P:(w["i"] + 1) * P],
                                          st["v"][:, w["k0"] // P + b, w["v"]:w["v"] + HD],
                                          st["pT"][:, v % 2, b * P:(b + 1) * P], start=b == 0, stop=b == nb - 1)
                        m.then_inc(s["mixed"], 1)


            pe.wait_ge(small_in, 48)
            n_sq, n_rt = 0, 0
            n_rt += 1
            full_norm(n_sq, n_rt)
            n_sq += KD
            first_tiles(S_IN, T_IN, 0)
            linear(S_IN, T_IN, 16, 1)
            for m in (16, 17):
                pe.wait_ge(evac, m - RING + 1)
                pe.wait_ge(lo_done, m + 1)
                tile(m % RING, B[m % RING][:, :])
            for m in range(18, N_IN, 2):
                tiles_by_token(S_IN, T_IN, m)
            pe.wait_ge(evac, T_OUT)
            def z_of(m):
                h, kb, w = blocks[m]
                rows = slice(HD * (h % 2), HD * (h % 2) + HD)
                return qk1[rows, 2 + h // 2, kb * P:(kb + 1) * P], qk1[rows, h // 2, kb * P:]

            for n in range(-1, len(blocks) + 1):
                if n + 1 < len(blocks):
                    m = n + 1
                    if m >= 2:
                        pe.wait_ge(lr_ready, m - 1)
                    pe.matmul(B[2 + m % 2][:, :blocks[m][2]], *z_of(m), start=True, stop=True).then_inc(z_done, 1)
                if 0 <= n < len(blocks):
                    h, kb, w = blocks[n]
                    pe.wait_ge(lr_ready, n + 1)
                    if n >= 2:
                        pe.wait_ge(w_exp, n - 1)
                        pe.wait_ge(s_masked, n - 1)
                    s, l = B[4 + n % 2], lr[:, h % 2, :, :]
                    pe.matmul(s[:, :w], *z_of(n), start=True, stop=False)
                    m = pe.matmul(s[:, :w], tri, l[:, kb, :w], start=False, stop=kb == TT - 1)
                    for nb in range(kb + 1, TT):
                        m = pe.matmul(s[:, (nb - kb) * P:w], ones, l[:, nb, :T - nb * P], start=False, stop=nb == TT - 1)
                    m.then_inc(s_done, 1)
                if n >= 1:
                    v = n - 1
                    h, kb, w = blocks[v]
                    pe.wait_ge(w_exp, v + 1)
                    pe.matmul(B[6 + h // 2][HD * (h % 2):HD * (h % 2) + HD, kb * P:], v1[:, kb, HD * h:HD * h + HD],
                              wz[:, v % 2, :w], start=kb == TT - 1, stop=kb == 0, skip_group_check=True).then_inc(sb_out, 1)
            pe.wait_ge(y_sb, 2)
            n_rt += 1
            group_norm(n_sq, n_rt, 0)
            n_sq += KD
            pe.wait_ge(in_ready, 2)
            attention(stage1)
            n_rt += 1
            group_norm(n_sq, n_rt, KD)
            n_sq += KD
            first_tiles(S_OUT, T_OUT, 1)
            linear(S_OUT, T_OUT, N_OUT, 1)
            n_rt += 1
            full_norm(n_sq, n_rt)
            n_sq += KD
            first_tiles(S_GU, T_GU, 2)
            linear(S_GU, T_GU, N_GU, 1)
            pe.wait_ge(evac, T_DOWN)
            with pe.Fori(0, 2) as i:
                for m in range(RING):
                    pe.wait_ge(evac, i * RING + (T_DOWN + m - RING + 1))
                    for k in range(KF):
                        s, r = k // KD, (3 * m + k // KD) % RING
                        if k % KD == 0:
                            pe.wait_ge(lo_done, i * 12 + (S_DOWN + 3 * m + s + 1))
                        c = slice(k % KD * P, (k % KD + 1) * P)
                        mm = mm3(B[m][:, :], hi[:, r, c], lo[:, r, c], actH[:, k, :], actL[:, k, :], k == 0, k == KF - 1)
                        if k % KD == KD - 1 or k == KF - 1:
                            mm.then_inc(slot_used, 1)
            n_rt += 1
            full_norm(n_sq, n_rt)
            n_sq += KD
            first_tiles(S_IN2, T_IN2, 3)

            def in2_tile(m):
                pe.wait_ge(evac, T_IN2 + m - RING + 1)
                pe.wait_ge(lo_done, S_IN2 + m + 1)
                tile(m % RING, B[m % RING][:, :])

            def mean(k, n_conv):
                pe.wait_ge(conv_done, n_conv)
                src = c2[:, k, :] if isinstance(k, int) else c2[:, bass.ds(k, 1), :].rearrange("p a t -> p (a t)")
                pe.matmul(B[4][:, :], ones, src, start=isinstance(k, int) and k == 0,
                          stop=isinstance(k, int) and k == KD - 1).then_inc(mean_done, 1)

            for m in range(4, 8):
                in2_tile(m)
            mean(0, 1)
            with pe.Fori(2, KD) as i:
                for r in range(RING):
                    pe.wait_ge(evac, i * RING + (T_IN2 + r - RING + 1))
                    pe.wait_ge(lo_done, i * RING + (S_IN2 + r + 1))
                    tile(r, B[r][:, :])
                mean(i - 1, i)
            for m in range(4 * KD, LN_TILE - 2):
                in2_tile(m)
            mean(KD - 1, KD)
            for m in range(LN_TILE - 2, LN_TILE):
                in2_tile(m)
            n_rt += 1
            square_sums(n_sq)
            in2_tile(LN_TILE)
            pe.wait_ge(recips, n_rt)
            spread_roots(n_sq, 0, 0)
            n_sq += KD
            for m in range(LN_TILE + 1, N_IN2 - 2):
                in2_tile(m)
            tiles_by_token(S_IN2, T_IN2, N_IN2 - 2)
            first_tiles(S_PW, T_PW, 4)
            linear(S_PW, T_PW, KD, 1)
            pe.wait_ge(evac, T_WO)
            attention(stage2)
            first_tiles(S_WO, T_WO, 5)
            linear(S_WO, T_WO, KD, 1)
            first_tiles(S_WO2, T_WO2, 6)
            linear(S_WO2, T_WO2, KD, 1)
            n_rt += 1
            full_norm(n_sq, n_rt)
            n_sq += KD
            def scores(m, n_evac):
                pe.wait_ge(evac, n_evac)
                for t in range(TT):
                    mm = pe.matmul(B[4 + m % 2][:, t * P:(t + 1) * P], qp[:, m % RING, t * P:(t + 1) * P], key_sb[:, m % 2, :],
                                   start=True, stop=True)
                mm.then_inc(sc_done, 1)

            def early_scores():
                pe.wait_ge(peer_in, 48)
                scores(0, T_Q + 1)
                scores(1, T_Q + 2)

            first_tiles(S_Q, T_Q, 7, early_scores)
            pe.wait_ge(sc_copied, 1)
            scores(2, T_Q + 3)
            with pe.Fori(1, N_Q // RING) as i:
                for r in range(RING):
                    pe.wait_ge(evac, i * RING + (T_Q + r - RING + 1))
                    pe.wait_ge(lo_done, i * RING + (S_Q + r + 1))
                    tile(r, B[r][:, :])
                    pe.wait_ge(sc_copied, i * RING + (r - 2))
                    scores(r - 1, i * RING + (T_Q + r))
            pe.wait_ge(sc_copied, N_Q - 2)
            scores(N_Q - 1, T_Q + N_Q)
            for e in (0, 1):
                pe.wait_ge(lo_done, S_PEER + 1 + e)
                tile(e, B[e][:, :], u_done)
            for t in range(TT):
                pe.wait_ge(sel_ready, t + 1)
                if t >= 2:
                    pe.wait_ge(selT_copied, t - 1)
                for j in range(3):
                    m = pe.transpose(B[6 + t % 2][:, j * P:(j + 1) * P], sel[:, t % 2, j, :], ident)
                m.then_inc(selT_done, 1)

            pe.wait_ge(selT_copied, TT)

            def build(r, n_oh, n_built):
                pe.wait_ge(oh_ready, n_oh)
                for half in (0, 1):
                    pe.wait_ge(g_evac, n_built + half - 1)
                    for t in range(8):
                        tok = half * 8 + t
                        m = pe.matmul(B[2 + half][:, t * 3 * GRP:(t + 1) * 3 * GRP], oh2[:, r, :, tok],
                                      ohg[:, r, :, :, tok], start=True, stop=True)
                    m.then_inc(g_built, 1)

            def build_first(r, n):
                pe.wait_ge(oh_ready, n + 1)
                for t in range(TB):
                    for part in range(3):
                        m = pe.matmul(B[2 + r][:, t * GRP:(t + 1) * GRP], oh2[:, r, :, t], ohg[:, r, part, :, t],
                                      start=part == 0, stop=part == 2)
                m.then_inc(g_built, 1)

            build_first(0, 0)
            build_first(1, 1)
            with pe.Fori(1, NB // 2) as i:
                for r in (0, 1):
                    pe.wait_ge(g_evac, i * 2 + (r - 1))
                    build_first(r, i * 2 + r)

            def a_tile(e, r, n, j):
                pe.wait_ge(lo_done, n)
                pe.wait_ge(w_done, j * 2 + (e - 1))
                tile(r, B[e][:, :], u_done)

            def y_tiles(k0, k1, wpar, j, r0):
                if k0 == 0:
                    pe.wait_ge(lo_done, j * 4 + (S_PEER + 6))
                    pe.wait_ge(w_done, j * 2 + 2)
                for k in range(k0, k1):
                    pe.wait_ge(y_added, j * KD + (k - 3)) if not (isinstance(j, int) and j * KD + k - 3 <= 0) else None
                    c = slice(k * P, (k + 1) * P)
                    for e in (0, 1):
                        m = mm3(B[4 + k % 4][:, :], hi[:, r0 + e, c], lo[:, r0 + e, c], WH[:, wpar, e, :], WL[:, wpar, e, :],
                                e == 0, e == 1)
                    m.then_inc(y_done, 1)

            def body(j, q, build_next, first=False, one=False):
                if not first:
                    a_tile(0, 2, j * 4 + (S_PEER - 2 + 1), j)
                ob, gb = j * 4 + NB, j * 8 + NB
                if build_next:
                    build(0, ob + 1, gb)
                if not first:
                    a_tile(1, 3, j * 4 + (S_PEER - 2 + 2), j)
                if build_next:
                    build(1, ob + 2, gb + 2)
                if not first:
                    y_tiles(0, 4, 1 - q, j - 1, 0)
                if build_next:
                    build(0, ob + 3, gb + 4)
                if not first:
                    y_tiles(4, KD, 1 - q, j - 1, 0)
                if build_next:
                    build(1, ob + 4, gb + 6)

            body(0, 0, True, first=True)
            body(1, 1, True)
            with pe.Fori(1, (N_GRP - 1) * PAIRS // 2) as i:
                for q in (0, 1):
                    body(i * 2 + q, q, True)
            with pe.Fori((N_GRP - 1) * PAIRS // 2, NKEY // 4) as i:
                for q in (0, 1):
                    body(i * 2 + q, q, False)
            last = NKEY // 2 - 1
            pe.wait_ge(lo_done, N_SLOTS)
            pe.wait_ge(w_done, 2 * last + 2)
            for k in range(KD):
                pe.wait_ge(y_added, last * KD + k - 3)
                c = slice(k * P, (k + 1) * P)
                for e in (0, 1):
                    m = mm3(B[4 + k % 4][:, :], hi[:, 2 + e, c], lo[:, 2 + e, c], WH[:, 1, e, :], WL[:, 1, e, :], e == 0, e == 1)
                m.then_inc(y_done, 1)
            full_norm(n_sq, n_rt + 1)

        return None


def lay_out(i):
    f = lambda a: np.asarray(a)

    def blocks(w):
        k, m = w.shape[0] // P, w.shape[1] // P
        return w.reshape(k, P, m, P).transpose(2, 1, 0, 3)

    def slots(w):
        b = blocks(w)
        return b.reshape(b.shape[0], P, D)

    w_in = f(i["w_in"])[0]
    o = np.cumsum([0, 256, 256, 256, 512, 512, 512, 256, 256, 256])
    part = lambda n: w_in[:, o[n]:o[n + 1]]
    win = slots(np.concatenate([part(n) for n in (0, 1, 3, 4, 6, 7, 8, 2, 5)], 1))
    wg, wu = slots(f(i["w_gate"])[0]), slots(f(i["w_up"])[0])
    gu = np.stack([wg, wu], 1).reshape(N_GU, P, D)
    wd = np.zeros((KD, P, KF_PAD, P), np.float32)
    wd[:, :, :KF] = blocks(f(i["w_down"])[0])
    wd = wd.reshape(KD, P, 3, D).transpose(0, 2, 1, 3).reshape(N_DOWN, P, D)
    w2 = f(i["w_in_2"])[0]
    a, b = slots(w2[:, :D]), slots(w2[:, D:2 * D])
    ab = np.stack([a, b], 1).reshape(16, P, D)
    heads = [4 * (2 * (j // 4) + half) + j % 4 for j in range(8) for half in (0, 1)]
    q2 = w2[:, 2048:3072].reshape(D, N_HEADS, HD)[:, heads].reshape(D, D)
    k2, vv2, g2 = w2[:, 3072:3328], w2[:, 3328:3584], w2[:, 3584:5632]
    others = np.concatenate([slots(q2), slots(k2), slots(g2), slots(vv2)])
    turns = np.concatenate([ab.reshape(KD, 2, P, D), others[:2 * KD].reshape(KD, 2, P, D)], 1)
    win2 = np.concatenate([turns.reshape(4 * KD, P, D), others[2 * KD:]])
    wo = f(i["attn_w_o_2"])[0].reshape(N_HEADS, HD, D)[heads].reshape(D, D)
    eu = f(i["peer_u_2"])[0].reshape(NKEY, NKEY, KD, P).transpose(0, 3, 2, 1).reshape(NKEY, P, D)
    ev = f(i["peer_v_2"])[0].reshape(NKEY, NKEY, D)
    stream = np.empty((N_SLOTS, P, D), np.float32)
    n = 0
    for w in (win, slots(f(i["w_out"])[0]), gu, wd, win2, slots(f(i["conv_w_pw_2"])[0]), slots(wo),
              slots(f(i["w_out_2"])[0]), slots(f(i["peer_w_query_2"])[0])):
        stream[n:n + len(w)] = w
        n += len(w)
    assert n == S_PEER
    stream[n:n + 2] = eu[0:2]
    rest = stream[n + 2:n + 2 + 4 * (NKEY // 2 - 1)].reshape(NKEY // 2 - 1, 4, P, D)
    rest[:, 0:2] = eu[2:].reshape(NKEY // 2 - 1, 2, P, D)
    rest[:, 2:4] = ev[:-2].reshape(NKEY // 2 - 1, 2, P, D)
    stream[-2:] = ev[-2:]

    gains = np.empty((P, N_GC), np.float32)

    def put(name, a):
        gains[:, GC[name]:GC[name] + a.shape[1]] = a

    feat = lambda a: f(a).reshape(-1, P).T
    put("attn", feat(i["attn_norm_w"]))
    put("out", feat(i["out_norm_w"]))
    put("ffn", feat(i["ffn_norm_w"]))
    put("norm1", feat(i["norm1_g_2"]))
    put("norm2", feat(i["norm2_g_2"]))
    put("final", feat(i["final_g_2"]))
    put("ln_g", feat(i["conv_ln_g_2"]))
    put("ln_b", feat(i["conv_ln_b_2"]))
    put("dw_b", feat(i["conv_dw_b_2"]))
    put("dw", f(i["conv_dw_w_2"])[0].reshape(CONV_TAPS, KD, P).transpose(2, 1, 0).reshape(P, KD * CONV_TAPS))
    put("conv", f(i["conv_w"])[0].reshape(3, 2, P).transpose(2, 1, 0).reshape(P, 6))
    put("qn", np.concatenate([f(i["q_norm_w"])[0]] * 2)[:, None])
    put("kn", np.concatenate([f(i["k_norm_w"])[0]] * 2)[:, None])
    put("sink", np.broadcast_to(f(i["attn_sink_2"])[0][None], (P, N_HEADS)))
    put("eps", np.full((P, 1), EPS, np.float32))

    rel = f(i["rel_bias"])[0][:, np.clip(T - 1 - np.arange(REL), -P, P) + P]
    rel = np.tile(rel, (1, P))

    keys = np.ascontiguousarray(f(i["peer_sub_keys_2"])[0].transpose(2, 0, 1))
    x = np.ascontiguousarray(f(i["x"])[0].reshape(T, KD, P).transpose(2, 1, 0))
    return dict(x=x, stream=stream, gains=gains, rel=np.ascontiguousarray(rel), keys=keys)


def constants():
    r = np.arange(P)
    c = np.zeros((P, N_CC), np.float32)
    c[:, CC["ident"]:CC["ident"] + P] = np.eye(P)
    c[:, CC["ones"]:CC["ones"] + P] = 1
    c[:, CC["blk"]:CC["blk"] + P] = (r[:, None] // HD == r[None] // HD)
    c[:, CC["tri"]:CC["tri"] + P] = r[:, None] >= r[None]
    c[:, CC["mask"]:CC["mask"] + P] = r[:, None] < r[None]
    c[:, CC["neg"]:CC["neg"] + P] = np.where(r[:, None] < r[None], 0, NEG)
    c[:, CC["iota"]:CC["iota"] + TOPK] = np.arange(TOPK)
    dist = np.abs(r[:, None] + P - np.arange(3 * P)[None]).astype(np.float32)
    slopes = np.exp2(-8.0 * np.arange(1, N_HEADS + 1, dtype=np.float32) / N_HEADS).astype(np.float32)
    order = [4 * (2 * (j // 4) + half) + j % 4 for j in range(8) for half in (0, 1)]
    gqa = np.where(dist <= P, -slopes[order, None, None] * dist, np.float32(NEG)).astype(np.float32)
    ohc = np.empty((P, NKEY + GRP, TB), np.float32)
    ohc[:, :NKEY] = np.arange(NKEY)[None, :, None]
    ohc[:, NKEY:] = np.arange(GRP)[None, :, None]
    ohc = (ohc.view(np.uint32) >> 16).astype(np.uint16)
    return dict(consts=c, gqa=gqa, ohc=ohc)


def kernel(**inputs):
    import concourse.bacc as _bacc
    from concourse.bass_utils import run_bass_kernel_spmd as _run

    arrays = {**lay_out(inputs), **constants()}
    nc = _bacc.Bacc("TRN2", target_bir_lowering=False, num_devices=1)
    args = {n: nc.dram_tensor(n, a.shape, mybir.dt.from_np(a.dtype), kind="ExternalInput").ap() for n, a in arrays.items()}
    out = nc.dram_tensor("out", (P, KD, T), F32, kind="ExternalOutput").ap()
    program(nc, out=out, **args)
    r = _run(nc, [arrays], core_ids=[0])
    got = r.results[0]["out"]
    return got.transpose(2, 1, 0).reshape(1, T, D)
```
